# Optimizing a Trainium2 kernel written in Bass

```python
import math
import jax, jax.numpy as jnp
from jax import lax
import numpy as np

D_MODEL = 1024
BATCH = 1
SEQ = 256
DEPTH = 1
DEC_BATCH = 8
DEC_SEQ = 4
PAST_LEN = 2048
PAGE_SIZE = 128

DN_HEADS = 4
DN_DK = 128
DN_DV = 128
DN_KEY = DN_HEADS * DN_DK
DN_VAL = DN_HEADS * DN_DV
DN_CONV = 4
DN_CONV_DIM = 2 * DN_KEY + DN_VAL
DN_CHUNK = 64
SSM_INNER = D_MODEL
SSM_HEADDIM = 64
SSM_HEADS = SSM_INNER // SSM_HEADDIM
SSM_GROUPS = 2
SSM_STATE = 128
SSM_CONV = 4
SSM_CONV_DIM = SSM_INNER + 2 * SSM_GROUPS * SSM_STATE
SSM_CHUNK = 64
MOE_GROUPS = 4
MOE_PER_GROUP = 8
MOE_EXPERTS = MOE_GROUPS * MOE_PER_GROUP
MOE_TOPK = 2
MOE_FF = D_MODEL // 4
EPS = 1e-6

IN_SIZES = (DN_CONV_DIM, DN_VAL, DN_HEADS, DN_HEADS,
            SSM_CONV_DIM, SSM_INNER, SSM_HEADS,
            D_MODEL, D_MODEL)
D_IN_PROJ = sum(IN_SIZES)

kernel_name = 'hybrid_gdn_ssd_hmoe_adaln_step'

def _rms_norm(x, w):
    xf = x.astype(jnp.float32)
    y = xf * lax.rsqrt(jnp.mean(xf * xf, axis=-1, keepdims=True) + EPS)
    return (y * w.astype(jnp.float32)).astype(x.dtype)

def _l2norm(t):
    t = t.astype(jnp.float32)
    return t * lax.rsqrt(jnp.sum(t * t, axis=-1, keepdims=True) + EPS)

def _causal_conv(u, buf, w):
    width, L = w.shape[0], u.shape[1]
    full = jnp.concatenate([buf.astype(u.dtype), u], axis=1)
    y = full[:, 0:L] * w[0]
    for i in range(1, width):
        y = y + full[:, i:i + L] * w[i]
    return y, full[:, L:]

def _chunk(t, C):
    Bsz, L = t.shape[:2]
    n = -(-L // C)
    t = jnp.pad(t, [(0, 0), (0, n * C - L)] + [(0, 0)] * (t.ndim - 2))
    t = t.reshape((Bsz, n, C) + t.shape[2:])
    return jnp.transpose(t, (1, 0, 3, 2) + tuple(range(4, t.ndim)))

def _unchunk(t, L):
    n, Bsz, H, C = t.shape[:4]
    t = jnp.transpose(t, (1, 0, 3, 2) + tuple(range(4, t.ndim)))
    return t.reshape((Bsz, n * C, H) + t.shape[4:])[:, :L]

def _gated_delta(q, k, v, g, beta, s0):
    L = q.shape[1]
    C = min(DN_CHUNK, L)
    tri_incl = jnp.tril(jnp.ones((C, C), bool))
    tri_strict = jnp.tril(jnp.ones((C, C), bool), -1)
    eye = jnp.eye(C, dtype=jnp.float32)

    def step(S, inp):
        qc, kc, vc, gc, bc = inp
        cs = jnp.cumsum(gc, axis=-1)
        decay = jnp.exp(jnp.where(tri_incl, cs[..., :, None] - cs[..., None, :], -jnp.inf))
        kk = jnp.einsum('bhid,bhjd->bhij', kc, kc)
        lmat = jnp.where(tri_strict, bc[..., :, None] * kk * decay, 0.0)
        rhs = jnp.concatenate([vc * bc[..., None], kc * (bc * jnp.exp(cs))[..., None]], axis=-1)
        sol = lax.linalg.triangular_solve(lmat + eye, rhs, left_side=True, lower=True)
        u, w = sol[..., :DN_DV], sol[..., DN_DV:]
        v_new = u - jnp.einsum('bhik,bhkv->bhiv', w, S)
        qk = jnp.einsum('bhid,bhjd->bhij', qc, kc) * decay
        o = (jnp.einsum('bhik,bhkv->bhiv', qc * jnp.exp(cs)[..., None], S)
             + jnp.einsum('bhij,bhjv->bhiv', qk, v_new))
        last = cs[..., -1:]
        S = (jnp.exp(last)[..., None] * S
             + jnp.einsum('bhjk,bhjv->bhkv', kc * jnp.exp(last - cs)[..., None], v_new))
        return S, o

    S, o = lax.scan(step, s0.astype(jnp.float32),
                    (_chunk(q, C), _chunk(k, C), _chunk(v, C), _chunk(g, C), _chunk(beta, C)))
    return _unchunk(o, L), S

def _ssd(x, dt, bm, cm, A, h0):
    Bsz, L = x.shape[:2]
    C = min(SSM_CHUNK, L)
    E = SSM_HEADS // SSM_GROUPS
    xc = _chunk(x, C)
    n = xc.shape[0]
    xc = xc.reshape(n, Bsz, SSM_GROUPS, E, C, SSM_HEADDIM)
    dtc = _chunk(dt, C).reshape(n, Bsz, SSM_GROUPS, E, C)
    bc, cc = _chunk(bm, C), _chunk(cm, C)
    a_ge = A.reshape(SSM_GROUPS, E)
    tri_incl = jnp.tril(jnp.ones((C, C), bool))

    def step(hs, inp):
        xk, dtk, bk, ck = inp
        cs = jnp.cumsum(dtk * a_ge[:, :, None], axis=-1)
        decay = jnp.exp(jnp.where(tri_incl, cs[..., :, None] - cs[..., None, :], -jnp.inf))
        xdt = xk * dtk[..., None]
        cb = jnp.einsum('bgin,bgjn->bgij', ck, bk)
        y = jnp.einsum('bgeij,bgejp->bgeip', cb[:, :, None] * decay, xdt)
        y = y + jnp.einsum('bgin,bgepn->bgeip', ck, hs) * jnp.exp(cs)[..., None]
        last = cs[..., -1:]
        hs = (jnp.exp(last)[..., None] * hs
              + jnp.einsum('bgjn,bgejp->bgepn', bk, xdt * jnp.exp(last - cs)[..., None]))
        return hs, y

    h0 = h0.astype(jnp.float32).reshape(Bsz, SSM_GROUPS, E, SSM_HEADDIM, SSM_STATE)
    hs, y = lax.scan(step, h0, (xc, dtc, bc, cc))
    y = y.reshape(n, Bsz, SSM_HEADS, C, SSM_HEADDIM)
    return _unchunk(y, L), hs.reshape(Bsz, SSM_HEADS, SSM_HEADDIM, SSM_STATE)

def _mixer(h, dn_conv_buf, dn_s, ssm_conv_buf, ssm_h, lp):
    Bsz, L, _ = h.shape
    f32 = jnp.float32
    split_at = np.cumsum(IN_SIZES)[:-1].tolist()
    (dn_qkv, dn_z, dn_a, dn_b, ssm_xbc, ssm_z, ssm_dt, gate_dn, gate_ssm) = jnp.split(
        h @ lp['w_in'], split_at, axis=-1)

    dn_qkv, dn_conv_new = _causal_conv(dn_qkv, dn_conv_buf, lp['dn_conv_w'])
    dn_qkv = jax.nn.silu(dn_qkv)
    q, k, v = jnp.split(dn_qkv, [DN_KEY, 2 * DN_KEY], axis=-1)
    q = _l2norm(q.reshape(Bsz, L, DN_HEADS, DN_DK)) * (DN_DK ** -0.5)
    k = _l2norm(k.reshape(Bsz, L, DN_HEADS, DN_DK))
    v = v.reshape(Bsz, L, DN_HEADS, DN_DV).astype(f32)
    g = -jnp.exp(lp['dn_A_log'].astype(f32)) * jax.nn.softplus(dn_a.astype(f32) + lp['dn_dt_bias'].astype(f32))
    beta = jax.nn.sigmoid(dn_b.astype(f32))
    o, dn_s_new = _gated_delta(q, k, v, g, beta, dn_s)
    o = _rms_norm(o, lp['dn_norm_w']) * jax.nn.silu(dn_z.reshape(Bsz, L, DN_HEADS, DN_DV).astype(f32))
    y_dn = o.reshape(Bsz, L, DN_VAL).astype(h.dtype) @ lp['w_dn_out']

    xbc, ssm_conv_new = _causal_conv(ssm_xbc, ssm_conv_buf, lp['ssm_conv_w'])
    xbc = jax.nn.silu(xbc + lp['ssm_conv_b'])
    xs, bm, cm = jnp.split(xbc, [SSM_INNER, SSM_INNER + SSM_GROUPS * SSM_STATE], axis=-1)
    xs = xs.reshape(Bsz, L, SSM_HEADS, SSM_HEADDIM).astype(f32)
    bm = bm.reshape(Bsz, L, SSM_GROUPS, SSM_STATE).astype(f32)
    cm = cm.reshape(Bsz, L, SSM_GROUPS, SSM_STATE).astype(f32)
    dt = jax.nn.softplus(ssm_dt.astype(f32) + lp['ssm_dt_bias'].astype(f32))
    A = -jnp.exp(lp['ssm_A_log'].astype(f32))
    y, ssm_h_new = _ssd(xs, dt, bm, cm, A, ssm_h)
    y = y + lp['ssm_D'].astype(f32)[:, None] * xs
    y = y.reshape(Bsz, L, SSM_INNER) * jax.nn.silu(ssm_z.astype(f32))
    y = _rms_norm(y.reshape(Bsz, L, SSM_GROUPS, SSM_INNER // SSM_GROUPS),
                  lp['ssm_norm_w'].reshape(SSM_GROUPS, SSM_INNER // SSM_GROUPS)).reshape(Bsz, L, SSM_INNER)
    y_ssm = y.astype(h.dtype) @ lp['w_ssm_out']

    merged = jax.nn.sigmoid(gate_dn) * y_dn + jax.nn.sigmoid(gate_ssm) * y_ssm
    return merged @ lp['w_out'], dn_conv_new, dn_s_new, ssm_conv_new, ssm_h_new

def _hier_moe(h, lp):
    Bsz, L, D = h.shape
    t = h.reshape(Bsz * L, D)
    g_logits = (t @ lp['w_group_router'] + lp['b_group_router']).astype(jnp.float32)
    g_sel = jnp.argmax(g_logits, axis=-1)
    p_group = jnp.take_along_axis(jax.nn.softmax(g_logits, axis=-1), g_sel[:, None], axis=-1)
    e_logits = (t @ lp['w_expert_router'] + lp['b_expert_router']).astype(jnp.float32)
    e_logits = jnp.take_along_axis(e_logits.reshape(-1, MOE_GROUPS, MOE_PER_GROUP),
                                   g_sel[:, None, None], axis=1)[:, 0]
    top_p, top_i = lax.top_k(jax.nn.softmax(e_logits, axis=-1), MOE_TOPK)
    comb = p_group * top_p / jnp.sum(top_p, axis=-1, keepdims=True)
    expert = g_sel[:, None] * MOE_PER_GROUP + top_i
    w_tok = jnp.sum(jax.nn.one_hot(expert, MOE_EXPERTS, dtype=jnp.float32) * comb[..., None], axis=1)
    gate = jnp.einsum('td,edf->tef', t, lp['w_exp_gate'])
    up = jnp.einsum('td,edf->tef', t, lp['w_exp_up'])
    act = jax.nn.silu(gate) * up * w_tok[..., None].astype(t.dtype)
    out = jnp.einsum('tef,efd->td', act, lp['w_exp_down'])
    return out.reshape(Bsz, L, D)

def _layer(x, c, dn_conv_buf, dn_s, ssm_conv_buf, ssm_h, lp):
    mod = (jax.nn.silu(c) @ lp['w_ada'] + lp['b_ada'])[:, None, :]
    sh1, sc1, gt1, sh2, sc2, gt2 = jnp.split(mod, 6, axis=-1)
    h = _rms_norm(x, lp['norm_mix_w']) * (1 + sc1) + sh1
    mix, dn_conv_new, dn_s_new, ssm_conv_new, ssm_h_new = _mixer(h, dn_conv_buf, dn_s, ssm_conv_buf, ssm_h, lp)
    x = x + gt1 * mix
    h = _rms_norm(x, lp['norm_ffn_w']) * (1 + sc2) + sh2
    x = x + gt2 * _hier_moe(h, lp)
    return x, dn_conv_new, dn_s_new, ssm_conv_new, ssm_h_new

def _trunk(x, c, dn_conv, dn_rec, ssm_conv, ssm_rec, layers, w_ada_final, b_ada_final, final_norm_w):
    n_dc, n_dr, n_sc, n_sr = [], [], [], []
    for l in range(DEPTH):
        x, a1, a2, a3, a4 = _layer(x, c, dn_conv[l], dn_rec[l], ssm_conv[l], ssm_rec[l], layers[l])
        n_dc.append(a1)
        n_dr.append(a2)
        n_sc.append(a3)
        n_sr.append(a4)
    shift, scale = jnp.split((jax.nn.silu(c) @ w_ada_final + b_ada_final)[:, None, :], 2, axis=-1)
    y = _rms_norm(x, final_norm_w) * (1 + scale) + shift
    return y, jnp.stack(n_dc), jnp.stack(n_dr), jnp.stack(n_sc), jnp.stack(n_sr)

def _dt_bias(key, n):
    dt = jnp.exp(jax.random.uniform(key, (DEPTH, n), jnp.float32, math.log(1e-3), math.log(1e-1)))
    return dt + jnp.log(-jnp.expm1(-dt))

def setup_inputs(seed: int = 0) -> dict:
    key = jax.random.key(seed)
    keys = jax.random.split(key, 64)
    counter = [0]
    f32 = jnp.float32

    def nk():
        counter[0] += 1
        return keys[counter[0] - 1]

    def nrm(shape, scale=1.0):
        return jax.random.normal(nk(), shape, f32) * scale

    def gain(shape):
        return 1.0 + nrm(shape, 0.02)

    D = D_MODEL
    sD = D ** -0.5
    return {
        'x_prompt': nrm((BATCH, SEQ, D)),
        'x_sample': nrm((DEC_BATCH, DEC_SEQ, D)),
        'c_prompt': nrm((BATCH, D)),
        'c_sample': nrm((DEC_BATCH, D)),
        'state_dn_conv': nrm((DEPTH, DEC_BATCH, DN_CONV - 1, DN_CONV_DIM)),
        'state_dn_rec': nrm((DEPTH, DEC_BATCH, DN_HEADS, DN_DK, DN_DV), 0.05),
        'state_ssm_conv': nrm((DEPTH, DEC_BATCH, SSM_CONV - 1, SSM_CONV_DIM)),
        'state_ssm_rec': nrm((DEPTH, DEC_BATCH, SSM_HEADS, SSM_HEADDIM, SSM_STATE), 0.05),
        'w_ada': nrm((DEPTH, D, 6 * D), sD),
        'b_ada': nrm((DEPTH, 6 * D), 0.02),
        'norm_mix_w': gain((DEPTH, D)),
        'w_in': nrm((DEPTH, D, D_IN_PROJ), sD),
        'dn_conv_w': nrm((DEPTH, DN_CONV, DN_CONV_DIM), DN_CONV ** -0.5),
        'dn_A_log': jnp.log(jax.random.uniform(nk(), (DEPTH, DN_HEADS), f32, 1.0, 16.0)),
        'dn_dt_bias': _dt_bias(nk(), DN_HEADS),
        'dn_norm_w': gain((DEPTH, DN_DV)),
        'w_dn_out': nrm((DEPTH, DN_VAL, D), DN_VAL ** -0.5),
        'ssm_conv_w': nrm((DEPTH, SSM_CONV, SSM_CONV_DIM), SSM_CONV ** -0.5),
        'ssm_conv_b': nrm((DEPTH, SSM_CONV_DIM), 0.02),
        'ssm_A_log': jnp.log(jax.random.uniform(nk(), (DEPTH, SSM_HEADS), f32, 1.0, 16.0)),
        'ssm_dt_bias': _dt_bias(nk(), SSM_HEADS),
        'ssm_D': 1.0 + nrm((DEPTH, SSM_HEADS), 0.1),
        'ssm_norm_w': gain((DEPTH, SSM_INNER)),
        'w_ssm_out': nrm((DEPTH, SSM_INNER, D), SSM_INNER ** -0.5),
        'w_out': nrm((DEPTH, D, D), sD),
        'norm_ffn_w': gain((DEPTH, D)),
        'w_group_router': nrm((DEPTH, D, MOE_GROUPS), sD),
        'b_group_router': nrm((DEPTH, MOE_GROUPS), 0.01),
        'w_expert_router': nrm((DEPTH, D, MOE_EXPERTS), sD),
        'b_expert_router': nrm((DEPTH, MOE_EXPERTS), 0.01),
        'w_exp_gate': nrm((DEPTH, MOE_EXPERTS, D, MOE_FF), sD),
        'w_exp_up': nrm((DEPTH, MOE_EXPERTS, D, MOE_FF), sD),
        'w_exp_down': nrm((DEPTH, MOE_EXPERTS, MOE_FF, D), MOE_FF ** -0.5),
        'w_ada_final': nrm((D, 2 * D), sD),
        'b_ada_final': nrm((2 * D,), 0.02),
        'final_norm_w': gain((D,)),
    }

def reference(x_prompt, x_sample, c_prompt, c_sample, state_dn_conv, state_dn_rec, state_ssm_conv,
              state_ssm_rec, w_ada, b_ada, norm_mix_w, w_in, dn_conv_w, dn_A_log, dn_dt_bias, dn_norm_w,
              w_dn_out, ssm_conv_w, ssm_conv_b, ssm_A_log, ssm_dt_bias, ssm_D, ssm_norm_w, w_ssm_out, w_out,
              norm_ffn_w, w_group_router, b_group_router, w_expert_router, b_expert_router, w_exp_gate,
              w_exp_up, w_exp_down, w_ada_final, b_ada_final, final_norm_w):
    layers = [dict(w_ada=w_ada[l], b_ada=b_ada[l], norm_mix_w=norm_mix_w[l], w_in=w_in[l],
                   dn_conv_w=dn_conv_w[l], dn_A_log=dn_A_log[l], dn_dt_bias=dn_dt_bias[l],
                   dn_norm_w=dn_norm_w[l], w_dn_out=w_dn_out[l], ssm_conv_w=ssm_conv_w[l],
                   ssm_conv_b=ssm_conv_b[l], ssm_A_log=ssm_A_log[l], ssm_dt_bias=ssm_dt_bias[l],
                   ssm_D=ssm_D[l], ssm_norm_w=ssm_norm_w[l], w_ssm_out=w_ssm_out[l], w_out=w_out[l],
                   norm_ffn_w=norm_ffn_w[l], w_group_router=w_group_router[l],
                   b_group_router=b_group_router[l], w_expert_router=w_expert_router[l],
                   b_expert_router=b_expert_router[l], w_exp_gate=w_exp_gate[l], w_exp_up=w_exp_up[l],
                   w_exp_down=w_exp_down[l])
              for l in range(DEPTH)]
    nb = x_prompt.shape[0]
    z_dn_conv = jnp.zeros((DEPTH, nb, DN_CONV - 1, DN_CONV_DIM), x_prompt.dtype)
    z_dn_rec = jnp.zeros((DEPTH, nb, DN_HEADS, DN_DK, DN_DV), jnp.float32)
    z_ssm_conv = jnp.zeros((DEPTH, nb, SSM_CONV - 1, SSM_CONV_DIM), x_prompt.dtype)
    z_ssm_rec = jnp.zeros((DEPTH, nb, SSM_HEADS, SSM_HEADDIM, SSM_STATE), jnp.float32)
    y_prompt, p_dn_conv, p_dn_rec, p_ssm_conv, p_ssm_rec = _trunk(
        x_prompt, c_prompt, z_dn_conv, z_dn_rec, z_ssm_conv, z_ssm_rec, layers,
        w_ada_final, b_ada_final, final_norm_w)
    y_sample, s_dn_conv, s_dn_rec, s_ssm_conv, s_ssm_rec = _trunk(
        x_sample, c_sample, state_dn_conv, state_dn_rec, state_ssm_conv, state_ssm_rec, layers,
        w_ada_final, b_ada_final, final_norm_w)
    return (y_prompt, y_sample, p_dn_conv, p_dn_rec, p_ssm_conv, p_ssm_rec,
            s_dn_conv, s_dn_rec, s_ssm_conv, s_ssm_rec)


_drawn_inputs = setup_inputs


def setup_inputs(seed=0):
    import zlib

    import numpy as np

    out = dict(_drawn_inputs(seed))
    spreads = {}
    factors = {'dn_norm_w': 16.565,
     'b_group_router': 23.571,
     'b_expert_router': 11.168,
     'b_ada_final': 2.669,
     'final_norm_w': 26.074,
     'ssm_norm_w': 15.071,
     'norm_ffn_w': 3.23}
    for name, (base, spread) in spreads.items():
        noise = np.random.default_rng([zlib.crc32(name.encode()), seed]).standard_normal(out[name].shape)
        drawn = base * np.exp(spread * noise) if base else spread * noise
        out[name] = __import__('jax').numpy.asarray(drawn.astype(out[name].dtype))
    for name, factor in factors.items():
        out[name] = (out[name] * factor).astype(out[name].dtype)
    return out
```

```python
from contextlib import ExitStack

import concourse.bass as bass
from concourse import mybir

F32 = mybir.dt.float32
I32 = mybir.dt.int32
ALU = mybir.AluOpType
ACT = mybir.ActivationFunctionType
AX = mybir.AxisListType

P = 128
D = 1024
KT = D // P
SEQ = 256
NB, NT = 8, 4
SMP = NB * NT
TOK = SEQ + SMP
TILES = [(0, P), (P, P), (SEQ, SMP)]
ORDER = [2, 0, 1]
NC = 1 + NB
DH = 4
SH = 16
HD = 64
NG = DH + SH
QKV = 1536
NQ = QKV // P
NU = 2 * NQ
HALO = 3
SROW = HALO + SEQ
STEP = HALO + NT
ROW = SROW + NB * STEP
CROW = ROW - HALO
ADA_N = 512
WN = 256
E = 32
EG, EPG = 4, 8
FF = 256
FT = FF // P
PAIRS = 2 * TOK
CW = 64
SLOTS = PAIRS + CW
ST = SLOTS // P
ESLOT = 4
EXW = 3 * D * FF // P
EPS = 1e-6
NEG = -1.0e30
C_Z, C_A, C_B, C_XBC, C_DT, C_GATE = 1536, 2048, 2052, 2056, 4616, 4632
RUNS = [(4, 0), (5, C_XBC), (4, C_GATE)]
ZT = 28
SHIFT1, SCALE1, GATE1, SHIFT2, SCALE2, GATE2, SHIFT_F, SCALE_F = range(0, 64, 8)
A_BADA, A_NORM, A_CONV = 0, 48, 56
B_CONV, B_CONVB, B_SNORM, B_FFN, B_BFIN, B_FIN, B_DNORM, B_ROWS = 0, 48, 60, 68, 76, 92, 100, 101
A_ROWS = 104


def hybrid_step(nc, T, O):
    ctx = ExitStack()
    with ctx:
        def sb(name, shape, dt=F32):
            return ctx.enter_context(nc.sbuf_tensor(name, shape, dt))

        sems = {}

        def S(name):
            if name not in sems:
                sems[name] = ctx.enter_context(nc.semaphore(name))
            return sems[name]

        ident = sb("ident", [P, P])
        ones = sb("ones", [P, P])
        tri = sb("tri", [P, P])
        neg = sb("neg", [P, P])
        tri_s = sb("tri_s", [SMP, SMP])
        neg_s = sb("neg_s", [SMP, SMP])
        same_s = sb("same_s", [SMP, SMP])
        seq_of = sb("seq_of", [SMP, NB])
        level = sb("level", [P, 7, P])
        head_rows = sb("head_rows", [SH, KT, P])
        eps_c = sb("eps_c", [P, 1])
        xT = sb("xT", [P, KT, TOK])
        modT = sb("modT", [P, 64, NC])
        colA = sb("colA", [P, A_ROWS])
        colB = sb("colB", [P, B_ROWS])
        scl = sb("scl", [P, KT, NC])
        gsm = sb("gsm", [P, 3, 24])
        rstd = sb("rstd", [P, TOK])
        cT = sb("cT", [P, KT, NC])
        wsm = sb("wsm", [P, KT, 24])
        MIX = 28970
        NA = MIX + (NU + ZT) * TOK
        arena = sb("arena", [P, NA])

        def carve(at, *shape, parts=P):
            n = 1
            for d in shape:
                n *= d
            assert at + n <= NA, (at, shape)
            ap = arena[0:parts, at:at + n]
            if len(shape) == 2:
                ap = ap.rearrange("p (a b) -> p a b", b=shape[1])
            if len(shape) == 3:
                ap = ap.rearrange("p (a b c) -> p a b c", b=shape[1], c=shape[2])
            return ap, at + n

        CO, at = carve(MIX, NU, TOK)
        ZC, at = carve(at, ZT, TOK)
        at = 0
        ada_ring, w_ring = [], []
        for _ in range(2):
            v, at = carve(at, KT, ADA_N)
            ada_ring.append(v)
        for _ in range(2):
            v, at = carve(at, KT, WN)
            w_ring.append(v)
        U, at = carve(at, NU, ROW)
        cv_at = at
        cv, at = carve(at, NQ, CROW)
        dn_halo, q = carve(cv_at, QKV, parts=NB * HALO)
        ssm_halo, q = carve(q, QKV, parts=NB * HALO)
        tabA, q = carve(q, P, parts=A_ROWS)
        tabB, q = carve(q, P, parts=B_ROWS)
        c_tok, _ = carve(at, D, parts=NC)
        HN, at = carve(at, KT, TOK)
        sq, _ = carve(at, KT, TOK)
        x_tok, at = carve(at, 3, D)
        at = 0
        Sin, at = carve(at, DH, NB, P)
        Hs, at = carve(at, 4, NB, P)
        cst, q = carve(at, NU, P, parts=27)
        c_new, q = carve(q, NU, 27)
        HsT, at = carve(at, NB, 4 * P)
        hT_out, _ = carve(at, KT, P)
        D2, at = carve(at, 8, P)
        EB, at = carve(at, 8, P)
        Qd, at = carve(at, DH, P)
        CBd, _ = carve(at, 8, P)
        Lt, at = carve(at, DH, P)
        Mk, at = carve(at, DH, P)
        CE, _ = carve(at, 8, P)
        Y, at = carve(at, DH, P)
        Yt, at = carve(at, DH, P)
        Wt, at = carve(at, DH, P)
        kTok, at = carve(at, DH, P)
        vTok, at = carve(at, DH, P)
        R, at = carve(at, DH, P)
        xdt, at = carve(at, 8, HD)
        xw, at = carve(at, 8, HD)
        vnew, at = carve(at, DH, P)
        kd, at = carve(at, DH, P)
        qe, at = carve(at, DH, P)
        Bm, _ = carve(at, NB, P, parts=SMP)
        Vm = []
        for _ in range(2):
            v, at = carve(at, NB, P, parts=SMP)
            Vm.append(v)
        Bt, at = carve(at, P)
        rs, at = carve(at, DH, P)
        sqm, at = carve(at, DH, P)
        Km, at = carve(at, NB, DH, SMP)
        Sd, at = carve(at, DH, P)
        hT, at = carve(at, SH, HD)

        w_dn, at = carve(0, DH, D)
        w_so, at = carve(at, KT, D)
        w_o, at = carve(at + 2 * 8 * P, KT, D)
        merged, at = carve(at, KT, TOK)
        mtmp, at = carve(at, 2, TOK)
        assert at <= MIX
        at = 0
        ex = []
        for i in range(ESLOT):
            at = (0, EXW, MIX, MIX + EXW)[i]
            wg, at = carve(at, KT, FF)
            wu, at = carve(at, KT, FF)
            wd, at = carve(at, FT, D)
            ex.append((wg, wu, wd))
        H2, at = carve(at, KT, TOK)
        XsT, at = carve(2 * EXW, KT, SLOTS)
        ys_at = at
        YsT, at = carve(at, KT, SLOTS)
        h2_tok, at = carve(at, 3, D)
        Pm, at = carve(at, 3, SLOTS)
        wbc, at = carve(at, SLOTS)
        iota, at = carve(at, SLOTS)
        assert at <= MIX
        Pw, q = carve(ys_at, 3, SLOTS)
        LG, q = carve(q, 3, EG + E)
        r_em, q = carve(q, 3, E)
        r_eq, q = carve(q, 3, E)
        r_o1, q = carve(q, 3, E)
        r_o2, q = carve(q, 3, E)
        r_sp, q = carve(q, 3, E)
        r_g, q = carve(q, 3, EG)
        r_g2, q = carve(q, 3, EG)
        r_m, q = carve(q, 10, 3)
        r_n, q = carve(q, 4, E)
        r_c, q = carve(q, E)
        second, q = carve(q, SLOTS)
        assert q <= ys_at + KT * SLOTS
        Ys, _ = carve(2 * EXW, ST, D)
        PT, _ = carve(ys_at + KT * SLOTS, ST, TOK)
        y_fin, _ = carve(ys_at, KT, TOK)
        o_tok, _ = carve(0, 3, D)
        w_rt = sb("w_rt", [P, KT, EG + E])
        b_rt = sb("b_rt", [P, EG + E])
        valid = sb("valid", [P, 3])
        tab = sb("tab", [P, 3, E], I32)
        hact = sb("hact", [P, FT, CW])
        bias_row = sb("bias_row", [P, NG])
        alog_row = sb("alog_row", [P, NG])
        dcol = sb("dcol", [SH, NC])
        sp = sb("sp", [P, 3, NG])
        t1 = sb("t1", [P, 3, NG])
        t2 = sb("t2", [P, 3, NG])
        G = sb("G", [P, 3, NG])
        csum = sb("csum", [P, 3, NG])
        ecs = sb("ecs", [P, 3, NG])
        dte = sb("dte", [P, 3, NG])
        beta = sb("beta", [P, 3, DH])
        nbeta = sb("nbeta", [P, 3, DH])
        elast = sb("elast", [P, 2, NG])
        GM = sb("GM", [SMP, NG, NB])
        EL2 = sb("EL2", [P, NG, NB])
        drep = sb("drep", [P, KT, NC])

        ps = ctx.enter_context(nc.psum_tensor("ps", [P, 8, 512], F32))

        def heads(i, n, cols, parts=P, width=P):
            k = -(-n * width // 512)
            v = ps[0:parts, i:i + k, :].rearrange("p a (h c) -> p (a h) c", c=width)
            return v[:, 0:n, 0:cols]

        wi = T["w_in"][0].rearrange("(k p) n -> p k n", p=P)
        block = ctx.enter_context(nc.Block())

        def tail_loads(e, load, store):
            e.wait_ge(S("y_out"), 6)
            load(w_o, T["w_out"][0].rearrange("(k p) n -> p k n", p=P), "wo_ld")
            wg_, wu_, wd_ = (T[n][0].rearrange("e (k p) f -> p e k f", p=P) for n in ("w_exp_gate", "w_exp_up", "w_exp_down"))

            def expert(idx, s):
                wg, wu, wd = ex[s]
                for dst, src in ((wg, wg_), (wu, wu_), (wd, wd_)):
                    load(dst, src[:, bass.ds(idx, 1)].rearrange("p e k f -> p (e k) f"), f"ex_ld{s}")

            e.wait_ge(S("ssm_mm"), KT)
            expert(0, 0)
            expert(1, 1)
            e.wait_ge(S("merged"), KT)
            expert(2, 2)
            expert(3, 3)
            e.wait_ge(S("tab"), 1)
            with e.Fori(1, E // ESLOT) as i:
                for s in range(ESLOT):
                    idx = e.snap(i * ESLOT + s, min_val=0, max_val=E - 1)
                    end = e.value_load(tab[0:1, 1, bass.ds(i * ESLOT + (s - ESLOT), 1)], min_val=1, max_val=E * 5)
                    e.wait_ge(S("down_mm"), end)
                    expert(idx, s)
            for t, (o, p) in enumerate(TILES):
                e.wait_ge(S("o_tok"), 2 * t + 2)
                if t < 2:
                    store(O["y_p"][0, o:o + p, :], o_tok[0:p, t, :])
                else:
                    store(O["y_s"].rearrange("b t d -> (b t) d"), o_tok[0:p, t, :])

        def tail_pool_early(e, link):
            g = nc.gpsimd
            link(g.memset(valid[:], 1.0))
            link(g.affine_select(out=valid[:, 2:3], in_=valid[:, 2:3], pattern=[[0, 1]], base=SMP - 1, channel_multiplier=-1,
                                 compare_op=ALU.is_ge, fill=0.0))

        def tail_pool(e, link):
            g = nc.gpsimd
            e.wait_ge(S("y_out"), 6)
            e.wait_ge(S("x2"), KT)
            link(g.iota(iota, pattern=[[1, SLOTS]], base=0, channel_multiplier=0, allow_small_or_imprecise_dtypes=True))
            link(g.memset(LG, 0.0))
            link(g.memset(XsT[:, :, PAIRS:SLOTS], 0.0))
            e.nop().then_inc(S("iota"), 1)

        def tail_pe(e):
            mm, tr = nc.tensor.matmul, nc.tensor.transpose
            e.wait_ge(S("wdn_ld"), 16)
            e.wait_ge(S("wso_ld"), 16)
            e.wait_ge(S("ht_out"), 2)
            for m in range(KT):
                b = 2 * (m % 2)
                if m >= 2:
                    e.wait_ge(S("merged"), m - 1)
                for k in range(DH):
                    mm(ps[:, b, 0:TOK], w_dn[:, k, m * P:(m + 1) * P], CO[:, k, :], start=(k == 0), stop=(k == DH - 1))
                for k in range(KT):
                    l = mm(ps[:, b + 1, 0:TOK], w_so[:, k, m * P:(m + 1) * P], CO[:, NQ + k, :], start=(k == 0), stop=(k == KT - 1))
                l.then_inc(S("ssm_mm"), 1)
            e.wait_ge(S("wo_ld"), 16)
            e.wait_ge(S("merged"), KT)
            for m in range(KT):
                if m >= 2:
                    e.wait_ge(S("x2"), m - 1)
                for k in range(KT):
                    l = mm(ps[:, 4 + m % 2, 0:TOK], w_o[:, k, m * P:(m + 1) * P], merged[:, k, :], start=(k == 0), stop=(k == KT - 1))
                l.then_inc(S("wo_mm"), 1)

            def mean_square(n):
                e.wait_ge(S("sq"), n)
                for k in range(KT):
                    l = mm(ps[:, 0, 0:TOK], ones[:, :], H2[:, k, :], start=(k == 0), stop=(k == KT - 1))
                l.then_inc(S("ms_mm"), 1)

            mean_square(2)
            e.wait_ge(S("h2"), 1)
            e.wait_ge(S("rt_ld"), 64)
            for t, (o, p) in enumerate(TILES):
                for k in range(KT):
                    l = mm(ps[0:p, 1, t * 36:(t + 1) * 36], H2[:, k, o:o + p], w_rt[:, k, :], start=(k == 0), stop=(k == KT - 1))
            l.then_inc(S("rt_mm"), 1)
            for t, (o, p) in enumerate(TILES):
                for half in range(2):
                    for k in range(4):
                        l = tr(ps[0:p, 2 + 2 * t + half if t < 2 else 6 + half, k * P:(k + 1) * P], H2[:, 4 * half + k, o:o + p], ident[:, :])
                    l.then_inc(S("h2t_mm"), 1)
            e.wait_ge(S("assign"), 1)
            for t in range(3):
                for u in range(t):
                    mm(ps[:, 0, t * E:(t + 1) * E], ones[:, :], r_eq[:, u, :], start=(u == 0), stop=False)
                mm(ps[:, 0, t * E:(t + 1) * E], tri[:, :], r_eq[:, t, :], start=(t == 0), stop=True)
            for t in range(3):
                l = mm(ps[:, 0, 3 * E:4 * E], ones[:, :], r_eq[:, t, :], start=(t == 0), stop=(t == 2))
            l.then_inc(S("count_mm"), 1)
            e.wait_ge(S("pw"), 1)
            for t in range(3):
                mm(ps[:, 1, :], ones[:, :], Pw[:, t, 0:512], start=(t == 0), stop=(t == 2))
            for t in range(3):
                l = mm(ps[:, 2, 0:SLOTS - 512], ones[:, :], Pw[:, t, 512:SLOTS], start=(t == 0), stop=(t == 2))
            l.then_inc(S("wbc_mm"), 1)
            e.wait_ge(S("h2_tok"), 6)
            e.wait_ge(S("pm"), 1)
            for k in range(KT):
                b = 4 + 2 * (k % 2)
                if k >= 2:
                    e.wait_ge(S("xs"), k - 1)
                for c0, n in ((0, 512), (512, PAIRS - 512)):
                    for t, (o, p) in enumerate(TILES):
                        l = mm(ps[:, b + c0 // 512, 0:n], h2_tok[0:p, t, k * P:(k + 1) * P], Pm[0:p, t, c0:c0 + n],
                               start=(t == 0), stop=(t == 2))
                l.then_inc(S("xs_mm"), 1)
            e.wait_ge(S("xs"), KT)
            e.wait_ge(S("wbc"), 1)
            e.wait_ge(S("tab"), 1)
            with e.Fori(0, E // ESLOT) as i:
                for s in range(ESLOT):
                    wg, wu, wd = ex[s]
                    e.wait_ge(S(f"ex_ld{s}"), i * 48 + 48)
                    first, end, slot = expert_range(e, i, s)
                    with e.Fori(first, end) as c:
                        off = window(e, c, first, slot)
                        for w, b in ((wg, 0), (wu, 1)):
                            for f in range(FT):
                                for k in range(KT):
                                    l = mm(ps[:, b, f * CW:(f + 1) * CW], w[:, k, f * P:(f + 1) * P], XsT[:, k, bass.ds(off, CW)],
                                           start=(k == 0), stop=(k == KT - 1))
                        l.then_inc(S("gu_mm"), 1)
                        e.wait_ge(S("hact"), c + 1)
                        for m in range(KT):
                            for f in range(FT):
                                l = mm(ps[:, 2, m * CW:(m + 1) * CW], wd[:, f, m * P:(m + 1) * P], hact[:, f, :],
                                       start=(f == 0), stop=(f == FT - 1))
                        l.then_inc(S("down_mm"), 1)
            e.wait_ge(S("ys_done"), 1)
            for s in range(ST):
                w = min(P, PAIRS - s * P)
                for half in range(2):
                    i = 2 * s + half
                    if i >= 4:
                        e.wait_ge(S("ys"), i - 3)
                    for k in range(4):
                        l = tr(ps[0:w, 4 + i % 4, k * P:(k + 1) * P], YsT[:, 4 * half + k, s * P:s * P + w], ident[:, :])
                    l.then_inc(S("ys_mm"), 1)
                if s >= 2:
                    e.wait_ge(S("pt"), s - 1)
                for t, (o, p) in enumerate(TILES):
                    l = tr(ps[0:w, s % 2, o:o + p], Pm[0:p, t, s * P:s * P + w], ident[0:p, 0:p])
                l.then_inc(S("pt_mm"), 1)
            e.wait_ge(S("ys"), 2 * ST)
            e.wait_ge(S("pt"), ST)
            for k in range(KT):
                if k >= 2:
                    e.wait_ge(S("x3"), k - 1)
                for s in range(ST):
                    w = min(P, PAIRS - s * P)
                    l = mm(ps[:, 2 + k % 2, 0:TOK], Ys[0:w, s, k * P:(k + 1) * P], PT[0:w, s, :], start=(s == 0), stop=(s == ST - 1))
                l.then_inc(S("comb_mm"), 1)
            mean_square(3)
            e.wait_ge(S("y_fin"), 1)
            for t, (o, p) in enumerate(TILES):
                for half in range(2):
                    i = 2 * t + half
                    for k in range(4):
                        l = tr(ps[0:p, 2 + i, k * P:(k + 1) * P], y_fin[:, 4 * half + k, o:o + p], ident[:, :])
                    l.then_inc(S("ot_mm"), 1)

        def expert_range(e, i, s):
            at_ = i * ESLOT + s
            return (e.value_load(tab[0:1, 0, bass.ds(at_, 1)], min_val=0, max_val=5 * E - 1),
                    e.value_load(tab[0:1, 1, bass.ds(at_, 1)], min_val=1, max_val=5 * E),
                    e.value_load(tab[0:1, 2, bass.ds(at_, 1)], min_val=0, max_val=PAIRS))

        def window(e, c, first, slot):
            return nc.s_assert_within((c - first) * CW + slot, min_val=0, max_val=PAIRS, 
                                      skip_runtime_bounds_check_because="a chunk starts before its expert's end, at slot 576 at most")

        def tail_act(e):
            act = nc.scalar.activation
            e.wait_ge(S("x2"), KT)
            e.wait_ge(S("merged"), KT)
            act(H2, xT[:], ACT.Square).then_inc(S("sq"), 1)
            e.wait_ge(S("ms"), 2)
            act(rstd[:], rstd[:], ACT.Sqrt).then_inc(S("root"), 1)
            for t, (o, p) in enumerate(TILES):
                for half in range(2):
                    e.wait_ge(S("h2t_mm"), 2 * t + half + 1)
                    act(h2_tok[0:p, t, half * 512:(half + 1) * 512], ps[0:p, 2 + 2 * t + half if t < 2 else 6 + half, :],
                        ACT.Copy).then_inc(S("h2_tok"), 1)
            e.wait_ge(S("r_exp_arg"), 1)
            act(r_g2, r_g2, ACT.Exp)
            act(r_m[:, 6, :], r_m[:, 6, :], ACT.Exp).then_inc(S("r_exp"), 1)
            e.wait_ge(S("wbc_mm"), 1)
            act(wbc[:, 0:512], ps[:, 1, :], ACT.Copy)
            act(wbc[:, 512:SLOTS], ps[:, 2, 0:SLOTS - 512], ACT.Copy).then_inc(S("wbc"), 1)
            for k in range(KT):
                e.wait_ge(S("xs_mm"), k + 1)
                b = 4 + 2 * (k % 2)
                act(XsT[:, k, 0:PAIRS], ps[:, b:b + 2, :].rearrange("p a n -> p (a n)")[:, 0:PAIRS], ACT.Copy).then_inc(S("xs"), 1)
            e.wait_ge(S("tab"), 1)
            with e.Fori(0, E // ESLOT) as i:
                for s in range(ESLOT):
                    first, end, slot = expert_range(e, i, s)
                    with e.Fori(first, end) as c:
                        off = window(e, c, first, slot)
                        e.wait_ge(S("gu_mm"), c + 1)
                        act(hact[:], ps[:, 0, 0:FT * CW].rearrange("p (f n) -> p f n", f=FT), ACT.Silu).then_inc(S("h_silu"), 1)
                        e.wait_ge(S("down_mm"), c + 1)
                        act(YsT[:, :, bass.ds(off, CW)], ps[:, 2, :].rearrange("p (k n) -> p k n", k=KT), ACT.Copy)
            e.nop().then_inc(S("act_tail"), 1)
            e.wait_ge(S("act_tail"), 1)
            act(eps_c[:], eps_c[:], ACT.Copy).then_inc(S("ys_done"), 1)
            for s in range(ST):
                w = min(P, PAIRS - s * P)
                for half in range(2):
                    i = 2 * s + half
                    e.wait_ge(S("ys_mm"), i + 1)
                    act(Ys[0:w, s, half * 512:(half + 1) * 512], ps[0:w, 4 + i % 4, :], ACT.Copy).then_inc(S("ys"), 1)
            e.wait_ge(S("x3"), KT)
            act(H2, xT[:], ACT.Square).then_inc(S("sq"), 1)
            e.wait_ge(S("ms"), 3)
            act(rstd[:], rstd[:], ACT.Sqrt).then_inc(S("root"), 1)
            for t, (o, p) in enumerate(TILES):
                for half in range(2):
                    i = 2 * t + half
                    e.wait_ge(S("ot_mm"), i + 1)
                    act(o_tok[0:p, t, half * 512:(half + 1) * 512], ps[0:p, 2 + i, :], ACT.Copy).then_inc(S("o_tok"), 1)

        def tail_dve(e, link, norm_scale, inverse_root, modulated):
            v = nc.vector
            tt, ts, stt = v.tensor_tensor, v.tensor_scalar, v.scalar_tensor_tensor

            for m in range(KT):
                e.wait_ge(S("ssm_mm"), m + 1)
                b = 2 * (m % 2)
                if m:
                    e.wait_ge(S("merged"), m)
                tt(mtmp[:, 0, :], ZC[:, 12 + m, :], ps[:, b, 0:TOK], ALU.mult)
                link(tt(mtmp[:, 1, :], ZC[:, 20 + m, :], ps[:, b + 1, 0:TOK], ALU.mult))
                tt(merged[:, m, :], mtmp[:, 0, :], mtmp[:, 1, :], ALU.add).then_inc(S("merged"), 1)

            def gated_add(m, src, gate, sem):
                stt(xT[:, m, 0:SEQ], src[:, 0:SEQ], modT[:, gate + m, 0:1], xT[:, m, 0:SEQ], ALU.mult, ALU.add)
                s = mtmp[:, 0, 0:SMP].rearrange("p (b t) -> p b t", t=NT)
                if m:
                    e.wait_ge(S(sem), m)
                link(tt(s, src[:, SEQ:TOK].rearrange("p (b t) -> p b t", t=NT),
                        modT[:, gate + m, 1:NC].unsqueeze(2).broadcast_to([P, NB, NT]), ALU.mult))
                tt(xT[:, m, SEQ:TOK], xT[:, m, SEQ:TOK], mtmp[:, 0, 0:SMP], ALU.add).then_inc(S(sem), 1)

            for m in range(KT):
                e.wait_ge(S("wo_mm"), m + 1)
                gated_add(m, ps[:, 4 + m % 2, :], GATE1, "x2")
            e.wait_ge(S("x2"), KT)
            norm_scale(colB[:, B_FFN:B_FFN + KT], SCALE2)
            inverse_root("ms_mm", "ms", "root", 2)
            modulated(H2, SHIFT2)
            e.nop().then_inc(S("h2"), 1)

            e.wait_ge(S("rt_mm"), 1)
            e.wait_ge(S("iota"), 1)
            for t, (o, p) in enumerate(TILES):
                l = tt(LG[0:p, t, :], ps[0:p, 1, t * 36:(t + 1) * 36], b_rt[0:p, :], ALU.add)
            link(l)
            gl, el = LG[:, :, 0:EG], LG[:, :, EG:EG + E]

            def first_of(out, src, maximum, n):
                link(v.tensor_reduce(out=maximum, in_=src, op=ALU.max, axis=AX.X))
                link(tt(out, src, maximum.unsqueeze(2).broadcast_to([P, 3, n]), ALU.is_equal))
                for t in range(3):
                    l = stt(out[:, t, :], out[:, t, :], -float(2 * E), iota[:, 0:n], ALU.mult, ALU.add)
                link(l)
                link(v.tensor_reduce(out=r_m[:, 9, :], in_=out, op=ALU.min, axis=AX.X))
                link(tt(out, out, r_m[:, 9, :].unsqueeze(2).broadcast_to([P, 3, n]), ALU.is_equal))

            first_of(r_g, gl, r_m[:, 0, :], EG)
            link(tt(r_g2, gl, r_m[:, 0, :].unsqueeze(2).broadcast_to([P, 3, EG]), ALU.subtract))
            em4 = r_em.rearrange("p t (g x) -> p t g x", g=EG)
            link(tt(em4, el.rearrange("p t (g x) -> p t g x", g=EG), r_g.unsqueeze(3).broadcast_to([P, 3, EG, EPG]), ALU.mult))
            link(ts(r_g, r_g, -NEG, NEG, ALU.mult, ALU.add))
            link(tt(em4, em4, r_g.unsqueeze(3).broadcast_to([P, 3, EG, EPG]), ALU.add))
            first_of(r_o1, r_em, r_m[:, 1, :], E)
            link(stt(r_em, r_o1, 2 * NEG, r_em, ALU.mult, ALU.add))
            first_of(r_o2, r_em, r_m[:, 2, :], E)
            link(tt(r_m[:, 6, :], r_m[:, 2, :], r_m[:, 1, :], ALU.subtract))
            e.nop().then_inc(S("r_exp_arg"), 1)
            for oh in (r_o1, r_o2):
                link(tt(oh, oh, valid[:].unsqueeze(2).broadcast_to([P, 3, E]), ALU.mult))
            link(tt(r_eq, r_o1, r_o2, ALU.add))
            e.nop().then_inc(S("assign"), 1)
            e.wait_ge(S("r_exp"), 1)
            link(v.tensor_reduce(out=r_m[:, 3, :], in_=r_g2, op=ALU.add, axis=AX.X))
            link(stt(r_m[:, 3, :], r_m[:, 6, :], 1.0, r_m[:, 3, :], ALU.add, ALU.mult))
            link(v.reciprocal(r_m[:, 4, :], r_m[:, 3, :]))
            link(tt(r_m[:, 5, :], r_m[:, 4, :], r_m[:, 6, :], ALU.mult))
            e.wait_ge(S("count_mm"), 1)
            link(v.tensor_copy(r_n[:, 0, :], ps[:, 0, 3 * E:4 * E]))
            link(v.memset(r_c, 1.0))
            link(v.tensor_tensor_scan(out=r_n[:, 1, :], data0=r_c, data1=r_n[:, 0, :], initial=0.0, op0=ALU.mult, op1=ALU.add))
            link(tt(r_n[:, 1, :], r_n[:, 1, :], r_n[:, 0, :], ALU.subtract))
            link(v.memset(r_n[:, 2, :], 1.0))
            for q_ in range(1, 5):
                link(stt(r_n[:, 2, :], r_n[:, 0, :], float(q_ * CW), r_n[:, 2, :], ALU.is_gt, ALU.add))
            link(v.tensor_tensor_scan(out=r_n[:, 3, :], data0=r_c, data1=r_n[:, 2, :], initial=0.0, op0=ALU.mult, op1=ALU.add))
            tt(tab[:, 0, :], r_n[:, 3, :], r_n[:, 2, :], ALU.subtract)
            v.tensor_copy(tab[:, 1, :], r_n[:, 3, :])
            v.tensor_copy(tab[:, 2, :], r_n[:, 1, :]).then_inc(S("tab"), 1)
            link(tt(r_sp, ps[:, 0, 0:3 * E].rearrange("p (t x) -> p t x", t=3), r_n[:, 1:2, :].broadcast_to([P, 3, E]), ALU.add))
            for oh, at_ in ((r_o1, 7), (r_o2, 8)):
                link(tt(oh, oh, r_sp, ALU.mult))
                link(v.tensor_reduce(out=r_m[:, at_, :], in_=oh, op=ALU.add, axis=AX.X))
                link(ts(r_m[:, at_, :], r_m[:, at_, :], -1.0, None, ALU.add))
            for t in range(3):
                s1, s2, w1, w2 = (r_m[:, x, t:t + 1] for x in (7, 8, 4, 5))
                ts(Pm[:, t, :], iota, s1, None, ALU.is_equal)
                link(ts(Pw[:, t, :], iota, s1, w1, ALU.is_equal, ALU.mult))
                stt(Pm[:, t, :], iota, s2, Pm[:, t, :], ALU.is_equal, ALU.add)
                link(ts(second, iota, s2, w2, ALU.is_equal, ALU.mult))
                link(tt(Pw[:, t, :], Pw[:, t, :], second, ALU.add))
            e.nop().then_inc(S("pm"), 1)
            e.nop().then_inc(S("pw"), 1)

            e.wait_ge(S("wbc"), 1)
            with e.Fori(0, E // ESLOT) as i:
                for s in range(ESLOT):
                    first, end, slot = expert_range(e, i, s)
                    with e.Fori(first, end) as c:
                        off = window(e, c, first, slot)
                        e.wait_ge(S("h_silu"), c + 1)
                        tt(hact[:], hact[:], ps[:, 1, 0:FT * CW].rearrange("p (f n) -> p f n", f=FT), ALU.mult).then_inc(S("h_up"), 1)
                        e.wait_ge(S("h_up"), c + 1)
                        tt(hact[:], hact[:], wbc[:, bass.ds(off, CW)].unsqueeze(1).broadcast_to([P, FT, CW]), ALU.mult).then_inc(S("hact"), 1)
            for s in range(ST):
                w = min(P, PAIRS - s * P)
                e.wait_ge(S("pt_mm"), s + 1)
                v.tensor_copy(PT[0:w, s, :], ps[0:w, s % 2, 0:TOK]).then_inc(S("pt"), 1)
            for k in range(KT):
                e.wait_ge(S("comb_mm"), k + 1)
                gated_add(k, ps[:, 2 + k % 2, :], GATE2, "x3")
            e.wait_ge(S("x3"), KT)
            norm_scale(colB[:, B_FIN:B_FIN + KT], SCALE_F)
            inverse_root("ms_mm", "ms", "root", 3)
            modulated(y_fin, SHIFT_F)
            e.nop().then_inc(S("y_fin"), 1)

        @block.sync
        def _(e):
            def load(dst, src, s):
                e.dma_start(dst, src).then_inc(S(s), 16)

            stores = [0]

            def store(dst, src):
                e.dma_start(dst, src).then_inc(S("stored"), 16)
                stores[0] += 1

            load(c_tok[0:1, :], T["c_prompt"], "c_ld")
            load(c_tok[1:NC, :], T["c_sample"], "c_ld")
            wa = T["w_ada"][0].rearrange("(k p) n -> p k n", p=P)
            wf = T["w_ada_final"].rearrange("(k p) n -> p k n", p=P)
            for sl in range(2):
                load(ada_ring[sl], wa[:, :, sl * ADA_N:(sl + 1) * ADA_N], f"ada_ld{sl}")
            r = 0
            for n, k in (("b_ada", 48), ("norm_mix_w", 8)):
                load(tabA[r:r + k, :], T[n][0].rearrange("(m p) -> m p", p=P), "tab_ld")
                r += k
            load(tabA[r:r + 48, :], T["dn_conv_w"][0].rearrange("i (m p) -> (i m) p", p=P), "tab_ld")
            load(tabB[0:48, :], T["ssm_conv_w"][0].rearrange("i (m p) -> (i m) p", p=P), "tab_ld")
            r = 48
            for n, k in (("ssm_conv_b", 12), ("ssm_norm_w", 8), ("norm_ffn_w", 8),
                         ("b_ada_final", 16), ("final_norm_w", 8), ("dn_norm_w", 1)):
                a = T[n] if n in ("b_ada_final", "final_norm_w") else T[n][0]
                load(tabB[r:r + k, :], a.rearrange("(m p) -> m p", p=P), "tab_ld")
                r += k
            for t in range(2):
                load(x_tok[:, t, :], T["x_prompt"][0, t * P:(t + 1) * P, :], "x_ld")
            load(x_tok[0:SMP, 2, :], T["x_sample"].rearrange("b t d -> (b t) d"), "x_ld")
            for sl in range(2):
                e.wait_ge(S("mod_mm"), sl + 1)
                load(ada_ring[sl], wa[:, :, (2 + sl) * ADA_N:(3 + sl) * ADA_N], f"ada_ld{sl}")
            load(wsm[:, :, 0:4], wi[:, :, C_A:C_A + 4], "small_ld")
            load(wsm[:, :, 4:20], wi[:, :, C_DT:C_DT + 16], "small_ld")
            load(wsm[:, :, 20:24], wi[:, :, C_B:C_B + 4], "small_ld")
            load(bias_row[:, 0:4], T["dn_dt_bias"].broadcast_to([P, 4]), "small_ld")
            load(bias_row[:, 4:20], T["ssm_dt_bias"].broadcast_to([P, 16]), "small_ld")
            load(alog_row[:, 0:4], T["dn_A_log"].broadcast_to([P, 4]), "small_ld")
            load(alog_row[:, 4:20], T["ssm_A_log"].broadcast_to([P, 16]), "small_ld")
            load(dcol[:, NB:NC], T["ssm_D"].rearrange("o h -> h o"), "small_ld")
            load(dn_halo, T["state_dn_conv"][0].rearrange("b t c -> (b t) c"), "halo_ld")
            load(ssm_halo, T["state_ssm_conv"][0].rearrange("b t c -> (b t) c"), "halo_ld")
            load(w_rt[:, :, 0:EG], T["w_group_router"][0].rearrange("(k p) n -> p k n", p=P), "rt_ld")
            load(w_rt[:, :, EG:], T["w_expert_router"][0].rearrange("(k p) n -> p k n", p=P), "rt_ld")
            load(b_rt[:, 0:EG], T["b_group_router"].broadcast_to([P, EG]), "rt_ld")
            load(b_rt[:, EG:], T["b_expert_router"].broadcast_to([P, E]), "rt_ld")
            done = 0
            for n, first in RUNS:
                wada, ada_first = (wf, -9 * ADA_N) if done == 9 else (wa, 3 * ADA_N)
                if done == 0:
                    for sl in range(2):
                        load(w_ring[sl], wi[:, :, first + sl * WN:first + (sl + 1) * WN], f"win_ld{sl}")
                with e.Fori(1 if done == 0 else 0, n) as i:
                    e.wait_ge(S("mod_mm"), i + (done + 3))
                    e.wait_ge(S("proj_mm"), i * 4 + (4 * done - 2))
                    load(w_ring[0], wi[:, :, bass.ds(i * (2 * WN) + first, WN)], "win_ld0")
                    load(ada_ring[0], wada[:, :, bass.ds(i * ADA_N + (done * ADA_N + ada_first), ADA_N)], "ada_ld0")
                    e.wait_ge(S("proj_mm"), i * 4 + 4 * done)
                    load(w_ring[1], wi[:, :, bass.ds(i * (2 * WN) + (first + WN), WN)], "win_ld1")
                done += n
            e.wait_ge(S("mod_mm"), 16)
            for h in range(DH):
                load(Sin[:, h], T["state_dn_rec"][0, :, h].rearrange("b k v -> k b v"), "sin_ld")
            hs_in = T["state_ssm_rec"][0].rearrange("b h p n -> (h p) b n")
            hs_out = O["ssm_rec_s"][0].rearrange("b h p n -> (h p) b n")
            for j in range(4):
                load(Hs[:, j], hs_in[j * P:(j + 1) * P], "hs_ld0")
            e.wait_ge(S("cstate"), 2)
            for name, c0 in (("dn_conv", 0), ("ssm_conv", NQ)):
                store(O[name + "_p"][0, 0], cst[0:3, c0:c0 + NQ, :].rearrange("p a b -> p (a b)"))
                store(O[name + "_s"][0].rearrange("b t c -> (b t) c"),
                      cst[3:27, c0:c0 + NQ, :].rearrange("p a b -> p (a b)"))
            e.wait_ge(S("stored"), 64)
            e.nop().then_inc(S("cstate_stored"), 1)
            for h in range(DH):
                e.wait_ge(S("sin_new"), h + 1)
                store(O["dn_rec_s"][0, :, h].rearrange("b k v -> k b v"), Sin[:, h])
            for g in range(2):
                for j in range(4):
                    e.wait_ge(S("hs_new"), 4 * g + j + 1)
                    e.dma_start(hs_out[(4 * g + j) * P:(4 * g + j + 1) * P], Hs[:, j]).then_inc(S("hs_stored"), 16)
                e.wait_ge(S("hs_stored"), 64 * (g + 1))
                if g == 0:
                    for j in range(4):
                        load(Hs[:, j], hs_in[(4 + j) * P:(5 + j) * P], "hs_ld1")
            e.wait_ge(S("stored"), 16 * stores[0])
            load(w_dn, T["w_dn_out"][0].rearrange("(k p) n -> p k n", p=P), "wdn_ld")
            load(w_so, T["w_ssm_out"][0].rearrange("(k p) n -> p k n", p=P), "wso_ld")
            e.wait_ge(S("sd_new"), 2)
            store(O["dn_rec_p"][0, 0].rearrange("h k v -> k h v"), Sd)
            e.wait_ge(S("ht_out"), 2)
            store(O["ssm_rec_p"][0, 0].rearrange("(j a) p n -> (a p) j n", a=2), hT_out)
            tail_loads(e, load, store)
            e.wait_ge(S("stored"), 16 * stores[0])

        @block.gpsimd
        def _(e):
            n = [0]

            def link(ins):
                n[0] += 1
                ins.then_inc(S("pool_chain"), 1)
                e.wait_ge(S("pool_chain"), n[0])

            g = nc.gpsimd
            tail_pool_early(e, link)

            def select(ap, pattern, base, mult, op=ALU.is_ge, fill=0.0):
                link(g.affine_select(out=ap, in_=ap, pattern=pattern, base=base, channel_multiplier=mult,
                                     compare_op=op, fill=fill))

            link(g.memset(ident[:], 0.0))
            select(ident[:], [[-1, P]], 0, 1, ALU.not_equal, 1.0)
            link(g.memset(ones[:], 1.0))
            link(g.memset(eps_c[:], EPS))
            link(g.memset(U[:, :, 0:HALO], 0.0))
            link(g.memset(gsm[:], 0.0))
            g.memset(dcol[:, 0:NB], 0.0).then_inc(S("consts0"), 1)
            link(g.memset(tri[:], 1.0))
            select(tri[:], [[1, P]], 0, -1)
            link(g.memset(neg[:], 0.0))
            select(neg[:], [[1, P]], 0, -1, fill=NEG)
            for m, start, fill in ((tri_s, 1.0, 0.0), (neg_s, 0.0, NEG)):
                link(g.memset(m[:], start))
                select(m[:], [[1, SMP]], 0, -1, fill=fill)
                select(m[:].rearrange("p (b t) -> p b t", t=NT), [[-NT, NB], [0, NT]], 0, 1, fill=fill)
            link(g.memset(same_s[:], 1.0))
            select(same_s[:].rearrange("p (b t) -> p b t", t=NT), [[-NT, NB], [0, NT]], 0, 1)
            select(same_s[:].rearrange("p (b t) -> p b t", t=NT), [[NT, NB], [0, NT]], NT - 1, -1)
            link(g.memset(seq_of[:], 1.0))
            select(seq_of[:], [[-NT, NB]], 0, 1)
            select(seq_of[:], [[NT, NB]], NT - 1, -1)
            link(g.memset(level[:], 0.0))
            for l in range(7):
                s = 1 << l
                odd = level[:, l, :].rearrange("p (n c s) -> p n c s", c=2, s=s)[:, :, 1, :]
                link(g.memset(odd, 1.0))
                select(odd, [[-2 * s, P // (2 * s)], [0, s]], 0, 1)
                select(odd, [[2 * s, P // (2 * s)], [0, s]], s - 1, -1)
            link(g.memset(head_rows[:], 0.0))
            hv = head_rows[:].rearrange("p j (a c) -> p j a c", a=2)
            g.affine_select(out=hv, in_=hv, pattern=[[-2, KT], [-1, 2], [0, HD]], base=0, channel_multiplier=1,
                            compare_op=ALU.not_equal, fill=1.0).then_inc(S("consts"), 1)
            e.wait_ge(S("proj_read"), 52)
            link(g.tensor_copy(out=c_new[:, :, 0:HALO], in_=U[:, :, SROW - HALO:SROW]))
            for b in range(NB):
                c0 = SROW + b * STEP + NT
                link(g.tensor_copy(out=c_new[:, :, HALO * (b + 1):HALO * (b + 2)], in_=U[:, :, c0:c0 + HALO]))
            e.nop().then_inc(S("c_new"), 1)
            e.wait_ge(S("qk_normed"), 1)
            e.wait_ge(S("conv_done"), 1)
            link(g.memset(Km, 0.0))
            for b in range(NB):
                c0 = SEQ + b * NT
                link(g.tensor_copy(out=Km[:, b, :, b * NT:(b + 1) * NT], in_=CO[:, DH:2 * DH, c0:c0 + NT]))
            e.nop().then_inc(S("km"), 1)
            e.wait_ge(S("vnew"), 1)
            for h in range(DH):
                if h >= 2:
                    e.wait_ge(S("sin_mm"), h - 1)
                link(g.tensor_tensor(out=Vm[h % 2], in0=vnew[0:SMP, h:h + 1, :].broadcast_to([SMP, NB, P]),
                                     in1=seq_of[:].unsqueeze(2).broadcast_to([SMP, NB, P]), op=ALU.mult))
                e.nop().then_inc(S("vm"), 1)
            e.wait_ge(S("o_mm"), 1)
            for h in range(DH):
                link(g.tensor_tensor(out=Sin[:, h], in0=Sin[:, h],
                                     in1=EL2[:, h, :].unsqueeze(2).broadcast_to([P, NB, P]), op=ALU.mult))
                e.nop().then_inc(S("sin_decayed"), 1)
            for h in range(2):
                e.wait_ge(S("bt"), h + 1)
                e.wait_ge(S("sin_mm"), DH)
                link(g.tensor_tensor(out=Bm, in0=Bt[0:SMP, :].unsqueeze(1).broadcast_to([SMP, NB, P]),
                                     in1=seq_of[:].unsqueeze(2).broadcast_to([SMP, NB, P]), op=ALU.mult))
                e.nop().then_inc(S("bm"), 1)
                e.wait_ge(S("hst_mm"), 8 * (h + 1))
                for j in range(4):
                    link(g.tensor_tensor(out=Hs[:, j], in0=Hs[:, j],
                                         in1=drep[:, 4 * h + j, 0:NB].unsqueeze(2).broadcast_to([P, NB, P]), op=ALU.mult))
                    e.nop().then_inc(S("hs_decayed"), 1)
            tail_pool(e, link)

        @block.tensor
        def _(e):
            mm, tr = nc.tensor.matmul, nc.tensor.transpose
            e.wait_ge(S("consts0"), 1)
            e.wait_ge(S("c_silu"), 1)
            for k in range(KT):
                l = tr(ps[:, 1, k * NC:(k + 1) * NC], c_tok[:, k * P:(k + 1) * P], ident[0:NC, 0:NC])
            l.then_inc(S("cT_mm"), 1)
            e.wait_ge(S("tab_ld"), 16 * 10)
            tr(ps[:, 0, 0:A_ROWS], tabA, ident[0:A_ROWS, 0:A_ROWS])
            tr(ps[:, 0, 128:128 + B_ROWS], tabB, ident[0:B_ROWS, 0:B_ROWS]).then_inc(S("tab_mm"), 1)

            def ada_block(slot, bank):
                for m in range(4):
                    for k in range(KT):
                        l = mm(ps[:, bank, m * NC:(m + 1) * NC], ada_ring[slot][:, k, m * P:(m + 1) * P], cT[:, k, :],
                               start=(k == 0), stop=(k == KT - 1))
                l.then_inc(S("mod_mm"), 1)

            e.wait_ge(S("cT"), 1)
            for i in range(2):
                for sl in range(2):
                    e.wait_ge(S(f"ada_ld{sl}"), i * 16 + 16)
                    if i:
                        e.wait_ge(S("mod_read"), sl + 1)
                    ada_block(sl, 6 + sl)
                if i == 0:
                    e.wait_ge(S("x_ld"), 48)
                    for k in range(KT):
                        if k >= 4:
                            e.wait_ge(S("xT"), k - 3)
                        for t, (o, p) in enumerate(TILES):
                            l = tr(ps[:, k % 4 + 2, o:o + p], x_tok[0:p, t, k * P:(k + 1) * P], ident[0:p, 0:p])
                        l.then_inc(S("x_mm"), 1)
            e.wait_ge(S("sq"), 1)
            e.wait_ge(S("col"), 1)
            for k in range(KT):
                l = mm(ps[:, 0, 0:TOK], ones[:, :], sq[:, k, :], start=(k == 0), stop=(k == KT - 1))
            l.then_inc(S("ms_mm"), 1)
            e.wait_ge(S("halo_ld"), 32)
            e.wait_ge(S("xT"), 8)
            for i, halo in enumerate((dn_halo, ssm_halo)):
                for m in range(NQ):
                    l = tr(ps[:, 2 + i, m * 24:(m + 1) * 24], halo[:, m * P:(m + 1) * P], ident[0:24, 0:24])
                l.then_inc(S("halo_mm"), 1)
            e.wait_ge(S("hn"), 1)
            e.wait_ge(S("small_ld"), 16 * 8)
            for t, (o, p) in enumerate(TILES):
                for k in range(KT):
                    l = mm(ps[0:p, 1, t * 24:(t + 1) * 24], HN[:, k, o:o + p], wsm[:, k, :], start=(k == 0), stop=(k == KT - 1))
            l.then_inc(S("gsm_mm"), 1)
            e.wait_ge(S("halo_read"), 2)
            e.wait_ge(S("mod_read"), 4)

            def project(i, first):
                for sl in range(2):
                    e.wait_ge(S(f"win_ld{sl}"), i * 16 + 16)
                    if not first:
                        e.wait_ge(S("proj_read"), i * 4 + (2 * sl - 2))
                    for m in range(2):
                        for k in range(KT):
                            l = mm(ps[:, 2 + 2 * sl + m, 0:TOK], w_ring[sl][:, k, m * P:(m + 1) * P], HN[:, k, :],
                                   start=(k == 0), stop=(k == KT - 1))
                        l.then_inc(S("proj_mm"), 1)
                    if sl == 0 and not first:
                        e.wait_ge(S("ada_ld0"), i * 16 + 32)
                        e.wait_ge(S("mod_read"), i + 3)
                        ada_block(0, 6)

            project(0, True)
            with e.Fori(1, 13) as i:
                project(i, False)

            e.wait_ge(S("c_new"), 1)
            e.wait_ge(S("proj_read"), 52)
            for i in range(2):
                for m in range(NQ):
                    l = tr(ps[0:27, 3 * i + m // 4, (m % 4) * P:(m % 4 + 1) * P], c_new[:, NQ * i + m, :], ident[:, :])
                l.then_inc(S("cstate_mm"), 1)
            e.wait_ge(S("cstate"), 2)
            e.wait_ge(S("qk_sq"), 1)
            for m in range(2 * DH):
                if m >= 4:
                    e.wait_ge(S("qk_root"), m - 3)
                mm(ps[:, m % 4, 0:TOK], ones[:, :], sq[:, m, :], start=True, stop=True).then_inc(S("qk_mm"), 1)
            e.wait_ge(S("consts"), 1)
            e.wait_ge(S("gates"), 1)
            e.wait_ge(S("gm"), 1)
            for t, (o, p) in enumerate(TILES):
                mm(ps[0:p, 4, t * NG:(t + 1) * NG], (tri if p == P else tri_s)[0:p, 0:p], G[0:p, t, :], start=True, stop=True)
                mm(ps[0:p, 5, t * NG:(t + 1) * NG], (ones if p == P else same_s)[0:p, 0:p], G[0:p, t, :], start=True, stop=True)
            mm(ps[:, 6, 0:NG * NB], ones[0:SMP, :], GM[:].rearrange("p a b -> p (a b)"), start=True, stop=True)
            mm(ps[0:SH, 7, 0:NB], G[0:SMP, 2, DH:NG], seq_of[:], start=True, stop=True).then_inc(S("sums_mm"), 1)
            e.wait_ge(S("dcol"), 1)
            for j in range(KT):
                l = mm(ps[:, 7, 16 + j * NC:16 + (j + 1) * NC], head_rows[:, j, :], dcol[:], start=True, stop=True)
            l.then_inc(S("drep_mm"), 1)
            e.wait_ge(S("sums"), 1)
            e.wait_ge(S("qk_normed"), 1)

            lv = [0]
            for n, t in enumerate(ORDER):
                o, p = TILES[t]
                U_ = (tri if p == P else tri_s)
                if n:
                    e.wait_ge(S("y_out"), 2 * n)
                for h in range(DH):
                    mm(heads(0, DH, p)[:, h], G[0:p, t, h:h + 1].broadcast_to([p, P]), U_[0:p, 0:p], start=True, stop=True)
                for h in range(DH):
                    mm(heads(1, DH, p)[:, h], beta[0:p, t, h:h + 1].broadcast_to([p, P]), ident[0:p, 0:p], start=True, stop=True)
                for h in range(DH):
                    k_, q_ = CO[:, DH + h, o:o + p], CO[:, h, o:o + p]
                    mm(heads(2, DH, p, p)[:, h], k_, k_, start=True, stop=True)
                    mm(heads(3, DH, p, p)[:, h], k_, q_, start=True, stop=True)
                for h in range(DH):
                    tr(heads(4, DH, P, p)[:, h], CO[:, DH + h, o:o + p], ident[:, :])
                    l = tr(heads(5, DH, P, p)[:, h], CO[:, 2 * DH + h, o:o + p], ident[:, :])
                l.then_inc(S("dn_mm"), 1)
                if t == 2:
                    e.wait_ge(S("km"), 1)
                    e.wait_ge(S("sin_ld"), 64)
                    for h in range(DH):
                        for b in range(NB):
                            l = mm(heads(6, DH, P, p)[:, h], Km[:, b, h, :], Sin[:, h, b, :], start=(b == 0), stop=(b == NB - 1))
                    l.then_inc(S("ks_mm"), 1)
                if t == 1:
                    e.wait_ge(S("sd_new"), 1)
                    for h in range(DH):
                        l = mm(heads(6, DH, P, p)[:, h], CO[:, DH + h, o:o + p], Sd[:, h, :], start=True, stop=True)
                    l.then_inc(S("ks_mm"), 1)
                e.wait_ge(S("y0"), n + 1)
                for h in range(DH):
                    l = tr(heads(0, DH, p, p)[:, h], Y[0:p, h, 0:p], ident[0:p, 0:p])
                l.then_inc(S("yt_mm"), 1)
                last = 7 if p == P else 2
                for l_ in range(1, last):
                    e.wait_ge(S("mk"), lv[0] + 1)
                    if l_ == 1:
                        e.wait_ge(S("yt"), n + 1)
                    for h in range(DH):
                        l = mm(heads(1, DH, p, p)[:, h], Mk[0:p, h, 0:p], Yt[0:p, h, 0:p], start=True, stop=True)
                    l.then_inc(S("w_mm"), 1)
                    e.wait_ge(S("w"), lv[0] + 1)
                    for h in range(DH):
                        l = mm(heads(2, DH, p, p)[:, h], Wt[0:p, h, 0:p], Y[0:p, h, 0:p], start=True, stop=True)
                        if l_ < last - 1:
                            l = mm(heads(3, DH, p, p)[:, h], Y[0:p, h, 0:p], Wt[0:p, h, 0:p], start=True, stop=True)
                    l.then_inc(S("wy_mm"), 1)
                    e.wait_ge(S("y_up"), lv[0] + 1)
                    lv[0] += 1
                e.wait_ge(S("r"), n + 1)
                for h in range(DH):
                    l = mm(heads(0, DH, P, p)[:, h], Y[0:p, h, 0:p], R[0:p, h, :], start=True, stop=True)
                l.then_inc(S("vnew_mm"), 1)
                e.wait_ge(S("vnew"), n + 1)
                for h in range(DH):
                    out = heads(4, DH, p)[:, h]
                    l = mm(out, vnew[0:p, h, :], Qd[0:p, h, 0:p], start=True, stop=(t == 0), skip_group_check=(t == 2))
                    if t == 1:
                        l = mm(out, Sd[:, h, :], qe[:, h, :], start=False, stop=True)
                    if t == 2:
                        for b in range(NB):
                            l = mm(out[:, b * NT:(b + 1) * NT], Sin[:, h, b, :], qe[:, h, b * NT:(b + 1) * NT],
                                   start=False, stop=(b == NB - 1), skip_group_check=True)
                l.then_inc(S("o_mm"), 1)
                if t != 2:
                    for h in range(DH):
                        l = mm(heads(5, DH, P)[:, h], kd[0:p, h, :], vnew[0:p, h, :], start=True, stop=True)
                    l.then_inc(S("ds_mm"), 1)
                else:
                    for h in range(DH):
                        e.wait_ge(S("vm"), h + 1)
                        if h >= 2:
                            e.wait_ge(S("sin_new"), h - 1)
                        for c in range(2):
                            l = mm(ps[:, 2 * (h % 2) + c, :], kd[0:p, h, :],
                                   Vm[h % 2][:, 4 * c:4 * c + 4, :].rearrange("p b v -> p (b v)"), start=True, stop=True)
                        l.then_inc(S("sin_mm"), 1)
                e.wait_ge(S("o_sq"), n + 1)
                mm(heads(6, DH, p), ones[:, :], sqm[:, :, 0:p], start=True, stop=True).then_inc(S("o_ms"), 1)

                for g in range(2):
                    i = 2 * n + g
                    e.wait_ge(S("o_out"), n + 1)
                    if g:
                        e.wait_ge(S("y_out"), i)
                        if t == 2:
                            e.wait_ge(S("hs_new"), 4)
                    elif t == 2:
                        e.wait_ge(S("sin_new"), DH)
                    B_, C_ = CO[:, 20 + g, o:o + p], CO[:, 22 + g, o:o + p]
                    mm(ps[0:p, 0, 0:p], B_, C_, start=True, stop=True)
                    for h in range(8):
                        mm(heads(1, 8, p)[:, h], G[0:p, t, DH + 8 * g + h:DH + 8 * g + h + 1].broadcast_to([p, P]), U_[0:p, 0:p],
                           start=True, stop=True)
                    tr(ps[0:p, 3, 0:P], B_, ident[:, :])
                    for j in range(4):
                        l = tr(heads(4, 4, P, p)[:, j], CO[:, NQ + 4 * g + j, o:o + p], ident[:, :])
                    l.then_inc(S("s_mm"), 1)
                    if t == 2:
                        e.wait_ge(S(f"hs_ld{g}"), 64)
                        if g == 0:
                            e.wait_ge(S("cstate_stored"), 1)
                        for b in range(NB):
                            if b >= 2:
                                e.wait_ge(S("hst"), 8 * g + b - 1)
                            for j in range(4):
                                l = tr(ps[:, 5 + b % 2, j * P:(j + 1) * P], Hs[:, j, b, :], ident[:, :])
                            l.then_inc(S("hst_mm"), 1)
                    e.wait_ge(S("s_ready"), i + 1)
                    if t == 2:
                        e.wait_ge(S("hst"), 8 * (g + 1))
                    for j in range(4):
                        for a in range(2):
                            h = 2 * j + a
                            out = heads(5, 4, p)[HD * a:HD * (a + 1), j]
                            l = mm(out, xdt[0:p, h, :], CBd[0:p, h, 0:p], start=True, stop=(t != 1))
                            if t == 1:
                                l = mm(out, hT[:, 8 * g + h, :], CE[:, h, :], start=False, stop=True)
                    if t == 2:
                        for j in range(4):
                            for b in range(NB):
                                l = mm(ps[:, 6, (j * NB + b) * 8:(j * NB + b + 1) * 8].rearrange("p (a t) -> p a t", a=2),
                                       HsT[:, b, j * P:(j + 1) * P], CE[:, 2 * j:2 * j + 2, b * NT:(b + 1) * NT],
                                       start=True, stop=True)
                    l.then_inc(S("y_mm"), 1)
                    if t != 2:
                        mm(ps[:, 7, :], Bt[0:p, :], xw[0:p, :, :].rearrange("p a b -> p (a b)"), start=True, stop=True).then_inc(S("dh_mm"), 1)
                    else:
                        e.wait_ge(S("bm"), g + 1)
                        for j in range(4):
                            if j >= 2:
                                e.wait_ge(S("hs_new"), 4 * g + j - 1)
                            for c in range(2):
                                l = mm(ps[:, 1 + 2 * (j % 2) + c, :], xw[0:p, 2 * j:2 * j + 2, :].rearrange("p a b -> p (a b)"),
                                       Bm[:, 4 * c:4 * c + 4, :].rearrange("p b v -> p (b v)"), start=True, stop=True)
                            l.then_inc(S("hs_mm"), 1)
                    e.wait_ge(S("y_sq"), i + 1)
                    for j in range(4):
                        l = mm(ps[:, 0, 0:p], ones[:, :], sqm[:, j, 0:p], start=(j == 0), stop=(j == 3))
                    l.then_inc(S("y_ms"), 1)
            e.wait_ge(S("ht"), 4)
            e.wait_ge(S("y_out"), 6)
            for j in range(KT):
                l = tr(ps[:, 2 + j // 4, (j % 4) * P:(j % 4 + 1) * P], hT[:, 2 * j:2 * j + 2, :].rearrange("p a b -> p (a b)"), ident[:, :])
                if j % 4 == 3:
                    l.then_inc(S("ht_mm"), 1)
            tail_pe(e)

        @block.scalar
        def _(e):
            act = nc.scalar.activation
            n_ = [0]

            def link(ins):
                n_[0] += 1
                ins.then_inc(S("act_chain"), 1)
                e.wait_ge(S("act_chain"), n_[0])

            e.wait_ge(S("c_ld"), 32)
            act(c_tok, c_tok, ACT.Silu).then_inc(S("c_silu"), 1)
            for k in range(KT):
                e.wait_ge(S("x_mm"), k + 1)
                act(xT[:, k, :], ps[:, k % 4 + 2, 0:TOK], ACT.Copy).then_inc(S("xT"), 1)
            e.wait_ge(S("xT"), KT)
            e.wait_ge(S("x_mm"), KT)
            act(sq, xT[:], ACT.Square).then_inc(S("sq"), 1)
            e.wait_ge(S("ms"), 1)
            act(rstd[:], rstd[:], ACT.Sqrt).then_inc(S("root"), 1)
            e.wait_ge(S("gsm1"), 1)
            act(t1[:], t1[:], ACT.Exp, scale=-1.0).then_inc(S("gsm_e"), 1)
            act(nbeta[:], gsm[:, :, NG:24], ACT.Exp, scale=-1.0)
            link(act(alog_row[:], alog_row[:], ACT.Exp))
            e.wait_ge(S("gsm2"), 1)
            act(t2[:], t2[:], ACT.Ln).then_inc(S("gsm_ln"), 1)

            def evac(i, kind):
                for m in range(4):
                    e.wait_ge(S("proj_mm"), i * 4 + (m + 1))
                    src = ps[:, 2 + m, 0:TOK]
                    if kind[0] == "u":
                        tile = i * 4 + (m + kind[1])
                        dst = U[:, bass.ds(tile, 1), :].rearrange("p a n -> p (a n)")
                        act(dst[:, HALO:SROW], src[:, 0:SEQ], ACT.Copy)
                        act(dst[:, SROW:ROW].rearrange("p (b t) -> p b t", t=STEP)[:, :, HALO:STEP],
                            src[:, SEQ:TOK].rearrange("p (b t) -> p b t", t=NT), ACT.Copy).then_inc(S("proj_read"), 1)
                    else:
                        dst = ZC[:, bass.ds(i * 4 + (m + kind[1]), 1), :].rearrange("p a n -> p (a n)")
                        act(dst, src, kind[0]).then_inc(S("proj_read"), 1)

            def mod_evac(i):
                e.wait_ge(S("mod_mm"), i + 4)
                act(modT[:, bass.ds(i * 4 + 12, 4), :], ps[:, 6, 0:4 * NC].rearrange("p (m c) -> p m c", c=NC),
                    ACT.Copy).then_inc(S("mod_read"), 1)

            def conv_silu(first, bias):
                for m in range(NQ):
                    e.wait_ge(S("cv"), first + m + 1)
                    b = {"bias": colB[:, B_CONVB + m:B_CONVB + m + 1]} if bias else {}
                    act(CO[:, first + m, 0:SEQ], cv[:, m, 0:SEQ], ACT.Silu, **b)
                    act(CO[:, first + m, SEQ:TOK].rearrange("p (b t) -> p b t", t=NT),
                        cv_sample(m), ACT.Silu, **b).then_inc(S("co"), 1)

            def cv_sample(m):
                return arena[:, cv_at + m * CROW + SROW:cv_at + m * CROW + SROW + NB * STEP].rearrange(
                    "p (b t) -> p b t", t=STEP)[:, :, 0:NT]

            e.wait_ge(S("halo_read"), 2)
            evac(0, ("u", 0))
            with e.Fori(1, 3) as i:
                evac(i, ("u", 0))
                mod_evac(i)
            with e.Fori(3, 4) as i:
                evac(i, (ACT.Silu, -12))
                mod_evac(i)
            conv_silu(0, False)
            with e.Fori(4, 7) as i:
                evac(i, ("u", -4))
                mod_evac(i)
            with e.Fori(7, 9) as i:
                evac(i, (ACT.Silu, -24))
                mod_evac(i)
            conv_silu(NQ, True)
            with e.Fori(9, 13) as i:
                evac(i, (ACT.Sigmoid, -24))
                mod_evac(i)

            for i in range(2):
                e.wait_ge(S("cstate_mm"), i + 1)
                act(cst[:, NQ * i:NQ * (i + 1), :].rearrange("p a b -> p (a b)"),
                    ps[0:27, 3 * i:3 * i + 3, :].rearrange("p a b -> p (a b)"), ACT.Copy).then_inc(S("cstate"), 1)
            e.wait_ge(S("co"), NU)
            act(sq, CO[:, 0:2 * DH, :], ACT.Square).then_inc(S("qk_sq"), 1)
            for m in range(2 * DH):
                e.wait_ge(S("qk_mm"), m + 1)
                if m == 0:
                    e.wait_ge(S("gates"), 1)
                act(sq[:, m, :], ps[:, m % 4, 0:TOK], ACT.Sqrt, bias=eps_c[:]).then_inc(S("qk_root"), 1)
            e.wait_ge(S("sums_mm"), 1)
            act(dcol[:, 0:NB], ps[0:SH, 7, 0:NB], ACT.Exp).then_inc(S("dcol"), 1)
            e.wait_ge(S("dte_arg"), 1)
            act(dte[:], dte[:], ACT.Exp)
            act(ecs[:], csum[:], ACT.Exp)
            act(elast[:].rearrange("p a b -> p (a b)"), ps[:, 5, 0:2 * NG], ACT.Exp)
            act(EL2[:].rearrange("p a b -> p (a b)"), ps[:, 6, 0:NG * NB], ACT.Exp).then_inc(S("sums"), 1)

            lv = 0
            for n, t in enumerate(ORDER):
                o, p = TILES[t]
                e.wait_ge(S("dn_mm"), n + 1)
                if n:
                    e.wait_ge(S("y_out"), 2 * n)
                act(EB[:, 0:DH, 0:p], heads(0, DH, p), ACT.Exp).then_inc(S("dn_eb"), 1)
                e.wait_ge(S("dn_arg"), n + 1)
                act(D2[0:p, 0:DH, 0:p], D2[0:p, 0:DH, 0:p], ACT.Exp).then_inc(S("dn_exp"), 1)
                e.wait_ge(S("yt_mm"), n + 1)
                act(Yt[0:p, :, 0:p], heads(0, DH, p, p), ACT.Copy).then_inc(S("yt"), 1)
                for l in range(1, 7 if p == P else 2):
                    e.wait_ge(S("w_mm"), lv + 1)
                    act(Wt[0:p, :, 0:p], heads(1, DH, p, p), ACT.Copy).then_inc(S("w"), 1)
                    lv += 1
                e.wait_ge(S("vnew_mm"), n + 1)
                act(vnew[0:p], heads(0, DH, P, p), ACT.Copy).then_inc(S("vnew"), 1)
                e.wait_ge(S("o_mm"), n + 1)
                act(sqm[:, :, 0:p], heads(4, DH, p), ACT.Square).then_inc(S("o_sq"), 1)
                e.wait_ge(S("o_ms"), n + 1)
                act(rs[:, :, 0:p], heads(6, DH, p), ACT.Sqrt, bias=eps_c[:], scale=1.0 / P).then_inc(S("o_root"), 1)
                for g in range(2):
                    i = 2 * n + g
                    e.wait_ge(S("s_mm"), i + 1)
                    e.wait_ge(S("o_out"), n + 1)
                    if g:
                        e.wait_ge(S("y_out"), i)
                    if t:
                        act(EB[:, :, 0:p], heads(1, 8, p), ACT.Exp).then_inc(S("s_eb"), 1)
                    e.wait_ge(S("s_arg"), i + 1)
                    act(D2[0:p, :, 0:p], D2[0:p, :, 0:p], ACT.Exp).then_inc(S("s_exp"), 1)
                    if t == 2:
                        for b in range(NB):
                            e.wait_ge(S("hst_mm"), 8 * g + b + 1)
                            act(HsT[:, b, :], ps[:, 5 + b % 2, :], ACT.Copy).then_inc(S("hst"), 1)
                    e.wait_ge(S("y1"), i + 1)
                    act(sqm[:, :, 0:p], R[:, :, 0:p], ACT.Square).then_inc(S("y_sq"), 1)
                    e.wait_ge(S("y_ms"), i + 1)
                    act(rs[:, 0, 0:p], ps[:, 0, 0:p], ACT.Sqrt, bias=eps_c[:], scale=1.0 / (4 * P)).then_inc(S("y_root"), 1)
            for i in range(2):
                e.wait_ge(S("ht_mm"), i + 1)
                act(hT_out[:, 4 * i:4 * i + 4, :].rearrange("p a b -> p (a b)"), ps[:, 2 + i, :], ACT.Copy).then_inc(S("ht_out"), 1)
            tail_act(e)

        @block.vector
        def _(e):
            v = nc.vector
            tt, ts, stt = v.tensor_tensor, v.tensor_scalar, v.scalar_tensor_tensor
            n_ = [0]

            def link(ins):
                n_[0] += 1
                ins.then_inc(S("dve_chain"), 1)
                e.wait_ge(S("dve_chain"), n_[0])

            e.wait_ge(S("cT_mm"), 1)
            v.tensor_copy(cT[:].rearrange("p a b -> p (a b)"), ps[:, 1, 0:KT * NC]).then_inc(S("cT"), 1)
            e.wait_ge(S("tab_mm"), 1)
            v.tensor_copy(colB[:], ps[:, 0, 128:128 + B_ROWS])
            link(v.tensor_copy(colA[:], ps[:, 0, 0:A_ROWS]))
            e.nop().then_inc(S("col"), 1)
            for i in range(4):
                e.wait_ge(S("mod_mm"), i + 1)
                v.tensor_copy(modT[:, 4 * i:4 * i + 4, :], ps[:, 6 + i % 2, 0:4 * NC].rearrange("p (m c) -> p m c", c=NC)).then_inc(S("mod_read"), 1)
            e.wait_ge(S("mod_read"), 4)

            def mod_bias(first, n, col):
                b = col.unsqueeze(2).broadcast_to([P, n, NC])
                link(tt(modT[:, first:first + n, :], modT[:, first:first + n, :], b, ALU.add))

            def norm_scale(weight, scale):
                link(stt(scl[:], modT[:, scale:scale + KT, :], 1.0, weight.unsqueeze(2).broadcast_to([P, KT, NC]),
                         ALU.add, ALU.mult))

            def modulated(out, shift):
                link(tt(out, xT[:], rstd[:].unsqueeze(1).broadcast_to([P, KT, TOK]), ALU.mult))
                for k in range(KT):
                    ts(out[:, k, 0:SEQ], out[:, k, 0:SEQ], scl[:, k, 0:1], modT[:, shift + k, 0:1], ALU.mult, ALU.add)
                s = out[:, :, SEQ:TOK].rearrange("p k (b t) -> p k b t", t=NT)
                link(tt(s, s, scl[:, :, 1:NC].unsqueeze(3).broadcast_to([P, KT, NB, NT]), ALU.mult))
                link(tt(s, s, modT[:, shift:shift + KT, 1:NC].unsqueeze(3).broadcast_to([P, KT, NB, NT]), ALU.add))

            def inverse_root(mm_sem, ms_sem, root_sem, n):
                e.wait_ge(S(mm_sem), n)
                ts(rstd[:], ps[:, 0, 0:TOK], 1.0 / D, EPS, ALU.mult, ALU.add).then_inc(S(ms_sem), 1)
                e.wait_ge(S(root_sem), n)
                link(v.reciprocal(rstd[:], rstd[:]))

            mod_bias(0, 16, colA[:, 0:16])
            norm_scale(colA[:, A_NORM:A_NORM + KT], SCALE1)
            inverse_root("ms_mm", "ms", "root", 1)
            modulated(HN, SHIFT1)
            e.nop().then_inc(S("hn"), 1)
            for i in range(2):
                e.wait_ge(S("halo_mm"), i + 1)
                for b in range(NB):
                    l = v.tensor_copy(U[:, NQ * i:NQ * (i + 1), SROW + b * STEP:SROW + b * STEP + HALO],
                                      ps[:, 2 + i, 0:NQ * 24].rearrange("p (m r) -> p m r", r=24)[:, :, 3 * b:3 * b + 3])
                l.then_inc(S("halo_read"), 1)
            e.wait_ge(S("gsm_mm"), 1)
            e.wait_ge(S("consts0"), 1)
            for t, (o, p) in enumerate(TILES):
                v.tensor_copy(gsm[0:p, t, NG:24], ps[0:p, 1, t * 24 + NG:t * 24 + 24])
                l = tt(gsm[0:p, t, 0:NG], ps[0:p, 1, t * 24:t * 24 + NG], bias_row[0:p, :], ALU.add)
            link(l)
            a = gsm[:, :, 0:NG]
            link(ts(t1[:], a, -1.0, None, ALU.mult))
            tt(t1[:], t1[:], a, ALU.max).then_inc(S("gsm1"), 1)
            e.wait_ge(S("gsm_e"), 1)
            link(ts(t2[:], t1[:], 1.0, None, ALU.add))
            link(ts(sp[:], t2[:], -1.0, 1e-30, ALU.add, ALU.add))
            link(v.reciprocal(sp[:], sp[:]))
            link(tt(sp[:], sp[:], t1[:], ALU.mult))
            e.nop().then_inc(S("gsm2"), 1)
            e.wait_ge(S("gsm_ln"), 1)
            e.wait_ge(S("act_chain"), 1)
            link(ts(t2[:], t2[:], 1e-30, None, ALU.add))
            link(tt(sp[:], sp[:], t2[:], ALU.mult))
            link(stt(sp[:], a, 0.0, sp[:], ALU.max, ALU.add))
            ts(nbeta[:], nbeta[:], 1.0, None, ALU.add)
            link(stt(G[:], sp[:], -1.0, alog_row[:].unsqueeze(1).broadcast_to([P, 3, NG]), ALU.mult, ALU.mult))
            link(v.reciprocal(beta[:], nbeta[:]))
            link(ts(nbeta[:], beta[:], -1.0, None, ALU.mult))
            e.nop().then_inc(S("gates"), 1)
            e.wait_ge(S("consts"), 1)
            tt(GM[:], G[0:SMP, 2, :].unsqueeze(2).broadcast_to([SMP, NG, NB]),
               seq_of[:].unsqueeze(1).broadcast_to([SMP, NG, NB]), ALU.mult).then_inc(S("gm"), 1)

            for first, conv in ((0, colA[:, A_CONV:A_CONV + 48]), (NQ, colB[:, B_CONV:B_CONV + 48])):
                for m in range(NQ):
                    tile = first + m
                    e.wait_ge(S("proj_read"), tile + 1 + (4 if first else 0))
                    if first:
                        e.wait_ge(S("co"), m + 1)
                    acc, u = cv[:, m, :], U[:, tile, :]
                    link(ts(acc, u[:, 0:CROW], conv[:, m:m + 1], None, ALU.mult))
                    for i in range(1, 4):
                        l = stt(acc, u[:, i:i + CROW], conv[:, NQ * i + m:NQ * i + m + 1], acc, ALU.mult, ALU.add)
                        if i < 3:
                            link(l)
                    l.then_inc(S("cv"), 1)
            e.wait_ge(S("co"), NU)
            e.nop().then_inc(S("conv_done"), 1)
            e.wait_ge(S("mod_read"), 16)
            mod_bias(16, 32, colA[:, 16:48])
            mod_bias(48, 16, colB[:, B_BFIN:B_BFIN + 16])
            for m in range(2 * DH):
                e.wait_ge(S("qk_root"), m + 1)
                link(v.reciprocal(sq[:, m, :], sq[:, m, :]))
                l = stt(CO[:, m, :], sq[:, m, :], P ** -0.5 if m < DH else 1.0, CO[:, m, :], ALU.mult, ALU.mult)
            link(l)
            e.nop().then_inc(S("qk_normed"), 1)
            e.wait_ge(S("sums_mm"), 1)
            link(v.memset(csum[:], 0.0))
            link(v.memset(dte[:], 0.0))
            for t, (o, p) in enumerate(TILES):
                l = v.tensor_copy(csum[0:p, t, :], ps[0:p, 4, t * NG:(t + 1) * NG])
            link(l)
            for t, (o, p) in enumerate(TILES):
                l = tt(dte[0:p, t, :], ps[0:p, 5, t * NG:(t + 1) * NG], csum[0:p, t, :], ALU.subtract)
            link(l)
            e.nop().then_inc(S("dte_arg"), 1)
            e.wait_ge(S("drep_mm"), 1)
            link(v.tensor_copy(drep[:].rearrange("p a b -> p (a b)"), ps[:, 7, 16:16 + KT * NC]))
            e.nop().then_inc(S("drep"), 1)
            e.wait_ge(S("sums"), 1)
            e.wait_ge(S("c_new"), 1)

            lv = [0]
            for n, t in enumerate(ORDER):
                o, p = TILES[t]
                ng = neg if p == P else neg_s
                e.wait_ge(S("dn_mm"), n + 1)
                e.wait_ge(S("dn_eb"), n + 1)
                for h in range(DH):
                    l = stt(D2[0:p, h, 0:p], heads(0, DH, p, p)[:, h], csum[0:p, t, h:h + 1], ng[0:p, 0:p], ALU.subtract, ALU.add)
                l.then_inc(S("dn_arg"), 1)
                v.tensor_copy(kTok[0:p], heads(4, DH, P, p))
                link(v.tensor_copy(vTok[0:p], heads(5, DH, P, p)))
                for h in range(DH):
                    ts(kd[0:p, h, :], kTok[0:p, h, :], dte[0:p, t, h:h + 1], None, ALU.mult)
                e.wait_ge(S("dn_exp"), n + 1)
                dec = D2[0:p, 0:DH, 0:p]
                link(tt(Lt[0:p, :, 0:p], heads(2, DH, p, p), dec, ALU.mult))
                tt(Qd[0:p, :, 0:p], heads(3, DH, p, p), dec, ALU.mult)
                link(tt(Lt[0:p, :, 0:p], heads(1, DH, p, p), Lt[0:p, :, 0:p], ALU.mult))

                def lev(l):
                    return level[0:p, l:l + 1, 0:p].broadcast_to([p, DH, p])

                link(tt(Y[0:p, :, 0:p], Lt[0:p, :, 0:p], lev(0), ALU.mult))
                tt(Mk[0:p, :, 0:p], Lt[0:p, :, 0:p], lev(1), ALU.mult).then_inc(S("mk"), 1)
                link(tt(Y[0:p, :, 0:p], ident[0:p, 0:p].unsqueeze(1).broadcast_to([p, DH, p]), Y[0:p, :, 0:p], ALU.subtract))
                e.nop().then_inc(S("y0"), 1)
                if t == 0:
                    for h in range(DH):
                        l = ts(R[0:p, h, :], vTok[0:p, h, :], beta[0:p, t, h:h + 1], None, ALU.mult)
                else:
                    e.wait_ge(S("ks_mm"), n if t == 1 else 1)
                    for h in range(DH):
                        l = stt(R[0:p, h, :], heads(6, DH, P, p)[:, h], ecs[0:p, t, h:h + 1], vTok[0:p, h, :], ALU.mult, ALU.subtract)
                    link(l)
                    for h in range(DH):
                        l = ts(R[0:p, h, :], R[0:p, h, :], nbeta[0:p, t, h:h + 1], None, ALU.mult)
                    tt(qe[:, :, 0:p], CO[:, 0:DH, o:o + p], EB[:, 0:DH, 0:p], ALU.mult)
                link(l)
                e.nop().then_inc(S("r"), 1)
                last = 7 if p == P else 2
                for l_ in range(1, last):
                    e.wait_ge(S("w_mm"), lv[0] + 1)
                    if l_ < last - 1:
                        tt(Mk[0:p, :, 0:p], Lt[0:p, :, 0:p], lev(l_ + 1), ALU.mult).then_inc(S("mk"), 1)
                    e.wait_ge(S("wy_mm"), lv[0] + 1)
                    if l_ < last - 1:
                        tt(Yt[0:p, :, 0:p], Yt[0:p, :, 0:p], heads(3, DH, p, p), ALU.subtract)
                    tt(Y[0:p, :, 0:p], Y[0:p, :, 0:p], heads(2, DH, p, p), ALU.subtract).then_inc(S("y_up"), 1)
                    lv[0] += 1
                if t == 2:
                    for h in range(DH):
                        e.wait_ge(S("sin_mm"), h + 1)
                        e.wait_ge(S("sin_decayed"), h + 1)
                        tt(Sin[:, h], Sin[:, h], heads(2 * (h % 2), NB, P), ALU.add).then_inc(S("sin_new"), 1)
                else:
                    e.wait_ge(S("ds_mm"), t + 1)
                    e.wait_ge(S("o_mm"), n + 1)
                    if t == 0:
                        l = v.tensor_copy(Sd, heads(5, DH, P))
                    else:
                        for h in range(DH):
                            l = stt(Sd[:, h, :], Sd[:, h, :], elast[:, t, h:h + 1], heads(5, DH, P)[:, h], ALU.mult, ALU.add)
                    l.then_inc(S("sd_new"), 1)
                e.wait_ge(S("o_root"), n + 1)
                link(v.reciprocal(rs[:, :, 0:p], rs[:, :, 0:p]))
                on = CO[:, 0:DH, o:o + p]
                link(tt(on, heads(4, DH, p), rs[:, :, 0:p], ALU.mult))
                link(stt(on, on, colB[:, B_DNORM:B_DNORM + 1], ZC[:, 0:DH, o:o + p], ALU.mult, ALU.mult))
                e.nop().then_inc(S("o_out"), 1)

                for g in range(2):
                    i = 2 * n + g
                    hs = slice(DH + 8 * g, DH + 8 * g + 8)
                    e.wait_ge(S("s_mm"), i + 1)
                    if t:
                        e.wait_ge(S("s_eb"), g + 1 + (2 if t == 1 else 0))
                    for h in range(8):
                        c = DH + 8 * g + h
                        l = stt(D2[0:p, h, 0:p], heads(1, 8, p, p)[:, h], csum[0:p, t, c:c + 1], ng[0:p, 0:p], ALU.subtract, ALU.add)
                    l.then_inc(S("s_arg"), 1)
                    v.tensor_copy(Bt[0:p, :], ps[0:p, 3, 0:P]).then_inc(S("bt"), 1)
                    x8 = heads(4, 8, HD, p, HD)
                    link(tt(xdt[0:p], x8, sp[0:p, t, hs].unsqueeze(2).broadcast_to([p, 8, HD]), ALU.mult))
                    tt(xw[0:p], xdt[0:p], dte[0:p, t, hs].unsqueeze(2).broadcast_to([p, 8, HD]), ALU.mult)
                    e.wait_ge(S("s_exp"), i + 1)
                    l = tt(CBd[0:p, :, 0:p], D2[0:p, :, 0:p], ps[0:p, 0:1, 0:p].broadcast_to([p, 8, p]), ALU.mult)
                    if t:
                        l = tt(CE[:, :, 0:p], EB[:, :, 0:p], CO[:, 22 + g:23 + g, o:o + p].broadcast_to([P, 8, p]), ALU.mult)
                    l.then_inc(S("s_ready"), 1)
                    e.wait_ge(S("y_mm"), i + 1)
                    for j in range(4):
                        l = stt(R[:, j, 0:p], CO[:, NQ + 4 * g + j, o:o + p], drep[:, 4 * g + j, NB:NC], heads(5, 4, p)[:, j],
                                ALU.mult, ALU.add)
                    link(l)
                    if t == 2:
                        inter = ps[:, 6, 0:256].rearrange("p (j b a t) -> p j b a t", j=4, b=NB, a=2)
                        for a in range(2):
                            half = slice(HD * a, HD * (a + 1))
                            for j in range(4):
                                r = R[half, j, 0:p].rearrange("p (b t) -> p b t", t=NT)
                                l = tt(r, r, inter[half, j, :, a, :], ALU.add)
                        link(l)
                    tt(R[:, :, 0:p], R[:, :, 0:p], ZC[:, 4 + 4 * g:8 + 4 * g, o:o + p], ALU.mult).then_inc(S("y1"), 1)
                    if t == 2:
                        for j in range(4):
                            e.wait_ge(S("hs_mm"), 4 * g + j + 1)
                            e.wait_ge(S("hs_decayed"), 4 * g + j + 1)
                            tt(Hs[:, j], Hs[:, j], heads(1 + 2 * (j % 2), NB, P), ALU.add).then_inc(S("hs_new"), 1)
                    else:
                        e.wait_ge(S("dh_mm"), 2 * t + g + 1)
                        hg = hT[:, 8 * g:8 * g + 8, :]
                        dh = heads(7, 8, HD, P, HD)
                        if t == 0:
                            v.tensor_copy(hg, dh).then_inc(S("ht"), 1)
                        else:
                            link(tt(hg, hg, elast[:, t, hs].unsqueeze(2).broadcast_to([P, 8, HD]), ALU.mult))
                            tt(hg, hg, dh, ALU.add).then_inc(S("ht"), 1)
                    e.wait_ge(S("y_root"), i + 1)
                    link(v.reciprocal(rs[:, 0, 0:p], rs[:, 0, 0:p]))
                    for j in range(4):
                        c = B_SNORM + 4 * g + j
                        l = stt(CO[:, NQ + 4 * g + j, o:o + p], R[:, j, 0:p], colB[:, c:c + 1], rs[:, 0, 0:p], ALU.mult, ALU.mult)
                    l.then_inc(S("y_out"), 1)
            tail_dve(e, link, norm_scale, inverse_root, modulated)


_INS = ["x_prompt", "x_sample", "c_prompt", "c_sample", "state_dn_conv", "state_dn_rec", "state_ssm_conv",
        "state_ssm_rec", "w_ada", "b_ada", "norm_mix_w", "w_in", "dn_conv_w", "dn_A_log", "dn_dt_bias", "dn_norm_w",
        "w_dn_out", "ssm_conv_w", "ssm_conv_b", "ssm_A_log", "ssm_dt_bias", "ssm_D", "ssm_norm_w", "w_ssm_out",
        "w_out", "norm_ffn_w", "w_group_router", "b_group_router", "w_expert_router", "b_expert_router",
        "w_exp_gate", "w_exp_up", "w_exp_down", "w_ada_final", "b_ada_final", "final_norm_w"]
_OUTS = [("y_p", (1, 256, 1024)), ("y_s", (8, 4, 1024)), ("dn_conv_p", (1, 1, 3, 1536)), ("dn_rec_p", (1, 1, 4, 128, 128)),
         ("ssm_conv_p", (1, 1, 3, 1536)), ("ssm_rec_p", (1, 1, 16, 64, 128)), ("dn_conv_s", (1, 8, 3, 1536)),
         ("dn_rec_s", (1, 8, 4, 128, 128)), ("ssm_conv_s", (1, 8, 3, 1536)), ("ssm_rec_s", (1, 8, 16, 64, 128))]


def kernel(**inputs):
    import numpy as _np
    import concourse.bacc as _bacc
    from concourse.bass_utils import run_bass_kernel_spmd as _run

    nc = _bacc.Bacc("TRN2", target_bir_lowering=False, num_devices=1)
    arrays, ins, outs = {}, {}, {}
    for name in _INS:
        a = _np.ascontiguousarray(inputs[name])
        arrays[f"in_{name}"] = a
        ins[name] = nc.dram_tensor(f"in_{name}", a.shape, F32, kind="ExternalInput").ap()
    for name, shape in _OUTS:
        outs[name] = nc.dram_tensor(f"out_{name}", shape, F32, kind="ExternalOutput").ap()
    hybrid_step(nc, ins, outs)
    r = _run(nc, [arrays], core_ids=[0])
    return tuple(r.results[0][f"out_{name}"] for name, _ in _OUTS)
```

```python
from contextlib import ExitStack

import concourse.bass as bass
from concourse import mybir

F32 = mybir.dt.float32
I32 = mybir.dt.int32
ALU = mybir.AluOpType
ACT = mybir.ActivationFunctionType
AX = mybir.AxisListType

P = 128
D = 1024
KT = D // P
SEQ = 256
NB, NT = 8, 4
SMP = NB * NT
TOK = SEQ + SMP
TILES = [(0, P), (P, P), (SEQ, SMP)]
HF = P // 2
ORDER = [2, 0, 1]
NC = 1 + NB
CPAD = 32
DH = 4
SH = 16
HD = 64
NG = DH + SH
QKV = 1536
NQ = QKV // P
NU = 2 * NQ
HALO = 3
SROW = HALO + SEQ
STEP = HALO + NT
ROW = SROW + NB * STEP
CROW = ROW - HALO
ADA_N = 512
WN = 256
E = 32
EG, EPG = 4, 8
FF = 256
FT = FF // P
PAIRS = 2 * TOK
CW = 64
SLOTS = PAIRS + CW
ST = SLOTS // P
ESLOT = 4
EXW = 3 * D * FF // P
EPS = 1e-6
NEG = -1.0e30
C_Z, C_A, C_B, C_XBC, C_DT, C_GATE = 1536, 2048, 2052, 2056, 4616, 4632
RUNS = [(4, 0), (5, C_XBC), (4, C_GATE)]
ZT = 28
SHIFT1, SCALE1, GATE1, SHIFT2, SCALE2, GATE2, SHIFT_F, SCALE_F = range(0, 64, 8)
A_BADA, A_NORM, A_CONV = 0, 48, 56
B_CONV, B_CONVB, B_SNORM, B_FFN, B_BFIN, B_FIN, B_DNORM, B_ROWS = 0, 48, 60, 68, 76, 92, 100, 101
A_ROWS = 104


def hybrid_step(nc, T, O):
    ctx = ExitStack()
    with ctx:
        def sb(name, shape, dt=F32):
            return ctx.enter_context(nc.sbuf_tensor(name, shape, dt))

        sems = {}

        def S(name):
            if name not in sems:
                sems[name] = ctx.enter_context(nc.semaphore(name))
            return sems[name]

        ident = sb("ident", [P, P])
        ones = sb("ones", [P, P])
        tri = sb("tri", [P, P])
        neg = sb("neg", [P, P])
        tri_s = sb("tri_s", [SMP, SMP])
        neg_s = sb("neg_s", [SMP, SMP])
        same_s = sb("same_s", [SMP, SMP])
        seq_of = sb("seq_of", [SMP, NB])
        level = sb("level", [P, 7, P])
        head_rows = sb("head_rows", [SH, KT, P])
        eps_c = sb("eps_c", [P, 1])
        xT = sb("xT", [P, KT, TOK])
        modT = sb("modT", [P, 64, NC])
        colA = sb("colA", [P, A_ROWS])
        colB = sb("colB", [P, B_ROWS])
        scl = sb("scl", [P, KT, NC])
        gsm = sb("gsm", [P, 3, 24])
        rstd = sb("rstd", [P, TOK])
        cT = sb("cT", [P, KT, CPAD])
        mod_rows = sb("mod_rows", [P, 2, P])
        wsm = sb("wsm", [P, KT, 24])
        c_new = sb("c_new", [P, NU, 27])
        MIX = 28970
        NA = MIX + (NU + ZT) * TOK
        arena = sb("arena", [P, NA])

        def carve(at, *shape, parts=P):
            n = 1
            for d in shape:
                n *= d
            assert at + n <= NA, (at, shape)
            ap = arena[0:parts, at:at + n]
            if len(shape) == 2:
                ap = ap.rearrange("p (a b) -> p a b", b=shape[1])
            if len(shape) == 3:
                ap = ap.rearrange("p (a b c) -> p a b c", b=shape[1], c=shape[2])
            return ap, at + n

        CO, at = carve(MIX, NU, TOK)
        ZC, at = carve(at, ZT, TOK)
        at = 0
        ada_ring, w_ring = [], []
        for _ in range(2):
            v, at = carve(at, KT, ADA_N)
            ada_ring.append(v)
        for _ in range(2):
            v, at = carve(at, KT, WN)
            w_ring.append(v)
        cst, _ = carve(KT * ADA_N, NU, P, parts=27)
        U, at = carve(at, NU, ROW)
        cv_at = at
        cv, at = carve(at, NQ, CROW)
        dn_halo, q = carve(cv_at, QKV, parts=NB * HALO)
        ssm_halo, q = carve(q, QKV, parts=NB * HALO)
        tabA, q = carve(q, P, parts=A_ROWS)
        tabB, q = carve(q, P, parts=B_ROWS)
        c_tok, _ = carve(at, D, parts=NC)
        HN, at = carve(at, KT, TOK)
        sq, _ = carve(at, KT, TOK)
        x_tok, at = carve(at, 3, D)
        at = 0
        Sin, at = carve(at, DH, NB, P)
        Hs, at = carve(at, 4, NB, P)
        HsT, at = carve(at, NB, 4 * P)
        hT_out, _ = carve(at, KT, P)
        D2, at = carve(at, 8, P)
        EB, at = carve(at, 8, P)
        Qd, at = carve(at, DH, P)
        CBd, _ = carve(at, 8, P)
        Lt, at = carve(at, DH, P)
        Mk, at = carve(at, DH, P)
        CE, _ = carve(at, 8, P)
        Y, at = carve(at, DH, P)
        Yt, at = carve(at, DH, P)
        Wt, at = carve(at, DH, P)
        kTok, at = carve(at, DH, P)
        vTok, at = carve(at, DH, P)
        Yt_c, Y_c, Mk_c, L_c = (m[:, :, c:c + HF] for m in (Yt, Mk) for c in (0, HF))
        R, at = carve(at, DH, P)
        xdt, at = carve(at, 8, HD)
        xw, at = carve(at, 8, HD)
        vnew, at = carve(at, DH, P)
        kd, at = carve(at, DH, P)
        qe, at = carve(at, DH, P)
        Bm, _ = carve(at, NB, P, parts=SMP)
        Vm = []
        for _ in range(2):
            v, at = carve(at, NB, P, parts=SMP)
            Vm.append(v)
        Bt, at = carve(at, P)
        rs, at = carve(at, DH, P)
        sqm, at = carve(at, DH, P)
        Km, at = carve(at, NB, DH, SMP)
        Sd, at = carve(at, DH, P)
        hT, at = carve(at, SH, HD)

        w_dn, at = carve(0, DH, D)
        w_so, at = carve(at, KT, D)
        w_o, at = carve(at + 2 * 8 * P, KT, D)
        merged, at = carve(at, KT, TOK)
        mtmp, at = carve(at, 2, TOK)
        assert at <= MIX
        at = 0
        ex = []
        for i in range(ESLOT):
            at = (0, EXW, MIX, MIX + EXW)[i]
            wgu, at = carve(at, 2 * KT, FF)
            wd, at = carve(at, FT, D)
            ex.append((wgu, wd))
        H2, at = carve(at, KT, TOK)
        XsT, at = carve(2 * EXW, KT, SLOTS)
        ys_at = at
        YsT, at = carve(at, KT, SLOTS)
        tok_at = at
        h2_tok, at = carve(at, 3, D)
        Pm, at = carve(at, 3, SLOTS)
        iota, at = carve(at, SLOTS)
        assert at <= MIX
        Pw, q = carve(ys_at, 3, SLOTS)
        LG, q = carve(q, 3, EG + E)
        r_em, q = carve(q, 3, E)
        r_eq, q = carve(q, 3, E)
        r_o1, q = carve(q, 3, E)
        r_o2, q = carve(q, 3, E)
        r_sp, q = carve(q, 3, E)
        r_g, q = carve(q, 3, EG)
        r_g2, q = carve(q, 3, EG)
        r_m, q = carve(q, 10, 3)
        r_n, q = carve(q, 4, E)
        r_c, q = carve(q, E)
        second, q = carve(q, SLOTS)
        assert q <= ys_at + KT * SLOTS
        Ys, _ = carve(2 * EXW, ST, D)
        PT, q = carve(tok_at, ST, TOK)
        xwin, q = carve(q, KT, CW)
        y_row, q = carve(q, D // 2)
        y_col, q = carve(q, 4, P)
        assert q <= tok_at + 3 * D
        y_fin, _ = carve(ys_at, KT, TOK)
        o_tok, _ = carve(0, 3, D)
        w_rt = sb("w_rt", [P, KT, EG + E])
        b_rt = sb("b_rt", [P, EG + E])
        valid = sb("valid", [P, 3])
        tab = sb("tab", [P, 3, E], I32)
        h_row = sb("h_row", [P, P])
        hact = sb("hact", [P, FT, CW])
        bias_row = sb("bias_row", [P, NG])
        alog_row = sb("alog_row", [P, NG])
        dcol = sb("dcol", [SH, NC])
        sp = sb("sp", [P, 3, NG])
        t1 = sb("t1", [P, 3, NG])
        t2 = sb("t2", [P, 3, NG])
        G = sb("G", [P, 3, NG])
        csum = sb("csum", [P, 3, NG])
        ecs = sb("ecs", [P, 3, NG])
        dte = sb("dte", [P, 3, NG])
        beta = sb("beta", [P, 3, DH])
        nbeta = sb("nbeta", [P, 3, DH])
        elast = sb("elast", [P, 2, NG])
        GM = sb("GM", [SMP, NG, NB])
        EL2 = sb("EL2", [P, NG, NB])
        drep = sb("drep", [P, KT, NC])

        ps = ctx.enter_context(nc.psum_tensor("ps", [P, 8, 512], F32))

        def heads(i, n, cols, parts=P, width=P):
            k = -(-n * width // 512)
            v = ps[0:parts, i:i + k, :].rearrange("p a (h c) -> p (a h) c", c=width)
            return v[:, 0:n, 0:cols]

        wi = T["w_in"][0].rearrange("(k p) n -> p k n", p=P)
        block = ctx.enter_context(nc.Block())

        def tail_loads(e, load, store):
            e.wait_ge(S("y_out"), 6)
            load(w_o, T["w_out"][0].rearrange("(k p) n -> p k n", p=P), "wo_ld")
            wg_, wu_, wd_ = (T[n][0].rearrange("e (k p) f -> p e k f", p=P) for n in ("w_exp_gate", "w_exp_up", "w_exp_down"))

            def expert(idx, s):
                wgu, wd = ex[s]
                for dst, src in ((wgu[:, 0:KT, :], wg_), (wgu[:, KT:2 * KT, :], wu_), (wd, wd_)):
                    load(dst, src[:, bass.ds(idx, 1)].rearrange("p e k f -> p (e k) f"), f"ex_ld{s}")

            e.wait_ge(S("ssm_mm"), KT)
            expert(0, 0)
            expert(1, 1)
            e.wait_ge(S("merged"), KT)
            expert(2, 2)
            expert(3, 3)
            e.wait_ge(S("tab"), 1)
            with e.Fori(1, E // ESLOT) as i:
                for s in range(ESLOT):
                    idx = e.snap(i * ESLOT + s, min_val=0, max_val=E - 1)
                    end = e.value_load(tab[0:1, 1, bass.ds(i * ESLOT + (s - ESLOT), 1)], min_val=1, max_val=E * 5)
                    e.wait_ge(S("down_mm"), end)
                    expert(idx, s)
            for t, (o, p) in enumerate(TILES):
                e.wait_ge(S("o_tok"), 2 * t + 2)
                if t < 2:
                    store(O["y_p"][0, o:o + p, :], o_tok[0:p, t, :])
                else:
                    store(O["y_s"].rearrange("b t d -> (b t) d"), o_tok[0:p, t, :])

        def tail_pool_early(e, link):
            g = nc.gpsimd
            link(g.memset(valid[:], 1.0))
            link(g.affine_select(out=valid[:, 2:3], in_=valid[:, 2:3], pattern=[[0, 1]], base=SMP - 1, channel_multiplier=-1,
                                 compare_op=ALU.is_ge, fill=0.0))

        def tail_pool(e, link):
            g = nc.gpsimd
            e.wait_ge(S("y_out"), 6)
            e.wait_ge(S("x2"), KT)
            link(g.iota(iota, pattern=[[1, SLOTS]], base=0, channel_multiplier=0, allow_small_or_imprecise_dtypes=True))
            link(g.memset(LG, 0.0))
            link(g.memset(XsT[:, :, PAIRS:SLOTS], 0.0))
            e.nop().then_inc(S("iota"), 1)
            e.wait_ge(S("tab"), 1)
            e.wait_ge(S("pt_mm"), ST)
            e.nop().then_inc(S("ys_w"), 2)
            with e.Fori(0, E // ESLOT) as i:
                for s in range(ESLOT):
                    first, end, slot = expert_range(e, i, s)
                    with e.Fori(first, end) as c:
                        off = window(e, c, first, slot)
                        e.wait_ge(S("y_col"), c + 3)
                        g.tensor_copy(out=YsT[:, :, bass.ds(off, CW)].rearrange("p (h m) n -> p m h n", h=2),
                                      in_=y_col.rearrange("p m (h n) -> p m h n", h=2)).then_inc(S("ys_w"), 1)

        def tail_pe(e):
            mm, tr = nc.tensor.matmul, nc.tensor.transpose
            e.wait_ge(S("wdn_ld"), 16)
            e.wait_ge(S("wso_ld"), 16)
            e.wait_ge(S("ht_out"), 2)
            for m in range(KT):
                b = 2 * (m % 2)
                if m >= 2:
                    e.wait_ge(S("merged"), m - 1)
                for k in range(DH):
                    mm(ps[:, b, 0:TOK], w_dn[:, k, m * P:(m + 1) * P], CO[:, k, :], start=(k == 0), stop=(k == DH - 1))
                for k in range(KT):
                    l = mm(ps[:, b + 1, 0:TOK], w_so[:, k, m * P:(m + 1) * P], CO[:, NQ + k, :], start=(k == 0), stop=(k == KT - 1))
                l.then_inc(S("ssm_mm"), 1)
            e.wait_ge(S("wo_ld"), 16)
            e.wait_ge(S("merged"), KT)
            for m in range(KT):
                if m >= 2:
                    e.wait_ge(S("x2"), m - 1)
                for k in range(KT):
                    l = mm(ps[:, 4 + m % 2, 0:TOK], w_o[:, k, m * P:(m + 1) * P], merged[:, k, :], start=(k == 0), stop=(k == KT - 1))
                l.then_inc(S("wo_mm"), 1)

            def mean_square(n):
                e.wait_ge(S("sq"), n)
                for k in range(KT):
                    l = mm(ps[:, 0, 0:TOK], ones[:, :], H2[:, k, :], start=(k == 0), stop=(k == KT - 1))
                l.then_inc(S("ms_mm"), 1)

            mean_square(2)
            e.wait_ge(S("h2"), 1)
            e.wait_ge(S("rt_ld"), 64)
            for t, (o, p) in enumerate(TILES):
                for k in range(KT):
                    l = mm(ps[0:p, 1, t * 36:(t + 1) * 36], H2[:, k, o:o + p], w_rt[:, k, :], start=(k == 0), stop=(k == KT - 1))
            l.then_inc(S("rt_mm"), 1)
            for t, (o, p) in enumerate(TILES):
                for half in range(2):
                    for k in range(4):
                        l = tr(ps[0:p, 2 + 2 * t + half if t < 2 else 6 + half, k * P:(k + 1) * P], H2[:, 4 * half + k, o:o + p], ident[:, :])
                    l.then_inc(S("h2t_mm"), 1)
            e.wait_ge(S("assign"), 1)
            for t in range(3):
                for u in range(t):
                    mm(ps[:, 0, t * E:(t + 1) * E], ones[:, :], r_eq[:, u, :], start=(u == 0), stop=False)
                mm(ps[:, 0, t * E:(t + 1) * E], tri[:, :], r_eq[:, t, :], start=(t == 0), stop=True)
            for t in range(3):
                l = mm(ps[:, 0, 3 * E:4 * E], ones[:, :], r_eq[:, t, :], start=(t == 0), stop=(t == 2))
            l.then_inc(S("count_mm"), 1)
            e.wait_ge(S("h2_tok"), 6)
            e.wait_ge(S("pm"), 1)
            for k in range(KT):
                b = 4 + 2 * (k % 2)
                if k >= 2:
                    e.wait_ge(S("xs"), k - 1)
                for c0, n in ((0, 512), (512, PAIRS - 512)):
                    for t, (o, p) in enumerate(TILES):
                        l = mm(ps[:, b + c0 // 512, 0:n], h2_tok[0:p, t, k * P:(k + 1) * P], Pm[0:p, t, c0:c0 + n],
                               start=(t == 0), stop=(t == 2))
                l.then_inc(S("xs_mm"), 1)
            e.wait_ge(S("pw"), 1)
            for s in range(ST):
                w = min(P, PAIRS - s * P)
                if s >= 2:
                    e.wait_ge(S("pt"), s - 1)
                for t, (o, p) in enumerate(TILES):
                    l = tr(ps[0:w, s % 2, o:o + p], Pw[0:p, t, s * P:s * P + w], ident[0:p, 0:p])
                l.then_inc(S("pt_mm"), 1)
            e.wait_ge(S("pt"), ST)
            e.wait_ge(S("tab"), 1)
            e.nop().then_inc(S("gu_mm"), 1)

            def result_transposed(n):
                e.wait_ge(S("y_row"), n + 1)
                e.wait_ge(S("y_col"), n + 1)
                for m in range(4):
                    l = tr(ps[:, 3, m * P:(m + 1) * P], y_row[:, m * P:(m + 1) * P], ident[:, :])
                l.then_inc(S("yrow_mm"), 1)

            with e.Fori(0, E // ESLOT) as i:
                bounds = [e.value_load(tab[0:1, 0, bass.ds(i * ESLOT, 1)], min_val=0, max_val=5 * E - 1)]
                for s in range(ESLOT):
                    wgu, wd = ex[s]
                    gate_up = wgu.rearrange("p (g k) f -> p g k f", g=2)
                    e.wait_ge(S(f"ex_ld{s}"), i * 48 + 48)
                    bounds.append(e.value_load(tab[0:1, 1, bass.ds(i * ESLOT + s, 1)], min_val=1, max_val=5 * E))
                    with e.Fori(bounds[s], bounds[s + 1]) as c:
                        e.wait_ge(S("xwin"), c + 1)
                        for k in range(KT):
                            for f in range(FT):
                                l = mm(ps[CW * f:CW * (f + 1), 0, 0:2 * P].rearrange("p (g f) -> p g f", g=2), xwin[:, k, :],
                                       gate_up[:, :, k, f * P:(f + 1) * P], start=(k == 0), stop=(k == KT - 1))
                        l.then_inc(S("gu_mm"), 1)
                        result_transposed(c)
                        e.wait_ge(S("h_row"), c + 1)
                        tr(ps[:, 1, 0:P], h_row[:], ident[:, :]).then_inc(S("h_mm"), 1)
                        e.wait_ge(S("hact"), c + 1)
                        for f in range(FT):
                            for m in range(2):
                                l = mm(ps[CW * m:CW * (m + 1), 2, :], hact[:, f, :], wd[:, f, m * 512:(m + 1) * 512],
                                       start=(f == 0), stop=(f == FT - 1))
                        l.then_inc(S("down_mm"), 1)
            chunks = e.value_load(tab[0:1, 1, E - 1:E], min_val=1, max_val=5 * E)
            result_transposed(chunks)
            e.wait_ge(S("ys_w"), chunks + 2)
            for s in range(ST):
                w = min(P, PAIRS - s * P)
                for half in range(2):
                    i = 2 * s + half
                    if i >= 4:
                        e.wait_ge(S("ys"), i - 3)
                    for k in range(4):
                        l = tr(ps[0:w, 4 + i % 4, k * P:(k + 1) * P], YsT[:, 4 * half + k, s * P:s * P + w], ident[:, :])
                    l.then_inc(S("ys_mm"), 1)
            e.wait_ge(S("ys"), 2 * ST)
            for k in range(KT):
                if k >= 2:
                    e.wait_ge(S("x3"), k - 1)
                for s in range(ST):
                    w = min(P, PAIRS - s * P)
                    l = mm(ps[:, 2 + k % 2, 0:TOK], Ys[0:w, s, k * P:(k + 1) * P], PT[0:w, s, :], start=(s == 0), stop=(s == ST - 1))
                l.then_inc(S("comb_mm"), 1)
            mean_square(3)
            e.wait_ge(S("y_fin"), 1)
            for t, (o, p) in enumerate(TILES):
                for half in range(2):
                    i = 2 * t + half
                    for k in range(4):
                        l = tr(ps[0:p, 2 + i, k * P:(k + 1) * P], y_fin[:, 4 * half + k, o:o + p], ident[:, :])
                    l.then_inc(S("ot_mm"), 1)

        def expert_range(e, i, s):
            at_ = i * ESLOT + s
            return (e.value_load(tab[0:1, 0, bass.ds(at_, 1)], min_val=0, max_val=5 * E - 1),
                    e.value_load(tab[0:1, 1, bass.ds(at_, 1)], min_val=1, max_val=5 * E),
                    e.value_load(tab[0:1, 2, bass.ds(at_, 1)], min_val=0, max_val=PAIRS))

        def window(e, c, first, slot):
            return nc.s_assert_within((c - first) * CW + slot, min_val=0, max_val=PAIRS, 
                                      skip_runtime_bounds_check_because="a chunk starts before its expert's end, at slot 576 at most")

        def tail_act(e, inverse_root):
            act = nc.scalar.activation
            e.wait_ge(S("x2"), KT)
            e.wait_ge(S("merged"), KT)
            act(H2, xT[:], ACT.Square).then_inc(S("sq"), 1)
            e.wait_ge(S("ms_mm"), 2)
            inverse_root(rstd[:], ps[:, 0, 0:TOK], D, "root")
            for t, (o, p) in enumerate(TILES):
                for half in range(2):
                    e.wait_ge(S("h2t_mm"), 2 * t + half + 1)
                    act(h2_tok[0:p, t, half * 512:(half + 1) * 512], ps[0:p, 2 + 2 * t + half if t < 2 else 6 + half, :],
                        ACT.Copy).then_inc(S("h2_tok"), 1)
            e.wait_ge(S("r_exp_arg"), 1)
            act(r_g2, r_g2, ACT.Exp)
            act(r_m[:, 6, :], r_m[:, 6, :], ACT.Exp).then_inc(S("r_exp"), 1)
            for k in range(KT):
                e.wait_ge(S("xs_mm"), k + 1)
                b = 4 + 2 * (k % 2)
                act(XsT[:, k, 0:PAIRS], ps[:, b:b + 2, :].rearrange("p a n -> p (a n)")[:, 0:PAIRS], ACT.Copy).then_inc(S("xs"), 1)
            e.wait_ge(S("tab"), 1)
            e.wait_ge(S("pt_mm"), ST)
            e.wait_ge(S("xs"), KT)
            e.wait_ge(S("iota"), 1)
            e.nop().then_inc(S("y_col"), 1)

            def result_copied(n):
                e.wait_ge(S("yrow_mm"), n + 1)
                e.wait_ge(S("ys_w"), n + 1)
                act(y_col.rearrange("p m n -> p (m n)"), ps[:, 3, :], ACT.Copy).then_inc(S("y_col"), 1)

            with e.Fori(0, E // ESLOT) as i:
                for s in range(ESLOT):
                    first, end, slot = expert_range(e, i, s)
                    with e.Fori(first, end) as c:
                        off = window(e, c, first, slot)
                        e.wait_ge(S("gu_mm"), c + 1)
                        act(xwin, XsT[:, :, bass.ds(off, CW)], ACT.Copy).then_inc(S("xwin"), 1)
                        e.wait_ge(S("gu_mm"), c + 2)
                        act(h_row[:], ps[:, 0, 0:P], ACT.Silu).then_inc(S("h_silu"), 1)
                        e.wait_ge(S("h_mm"), c + 1)
                        act(hact[:].rearrange("p f n -> p (f n)"), ps[:, 1, 0:P], ACT.Copy).then_inc(S("hact"), 1)
                        result_copied(c)
            result_copied(e.value_load(tab[0:1, 1, E - 1:E], min_val=1, max_val=5 * E))
            for s in range(ST):
                w = min(P, PAIRS - s * P)
                for half in range(2):
                    i = 2 * s + half
                    e.wait_ge(S("ys_mm"), i + 1)
                    act(Ys[0:w, s, half * 512:(half + 1) * 512], ps[0:w, 4 + i % 4, :], ACT.Copy).then_inc(S("ys"), 1)
            e.wait_ge(S("x3"), KT)
            act(H2, xT[:], ACT.Square).then_inc(S("sq"), 1)
            e.wait_ge(S("ms_mm"), 3)
            inverse_root(rstd[:], ps[:, 0, 0:TOK], D, "root")
            for t, (o, p) in enumerate(TILES):
                for half in range(2):
                    i = 2 * t + half
                    e.wait_ge(S("ot_mm"), i + 1)
                    act(o_tok[0:p, t, half * 512:(half + 1) * 512], ps[0:p, 2 + i, :], ACT.Copy).then_inc(S("o_tok"), 1)

        def tail_dve(e, link, norm_scale, modulated):
            v = nc.vector
            tt, ts, stt = v.tensor_tensor, v.tensor_scalar, v.scalar_tensor_tensor

            for m in range(KT):
                e.wait_ge(S("ssm_mm"), m + 1)
                b = 2 * (m % 2)
                if m:
                    e.wait_ge(S("merged"), m)
                tt(mtmp[:, 0, :], ZC[:, 12 + m, :], ps[:, b, 0:TOK], ALU.mult)
                link(tt(mtmp[:, 1, :], ZC[:, 20 + m, :], ps[:, b + 1, 0:TOK], ALU.mult))
                tt(merged[:, m, :], mtmp[:, 0, :], mtmp[:, 1, :], ALU.add).then_inc(S("merged"), 1)

            def gated_add(m, src, gate, sem):
                stt(xT[:, m, 0:SEQ], src[:, 0:SEQ], modT[:, gate + m, 0:1], xT[:, m, 0:SEQ], ALU.mult, ALU.add)
                s = mtmp[:, 0, 0:SMP].rearrange("p (b t) -> p b t", t=NT)
                if m:
                    e.wait_ge(S(sem), m)
                link(tt(s, src[:, SEQ:TOK].rearrange("p (b t) -> p b t", t=NT),
                        modT[:, gate + m, 1:NC].unsqueeze(2).broadcast_to([P, NB, NT]), ALU.mult))
                tt(xT[:, m, SEQ:TOK], xT[:, m, SEQ:TOK], mtmp[:, 0, 0:SMP], ALU.add).then_inc(S(sem), 1)

            for m in range(KT):
                e.wait_ge(S("wo_mm"), m + 1)
                gated_add(m, ps[:, 4 + m % 2, :], GATE1, "x2")
            e.wait_ge(S("x2"), KT)
            norm_scale(colB[:, B_FFN:B_FFN + KT], SCALE2)
            e.wait_ge(S("root"), 2)
            modulated(H2, SHIFT2)
            e.nop().then_inc(S("h2"), 1)

            e.wait_ge(S("rt_mm"), 1)
            e.wait_ge(S("iota"), 1)
            for t, (o, p) in enumerate(TILES):
                l = tt(LG[0:p, t, :], ps[0:p, 1, t * 36:(t + 1) * 36], b_rt[0:p, :], ALU.add)
            link(l)
            gl, el = LG[:, :, 0:EG], LG[:, :, EG:EG + E]

            def first_of(out, src, maximum, n):
                link(v.tensor_reduce(out=maximum, in_=src, op=ALU.max, axis=AX.X))
                link(tt(out, src, maximum.unsqueeze(2).broadcast_to([P, 3, n]), ALU.is_equal))
                for t in range(3):
                    l = stt(out[:, t, :], out[:, t, :], -float(2 * E), iota[:, 0:n], ALU.mult, ALU.add)
                link(l)
                link(v.tensor_reduce(out=r_m[:, 9, :], in_=out, op=ALU.min, axis=AX.X))
                link(tt(out, out, r_m[:, 9, :].unsqueeze(2).broadcast_to([P, 3, n]), ALU.is_equal))

            first_of(r_g, gl, r_m[:, 0, :], EG)
            link(tt(r_g2, gl, r_m[:, 0, :].unsqueeze(2).broadcast_to([P, 3, EG]), ALU.subtract))
            em4 = r_em.rearrange("p t (g x) -> p t g x", g=EG)
            link(tt(em4, el.rearrange("p t (g x) -> p t g x", g=EG), r_g.unsqueeze(3).broadcast_to([P, 3, EG, EPG]), ALU.mult))
            link(ts(r_g, r_g, -NEG, NEG, ALU.mult, ALU.add))
            link(tt(em4, em4, r_g.unsqueeze(3).broadcast_to([P, 3, EG, EPG]), ALU.add))
            first_of(r_o1, r_em, r_m[:, 1, :], E)
            link(stt(r_em, r_o1, 2 * NEG, r_em, ALU.mult, ALU.add))
            first_of(r_o2, r_em, r_m[:, 2, :], E)
            link(tt(r_m[:, 6, :], r_m[:, 2, :], r_m[:, 1, :], ALU.subtract))
            e.nop().then_inc(S("r_exp_arg"), 1)
            for oh in (r_o1, r_o2):
                link(tt(oh, oh, valid[:].unsqueeze(2).broadcast_to([P, 3, E]), ALU.mult))
            link(tt(r_eq, r_o1, r_o2, ALU.add))
            e.nop().then_inc(S("assign"), 1)
            e.wait_ge(S("r_exp"), 1)
            link(v.tensor_reduce(out=r_m[:, 3, :], in_=r_g2, op=ALU.add, axis=AX.X))
            link(stt(r_m[:, 3, :], r_m[:, 6, :], 1.0, r_m[:, 3, :], ALU.add, ALU.mult))
            link(v.reciprocal(r_m[:, 4, :], r_m[:, 3, :]))
            link(tt(r_m[:, 5, :], r_m[:, 4, :], r_m[:, 6, :], ALU.mult))
            e.wait_ge(S("count_mm"), 1)
            link(v.tensor_copy(r_n[:, 0, :], ps[:, 0, 3 * E:4 * E]))
            link(v.memset(r_c, 1.0))
            link(v.tensor_tensor_scan(out=r_n[:, 1, :], data0=r_c, data1=r_n[:, 0, :], initial=0.0, op0=ALU.mult, op1=ALU.add))
            link(tt(r_n[:, 1, :], r_n[:, 1, :], r_n[:, 0, :], ALU.subtract))
            link(v.memset(r_n[:, 2, :], 1.0))
            for q_ in range(1, 5):
                link(stt(r_n[:, 2, :], r_n[:, 0, :], float(q_ * CW), r_n[:, 2, :], ALU.is_gt, ALU.add))
            link(v.tensor_tensor_scan(out=r_n[:, 3, :], data0=r_c, data1=r_n[:, 2, :], initial=0.0, op0=ALU.mult, op1=ALU.add))
            tt(tab[:, 0, :], r_n[:, 3, :], r_n[:, 2, :], ALU.subtract)
            v.tensor_copy(tab[:, 1, :], r_n[:, 3, :])
            v.tensor_copy(tab[:, 2, :], r_n[:, 1, :]).then_inc(S("tab"), 1)
            link(tt(r_sp, ps[:, 0, 0:3 * E].rearrange("p (t x) -> p t x", t=3), r_n[:, 1:2, :].broadcast_to([P, 3, E]), ALU.add))
            for oh, at_ in ((r_o1, 7), (r_o2, 8)):
                link(tt(oh, oh, r_sp, ALU.mult))
                link(v.tensor_reduce(out=r_m[:, at_, :], in_=oh, op=ALU.add, axis=AX.X))
                link(ts(r_m[:, at_, :], r_m[:, at_, :], -1.0, None, ALU.add))
            for t in range(3):
                s1, s2 = r_m[:, 7, t:t + 1], r_m[:, 8, t:t + 1]
                link(ts(Pm[:, t, :], iota, s1, None, ALU.is_equal))
                link(stt(Pm[:, t, :], iota, s2, Pm[:, t, :], ALU.is_equal, ALU.add))
            e.nop().then_inc(S("pm"), 1)
            for t in range(3):
                s1, s2, w1, w2 = (r_m[:, x, t:t + 1] for x in (7, 8, 4, 5))
                ts(Pw[:, t, :], iota, s1, w1, ALU.is_equal, ALU.mult)
                link(ts(second, iota, s2, w2, ALU.is_equal, ALU.mult))
                link(tt(Pw[:, t, :], Pw[:, t, :], second, ALU.add))
            e.nop().then_inc(S("pw"), 1)

            for s in range(ST):
                w = min(P, PAIRS - s * P)
                e.wait_ge(S("pt_mm"), s + 1)
                v.tensor_copy(PT[0:w, s, :], ps[0:w, s % 2, 0:TOK]).then_inc(S("pt"), 1)
            v.memset(y_row, 0.0).then_inc(S("y_row"), 1)
            chunks = e.value_load(tab[0:1, 1, E - 1:E], min_val=1, max_val=5 * E)
            with e.Fori(0, chunks) as c:
                e.wait_ge(S("h_silu"), c + 1)
                tt(h_row[:], h_row[:], ps[:, 0, P:2 * P], ALU.mult).then_inc(S("h_row"), 1)
                e.wait_ge(S("down_mm"), c + 1)
                e.wait_ge(S("yrow_mm"), c + 1)
                v.tensor_copy(y_row, ps[:, 2, :]).then_inc(S("y_row"), 1)
            for k in range(KT):
                e.wait_ge(S("comb_mm"), k + 1)
                gated_add(k, ps[:, 2 + k % 2, :], GATE2, "x3")
            e.wait_ge(S("x3"), KT)
            norm_scale(colB[:, B_FIN:B_FIN + KT], SCALE_F)
            e.wait_ge(S("root"), 3)
            modulated(y_fin, SHIFT_F)
            e.nop().then_inc(S("y_fin"), 1)

        @block.sync
        def _(e):
            def load(dst, src, s):
                e.dma_start(dst, src).then_inc(S(s), 16)

            stores = [0]

            def store(dst, src):
                e.dma_start(dst, src).then_inc(S("stored"), 16)
                stores[0] += 1

            load(c_tok[0:1, :], T["c_prompt"], "c_ld")
            load(c_tok[1:NC, :], T["c_sample"], "c_ld")
            wa = T["w_ada"][0].rearrange("(k p) n -> p k n", p=P)
            wf = T["w_ada_final"].rearrange("(k p) n -> p k n", p=P)
            for sl in range(2):
                load(ada_ring[sl], wa[:, :, sl * ADA_N:(sl + 1) * ADA_N], f"ada_ld{sl}")
            r = 0
            for n, k in (("b_ada", 48), ("norm_mix_w", 8)):
                load(tabA[r:r + k, :], T[n][0].rearrange("(m p) -> m p", p=P), "tab_ld")
                r += k
            load(tabA[r:r + 48, :], T["dn_conv_w"][0].rearrange("i (m p) -> (i m) p", p=P), "tab_ld")
            load(tabB[0:48, :], T["ssm_conv_w"][0].rearrange("i (m p) -> (i m) p", p=P), "tab_ld")
            r = 48
            for n, k in (("ssm_conv_b", 12), ("ssm_norm_w", 8), ("norm_ffn_w", 8),
                         ("b_ada_final", 16), ("final_norm_w", 8), ("dn_norm_w", 1)):
                a = T[n] if n in ("b_ada_final", "final_norm_w") else T[n][0]
                load(tabB[r:r + k, :], a.rearrange("(m p) -> m p", p=P), "tab_ld")
                r += k
            for t in range(2):
                load(x_tok[:, t, :], T["x_prompt"][0, t * P:(t + 1) * P, :], "x_ld")
            load(x_tok[0:SMP, 2, :], T["x_sample"].rearrange("b t d -> (b t) d"), "x_ld")
            for sl in range(2):
                e.wait_ge(S("ada_mm"), sl + 1)
                load(ada_ring[sl], wa[:, :, (2 + sl) * ADA_N:(3 + sl) * ADA_N], f"ada_ld{sl}")
            load(wsm[:, :, 0:4], wi[:, :, C_A:C_A + 4], "small_ld")
            load(wsm[:, :, 4:20], wi[:, :, C_DT:C_DT + 16], "small_ld")
            load(wsm[:, :, 20:24], wi[:, :, C_B:C_B + 4], "small_ld")
            load(bias_row[:, 0:4], T["dn_dt_bias"].broadcast_to([P, 4]), "small_ld")
            load(bias_row[:, 4:20], T["ssm_dt_bias"].broadcast_to([P, 16]), "small_ld")
            load(alog_row[:, 0:4], T["dn_A_log"].broadcast_to([P, 4]), "small_ld")
            load(alog_row[:, 4:20], T["ssm_A_log"].broadcast_to([P, 16]), "small_ld")
            load(dcol[:, NB:NC], T["ssm_D"].rearrange("o h -> h o"), "small_ld")
            load(dn_halo, T["state_dn_conv"][0].rearrange("b t c -> (b t) c"), "halo_ld")
            load(ssm_halo, T["state_ssm_conv"][0].rearrange("b t c -> (b t) c"), "halo_ld")
            load(w_rt[:, :, 0:EG], T["w_group_router"][0].rearrange("(k p) n -> p k n", p=P), "rt_ld")
            load(w_rt[:, :, EG:], T["w_expert_router"][0].rearrange("(k p) n -> p k n", p=P), "rt_ld")
            load(b_rt[:, 0:EG], T["b_group_router"].broadcast_to([P, EG]), "rt_ld")
            load(b_rt[:, EG:], T["b_expert_router"].broadcast_to([P, E]), "rt_ld")
            done = 0
            for n, first in RUNS:
                wada, ada_first = (wf, -9 * ADA_N) if done == 9 else (wa, 3 * ADA_N)
                if done == 0:
                    for sl in range(2):
                        load(w_ring[sl], wi[:, :, first + sl * WN:first + (sl + 1) * WN], f"win_ld{sl}")
                with e.Fori(1 if done == 0 else 0, n) as i:
                    e.wait_ge(S("ada_mm"), i + (done + 3))
                    e.wait_ge(S("proj_mm"), i * 4 + (4 * done - 2))
                    load(w_ring[0], wi[:, :, bass.ds(i * (2 * WN) + first, WN)], "win_ld0")
                    load(ada_ring[0], wada[:, :, bass.ds(i * ADA_N + (done * ADA_N + ada_first), ADA_N)], "ada_ld0")
                    e.wait_ge(S("proj_mm"), i * 4 + 4 * done)
                    load(w_ring[1], wi[:, :, bass.ds(i * (2 * WN) + (first + WN), WN)], "win_ld1")
                done += n
            e.wait_ge(S("ada_mm"), 16)
            for h in range(DH):
                load(Sin[:, h], T["state_dn_rec"][0, :, h].rearrange("b k v -> k b v"), "sin_ld")
            hs_in = T["state_ssm_rec"][0].rearrange("b h p n -> (h p) b n")
            hs_out = O["ssm_rec_s"][0].rearrange("b h p n -> (h p) b n")
            e.wait_ge(S("cstate"), NU // 4)
            for name, c0 in (("dn_conv", 0), ("ssm_conv", NQ)):
                store(O[name + "_p"][0, 0], cst[0:3, c0:c0 + NQ, :].rearrange("p a b -> p (a b)"))
                store(O[name + "_s"][0].rearrange("b t c -> (b t) c"),
                      cst[3:27, c0:c0 + NQ, :].rearrange("p a b -> p (a b)"))
            e.wait_ge(S("stored"), 64)
            for j in range(4):
                load(Hs[:, j], hs_in[j * P:(j + 1) * P], "hs_ld0")
            for h in range(DH):
                e.wait_ge(S("sin_new"), h + 1)
                store(O["dn_rec_s"][0, :, h].rearrange("b k v -> k b v"), Sin[:, h])
            for g in range(2):
                for j in range(4):
                    e.wait_ge(S("hs_new"), 4 * g + j + 1)
                    e.dma_start(hs_out[(4 * g + j) * P:(4 * g + j + 1) * P], Hs[:, j]).then_inc(S("hs_stored"), 16)
                e.wait_ge(S("hs_stored"), 64 * (g + 1))
                if g == 0:
                    for j in range(4):
                        load(Hs[:, j], hs_in[(4 + j) * P:(5 + j) * P], "hs_ld1")
            e.wait_ge(S("stored"), 16 * stores[0])
            load(w_dn, T["w_dn_out"][0].rearrange("(k p) n -> p k n", p=P), "wdn_ld")
            load(w_so, T["w_ssm_out"][0].rearrange("(k p) n -> p k n", p=P), "wso_ld")
            e.wait_ge(S("sd_new"), 2)
            store(O["dn_rec_p"][0, 0].rearrange("h k v -> k h v"), Sd)
            e.wait_ge(S("ht_out"), 2)
            store(O["ssm_rec_p"][0, 0].rearrange("(j a) p n -> (a p) j n", a=2), hT_out)
            tail_loads(e, load, store)
            e.wait_ge(S("stored"), 16 * stores[0])

        @block.gpsimd
        def _(e):
            n = [0]

            def link(ins):
                n[0] += 1
                ins.then_inc(S("pool_chain"), 1)
                e.wait_ge(S("pool_chain"), n[0])

            g = nc.gpsimd
            tail_pool_early(e, link)

            def select(ap, pattern, base, mult, op=ALU.is_ge, fill=0.0):
                link(g.affine_select(out=ap, in_=ap, pattern=pattern, base=base, channel_multiplier=mult,
                                     compare_op=op, fill=fill))

            link(g.memset(ident[:], 0.0))
            select(ident[:], [[-1, P]], 0, 1, ALU.not_equal, 1.0)
            link(g.memset(ones[:], 1.0))
            link(g.memset(eps_c[:], EPS))
            link(g.memset(U[:, :, 0:HALO], 0.0))
            link(g.memset(gsm[:], 0.0))
            g.memset(dcol[:, 0:NB], 0.0).then_inc(S("consts0"), 1)
            link(g.memset(tri[:], 1.0))
            select(tri[:], [[1, P]], 0, -1)
            link(g.memset(neg[:], 0.0))
            select(neg[:], [[1, P]], 0, -1, fill=NEG)
            for m, start, fill in ((tri_s, 1.0, 0.0), (neg_s, 0.0, NEG)):
                link(g.memset(m[:], start))
                select(m[:], [[1, SMP]], 0, -1, fill=fill)
                select(m[:].rearrange("p (b t) -> p b t", t=NT), [[-NT, NB], [0, NT]], 0, 1, fill=fill)
            link(g.memset(same_s[:], 1.0))
            select(same_s[:].rearrange("p (b t) -> p b t", t=NT), [[-NT, NB], [0, NT]], 0, 1)
            select(same_s[:].rearrange("p (b t) -> p b t", t=NT), [[NT, NB], [0, NT]], NT - 1, -1)
            link(g.memset(seq_of[:], 1.0))
            select(seq_of[:], [[-NT, NB]], 0, 1)
            select(seq_of[:], [[NT, NB]], NT - 1, -1)
            link(g.memset(level[:], 0.0))
            for l in range(7):
                s = 1 << l
                odd = level[:, l, :].rearrange("p (n c s) -> p n c s", c=2, s=s)[:, :, 1, :]
                link(g.memset(odd, 1.0))
                select(odd, [[-2 * s, P // (2 * s)], [0, s]], 0, 1)
                select(odd, [[2 * s, P // (2 * s)], [0, s]], s - 1, -1)
            link(g.tensor_copy(out=level[HF:P, 0:6, 0:HF], in_=level[HF:P, 0:6, HF:P]))
            link(g.memset(head_rows[:], 0.0))
            hv = head_rows[:].rearrange("p j (a c) -> p j a c", a=2)
            g.affine_select(out=hv, in_=hv, pattern=[[-2, KT], [-1, 2], [0, HD]], base=0, channel_multiplier=1,
                            compare_op=ALU.not_equal, fill=1.0).then_inc(S("consts"), 1)
            e.wait_ge(S("proj_read"), 28)
            link(g.tensor_copy(out=c_new[:, :, 0:HALO], in_=U[:, :, SROW - HALO:SROW]))
            for b in range(NB):
                c0 = SROW + b * STEP + NT
                link(g.tensor_copy(out=c_new[:, :, HALO * (b + 1):HALO * (b + 2)], in_=U[:, :, c0:c0 + HALO]))
            e.nop().then_inc(S("c_new"), 1)
            e.wait_ge(S("qk_normed"), 1)
            e.wait_ge(S("co"), NU)
            e.wait_ge(S("proj_mm"), 52)
            link(g.memset(Km, 0.0))
            for b in range(NB):
                c0 = SEQ + b * NT
                link(g.tensor_copy(out=Km[:, b, :, b * NT:(b + 1) * NT], in_=CO[:, DH:2 * DH, c0:c0 + NT]))
            e.nop().then_inc(S("km"), 1)
            e.wait_ge(S("vnew"), 1)
            for h in range(DH):
                if h >= 2:
                    e.wait_ge(S("sin_mm"), h - 1)
                link(g.tensor_tensor(out=Vm[h % 2], in0=vnew[0:SMP, h:h + 1, :].broadcast_to([SMP, NB, P]),
                                     in1=seq_of[:].unsqueeze(2).broadcast_to([SMP, NB, P]), op=ALU.mult))
                e.nop().then_inc(S("vm"), 1)
            e.wait_ge(S("o_mm"), 1)
            for h in range(DH):
                link(g.tensor_tensor(out=Sin[:, h], in0=Sin[:, h],
                                     in1=EL2[:, h, :].unsqueeze(2).broadcast_to([P, NB, P]), op=ALU.mult))
                e.nop().then_inc(S("sin_decayed"), 1)
            for h in range(2):
                e.wait_ge(S("bt"), h + 1)
                e.wait_ge(S("sin_mm"), DH)
                link(g.tensor_tensor(out=Bm, in0=Bt[0:SMP, :].unsqueeze(1).broadcast_to([SMP, NB, P]),
                                     in1=seq_of[:].unsqueeze(2).broadcast_to([SMP, NB, P]), op=ALU.mult))
                e.nop().then_inc(S("bm"), 1)
                e.wait_ge(S("hst_mm"), 8 * (h + 1))
                for j in range(4):
                    link(g.tensor_tensor(out=Hs[:, j], in0=Hs[:, j],
                                         in1=drep[:, 4 * h + j, 0:NB].unsqueeze(2).broadcast_to([P, NB, P]), op=ALU.mult))
                    e.nop().then_inc(S("hs_decayed"), 1)
            tail_pool(e, link)

        @block.tensor
        def _(e):
            mm, tr = nc.tensor.matmul, nc.tensor.transpose
            e.wait_ge(S("consts0"), 1)
            e.wait_ge(S("c_silu"), 1)
            for k in range(KT):
                l = tr(ps[:, 1, k * NC:(k + 1) * NC], c_tok[:, k * P:(k + 1) * P], ident[0:NC, 0:NC])
            l.then_inc(S("cT_mm"), 1)
            e.wait_ge(S("tab_ld"), 16 * 10)
            tr(ps[:, 0, 0:A_ROWS], tabA, ident[0:A_ROWS, 0:A_ROWS])
            tr(ps[:, 0, 128:128 + B_ROWS], tabB, ident[0:B_ROWS, 0:B_ROWS]).then_inc(S("tab_mm"), 1)

            def ada_products(slot, bank):
                for k in range(KT):
                    for q in range(4):
                        l = mm(ps[CPAD * q:CPAD * (q + 1), bank, 0:P], cT[:, k, :], ada_ring[slot][:, k, q * P:(q + 1) * P],
                               start=(k == 0), stop=(k == KT - 1))
                l.then_inc(S("ada_mm"), 1)

            def ada_transposed(slot, bank):
                tr(ps[:, bank, P:2 * P], mod_rows[:, slot, :], ident[:, :]).then_inc(S("mod_mm"), 1)

            e.wait_ge(S("cT"), 1)
            for i in range(2):
                for sl in range(2):
                    e.wait_ge(S(f"ada_ld{sl}"), i * 16 + 16)
                    if i:
                        e.wait_ge(S("mod_read"), sl + 1)
                    ada_products(sl, 6 + sl)
                    e.wait_ge(S("mod_row"), 2 * i + sl + 1)
                    ada_transposed(sl, 6 + sl)
                if i == 0:
                    e.wait_ge(S("x_ld"), 48)
                    for k in range(KT):
                        if k >= 4:
                            e.wait_ge(S("xT"), k - 3)
                        for t, (o, p) in enumerate(TILES):
                            l = tr(ps[:, k % 4 + 2, o:o + p], x_tok[0:p, t, k * P:(k + 1) * P], ident[0:p, 0:p])
                        l.then_inc(S("x_mm"), 1)
            e.wait_ge(S("sq"), 1)
            e.wait_ge(S("col"), 1)
            for k in range(KT):
                l = mm(ps[:, 0, 0:TOK], ones[:, :], sq[:, k, :], start=(k == 0), stop=(k == KT - 1))
            l.then_inc(S("ms_mm"), 1)
            e.wait_ge(S("halo_ld"), 32)
            e.wait_ge(S("xT"), 8)
            for i, halo in enumerate((dn_halo, ssm_halo)):
                for m in range(NQ):
                    l = tr(ps[:, 2 + i, m * 24:(m + 1) * 24], halo[:, m * P:(m + 1) * P], ident[0:24, 0:24])
                l.then_inc(S("halo_mm"), 1)
            e.wait_ge(S("hn"), 1)
            e.wait_ge(S("small_ld"), 16 * 8)
            for t, (o, p) in enumerate(TILES):
                for k in range(KT):
                    l = mm(ps[0:p, 1, t * 24:(t + 1) * 24], HN[:, k, o:o + p], wsm[:, k, :], start=(k == 0), stop=(k == KT - 1))
            l.then_inc(S("gsm_mm"), 1)
            e.wait_ge(S("halo_read"), 2)
            e.wait_ge(S("mod_read"), 4)

            def project(i, first):
                for sl in range(2):
                    e.wait_ge(S(f"win_ld{sl}"), i * 16 + 16)
                    if not first:
                        e.wait_ge(S("proj_read"), i * 4 + (2 * sl - 2))
                    for m in range(2):
                        for k in range(KT):
                            l = mm(ps[:, 2 + 2 * sl + m, 0:TOK], w_ring[sl][:, k, m * P:(m + 1) * P], HN[:, k, :],
                                   start=(k == 0), stop=(k == KT - 1))
                        l.then_inc(S("proj_mm"), 1)
                    if sl == 1 and not first:
                        e.wait_ge(S("mod_row"), i + 4)
                        ada_transposed(0, 6)
                    if sl == 0 and not first:
                        e.wait_ge(S("ada_ld0"), i * 16 + 32)
                        e.wait_ge(S("mod_read"), i + 3)
                        ada_products(0, 6)

            project(0, True)
            with e.Fori(1, 9) as i:
                project(i, False)
            e.wait_ge(S("qk_sq"), 1)
            for m in range(2 * DH):
                if m >= 2:
                    e.wait_ge(S("qk_ln"), m - 1)
                mm(ps[:, m % 2, 0:TOK], ones[:, :], sq[:, m, :], start=True, stop=True).then_inc(S("qk_mm"), 1)
            e.wait_ge(S("consts"), 1)
            e.wait_ge(S("gates"), 1)
            e.wait_ge(S("gm"), 1)
            e.wait_ge(S("qk_ln"), 2 * DH)
            for t, (o, p) in enumerate(TILES):
                mm(ps[0:p, 0, t * NG:(t + 1) * NG], (tri if p == P else tri_s)[0:p, 0:p], G[0:p, t, :], start=True, stop=True)
                mm(ps[0:p, 0, 64 + t * NG:64 + (t + 1) * NG], (ones if p == P else same_s)[0:p, 0:p], G[0:p, t, :],
                   start=True, stop=True)
            mm(ps[:, 1, 0:NG * NB], ones[0:SMP, :], GM[:].rearrange("p a b -> p (a b)"), start=True, stop=True)
            mm(ps[0:SH, 7, 0:NB], G[0:SMP, 2, DH:NG], seq_of[:], start=True, stop=True).then_inc(S("sums_mm"), 1)
            e.wait_ge(S("dcol"), 1)
            for j in range(KT):
                l = mm(ps[:, 7, 16 + j * NC:16 + (j + 1) * NC], head_rows[:, j, :], dcol[:], start=True, stop=True)
            l.then_inc(S("drep_mm"), 1)
            with e.Fori(9, 11) as i:
                project(i, False)
            e.wait_ge(S("c_new"), 1)
            e.wait_ge(S("sums"), 1)
            e.wait_ge(S("drep"), 1)
            for i in range(NU // 4):
                if i >= 2:
                    e.wait_ge(S("cstate"), i - 1)
                for m in range(4):
                    l = tr(ps[0:27, i % 2, m * P:(m + 1) * P], c_new[:, 4 * i + m, :], ident[:, :])
                l.then_inc(S("cstate_mm"), 1)
            with e.Fori(11, 13) as i:
                project(i, False)
            e.wait_ge(S("proj_read"), 52)
            e.wait_ge(S("cstate"), NU // 4)
            e.wait_ge(S("mod_read"), 16)

            e.wait_ge(S("sums"), 1)
            e.wait_ge(S("qk_normed"), 1)

            lv, mk = [0], [0]
            for n, t in enumerate(ORDER):
                o, p = TILES[t]
                U_ = (tri if p == P else tri_s)
                if n:
                    e.wait_ge(S("y_out"), 2 * n)
                for h in range(DH):
                    mm(heads(0, DH, p)[:, h], G[0:p, t, h:h + 1].broadcast_to([p, P]), U_[0:p, 0:p], start=True, stop=True)
                for h in range(DH):
                    mm(heads(1, DH, p)[:, h], beta[0:p, t, h:h + 1].broadcast_to([p, P]), ident[0:p, 0:p], start=True, stop=True)
                for h in range(DH):
                    k_, q_ = CO[:, DH + h, o:o + p], CO[:, h, o:o + p]
                    mm(heads(2, DH, p, p)[:, h], k_, k_, start=True, stop=True)
                    mm(heads(3, DH, p, p)[:, h], k_, q_, start=True, stop=True)
                for h in range(DH):
                    tr(heads(4, DH, P, p)[:, h], CO[:, DH + h, o:o + p], ident[:, :])
                    l = tr(heads(5, DH, P, p)[:, h], CO[:, 2 * DH + h, o:o + p], ident[:, :])
                l.then_inc(S("dn_mm"), 1)
                if t == 2:
                    e.wait_ge(S("km"), 1)
                    e.wait_ge(S("sin_ld"), 64)
                    for h in range(DH):
                        for b in range(NB):
                            l = mm(heads(6, DH, P, p)[:, h], Km[:, b, h, :], Sin[:, h, b, :], start=(b == 0), stop=(b == NB - 1))
                    l.then_inc(S("ks_mm"), 1)
                if t == 1:
                    e.wait_ge(S("sd_new"), 1)
                    for h in range(DH):
                        l = mm(heads(6, DH, P, p)[:, h], CO[:, DH + h, o:o + p], Sd[:, h, :], start=True, stop=True)
                    l.then_inc(S("ks_mm"), 1)
                e.wait_ge(S("y0"), n + 1)
                if t == 2:
                    for h in range(DH):
                        l = tr(heads(0, DH, p, p)[:, h], Y[0:p, h, 0:p], ident[0:p, 0:p])
                    l.then_inc(S("yt_mm"), 1)
                    e.wait_ge(S("mk"), 1)
                    mk[0] += 1
                    e.wait_ge(S("yt"), 1)
                    for h in range(DH):
                        l = mm(heads(1, DH, p, p)[:, h], Mk[0:p, h, 0:p], Yt[0:p, h, 0:p], start=True, stop=True)
                    l.then_inc(S("w_mm"), 1)
                    e.wait_ge(S("w"), 1)
                    for h in range(DH):
                        l = mm(heads(2, DH, p, p)[:, h], Wt[0:p, h, 0:p], Y[0:p, h, 0:p], start=True, stop=True)
                    l.then_inc(S("wy_mm"), 1)
                    e.wait_ge(S("y_up"), 1)
                    lv[0] += 1
                else:
                    blocks = [(h, slice(HF * b, HF * (b + 1))) for h in range(DH) for b in range(2)]

                    def half(bank, h, rows):
                        return ps[rows, bank, h * HF:(h + 1) * HF]

                    for h, r in blocks:
                        l = mm(half(0, h, r), Y_c[r, h, :], ident[r, r], start=True, stop=True)
                    l.then_inc(S("yt_mm"), 1)
                    for l_ in range(1, 6):
                        e.wait_ge(S("mk"), mk[0] + 1)
                        mk[0] += 1
                        if l_ == 1:
                            e.wait_ge(S("yt"), n + 1)
                        for h, r in blocks:
                            l = mm(half(1, h, r), Mk_c[r, h, :], Yt_c[r, h, :], start=True, stop=True)
                        l.then_inc(S("w_mm"), 1)
                        e.wait_ge(S("w"), lv[0] + 1)
                        for h, r in blocks:
                            mm(half(2, h, r), Wt[r, h, 0:HF], Y_c[r, h, :], start=True, stop=True)
                            l = mm(half(3, h, r), Y_c[r, h, :], Wt[r, h, 0:HF], start=True, stop=True)
                        l.then_inc(S("wy_mm"), 1)
                        e.wait_ge(S("y_up"), lv[0] + 1)
                        lv[0] += 1
                    lo, hi = slice(0, HF), slice(HF, P)
                    for h in range(DH):
                        l = mm(half(1, h, hi), Lt[lo, h, HF:P], Yt_c[lo, h, :], start=True, stop=True)
                    l.then_inc(S("w_mm"), 1)
                    e.wait_ge(S("w"), lv[0] + 1)
                    for h in range(DH):
                        l = mm(half(2, h, lo), Wt[hi, h, 0:HF], Y_c[hi, h, :], start=True, stop=True)
                    l.then_inc(S("wy_mm"), 1)
                    e.wait_ge(S("y_up"), lv[0] + 1)
                    lv[0] += 1
                e.wait_ge(S("r"), n + 1)
                for h in range(DH):
                    l = mm(heads(0, DH, P, p)[:, h], Y[0:p, h, 0:p], R[0:p, h, :], start=True, stop=True)
                l.then_inc(S("vnew_mm"), 1)
                e.wait_ge(S("vnew"), n + 1)
                for h in range(DH):
                    out = heads(4, DH, p)[:, h]
                    l = mm(out, vnew[0:p, h, :], Qd[0:p, h, 0:p], start=True, stop=(t == 0), skip_group_check=(t == 2))
                    if t == 1:
                        l = mm(out, Sd[:, h, :], qe[:, h, :], start=False, stop=True)
                    if t == 2:
                        for b in range(NB):
                            l = mm(out[:, b * NT:(b + 1) * NT], Sin[:, h, b, :], qe[:, h, b * NT:(b + 1) * NT],
                                   start=False, stop=(b == NB - 1), skip_group_check=True)
                l.then_inc(S("o_mm"), 1)
                if t != 2:
                    for h in range(DH):
                        l = mm(heads(5, DH, P)[:, h], kd[0:p, h, :], vnew[0:p, h, :], start=True, stop=True)
                    l.then_inc(S("ds_mm"), 1)
                else:
                    for h in range(DH):
                        e.wait_ge(S("vm"), h + 1)
                        if h >= 2:
                            e.wait_ge(S("sin_new"), h - 1)
                        for c in range(2):
                            l = mm(ps[:, 2 * (h % 2) + c, :], kd[0:p, h, :],
                                   Vm[h % 2][:, 4 * c:4 * c + 4, :].rearrange("p b v -> p (b v)"), start=True, stop=True)
                        l.then_inc(S("sin_mm"), 1)
                e.wait_ge(S("o_sq"), n + 1)
                mm(heads(6, DH, p), ones[:, :], sqm[:, :, 0:p], start=True, stop=True).then_inc(S("o_ms"), 1)

                for g in range(2):
                    i = 2 * n + g
                    e.wait_ge(S("o_out"), n + 1)
                    if g:
                        e.wait_ge(S("y_out"), i)
                        if t == 2:
                            e.wait_ge(S("hs_new"), 4)
                    elif t == 2:
                        e.wait_ge(S("sin_new"), DH)
                    B_, C_ = CO[:, 20 + g, o:o + p], CO[:, 22 + g, o:o + p]
                    mm(ps[0:p, 0, 0:p], B_, C_, start=True, stop=True)
                    for h in range(8):
                        mm(heads(1, 8, p)[:, h], G[0:p, t, DH + 8 * g + h:DH + 8 * g + h + 1].broadcast_to([p, P]), U_[0:p, 0:p],
                           start=True, stop=True)
                    tr(ps[0:p, 3, 0:P], B_, ident[:, :])
                    for j in range(4):
                        l = tr(heads(4, 4, P, p)[:, j], CO[:, NQ + 4 * g + j, o:o + p], ident[:, :])
                    l.then_inc(S("s_mm"), 1)
                    if t == 2:
                        e.wait_ge(S(f"hs_ld{g}"), 64)
                        for b in range(NB):
                            if b >= 2:
                                e.wait_ge(S("hst"), 8 * g + b - 1)
                            for j in range(4):
                                l = tr(ps[:, 5 + b % 2, j * P:(j + 1) * P], Hs[:, j, b, :], ident[:, :])
                            l.then_inc(S("hst_mm"), 1)
                    e.wait_ge(S("s_ready"), i + 1)
                    if t == 2:
                        e.wait_ge(S("hst"), 8 * (g + 1))
                    for j in range(4):
                        for a in range(2):
                            h = 2 * j + a
                            out = heads(5, 4, p)[HD * a:HD * (a + 1), j]
                            l = mm(out, xdt[0:p, h, :], CBd[0:p, h, 0:p], start=True, stop=(t != 1))
                            if t == 1:
                                l = mm(out, hT[:, 8 * g + h, :], CE[:, h, :], start=False, stop=True)
                    if t == 2:
                        for j in range(4):
                            for b in range(NB):
                                l = mm(ps[:, 6, (j * NB + b) * 8:(j * NB + b + 1) * 8].rearrange("p (a t) -> p a t", a=2),
                                       HsT[:, b, j * P:(j + 1) * P], CE[:, 2 * j:2 * j + 2, b * NT:(b + 1) * NT],
                                       start=True, stop=True)
                    l.then_inc(S("y_mm"), 1)
                    if t != 2:
                        mm(ps[:, 7, :], Bt[0:p, :], xw[0:p, :, :].rearrange("p a b -> p (a b)"), start=True, stop=True).then_inc(S("dh_mm"), 1)
                    else:
                        e.wait_ge(S("bm"), g + 1)
                        for j in range(4):
                            if j >= 2:
                                e.wait_ge(S("hs_new"), 4 * g + j - 1)
                            for c in range(2):
                                l = mm(ps[:, 1 + 2 * (j % 2) + c, :], xw[0:p, 2 * j:2 * j + 2, :].rearrange("p a b -> p (a b)"),
                                       Bm[:, 4 * c:4 * c + 4, :].rearrange("p b v -> p (b v)"), start=True, stop=True)
                            l.then_inc(S("hs_mm"), 1)
                    e.wait_ge(S("y_sq"), i + 1)
                    for j in range(4):
                        l = mm(ps[:, 0, 0:p], ones[:, :], sqm[:, j, 0:p], start=(j == 0), stop=(j == 3))
                    l.then_inc(S("y_ms"), 1)
            e.wait_ge(S("ht"), 4)
            e.wait_ge(S("y_out"), 6)
            for j in range(KT):
                l = tr(ps[:, 2 + j // 4, (j % 4) * P:(j % 4 + 1) * P], hT[:, 2 * j:2 * j + 2, :].rearrange("p a b -> p (a b)"), ident[:, :])
                if j % 4 == 3:
                    l.then_inc(S("ht_mm"), 1)
            tail_pe(e)

        @block.scalar
        def _(e):
            act = nc.scalar.activation
            n_ = [0]

            def link(ins):
                n_[0] += 1
                ins.then_inc(S("act_chain"), 1)
                e.wait_ge(S("act_chain"), n_[0])

            e.wait_ge(S("c_ld"), 32)
            act(c_tok, c_tok, ACT.Silu).then_inc(S("c_silu"), 1)
            for k in range(KT):
                e.wait_ge(S("x_mm"), k + 1)
                act(xT[:, k, :], ps[:, k % 4 + 2, 0:TOK], ACT.Copy).then_inc(S("xT"), 1)
            e.wait_ge(S("xT"), KT)
            e.wait_ge(S("x_mm"), KT)
            act(sq, xT[:], ACT.Square).then_inc(S("sq"), 1)

            def inverse_root(out, src, n, sem):
                link(act(out, src, ACT.Ln, bias=eps_c[:], scale=1.0 / n))
                act(out, out, ACT.Exp, scale=-0.5).then_inc(S(sem), 1)

            e.wait_ge(S("ms_mm"), 1)
            inverse_root(rstd[:], ps[:, 0, 0:TOK], D, "root")
            e.wait_ge(S("gsm1"), 1)
            act(t1[:], t1[:], ACT.Exp, scale=-1.0).then_inc(S("gsm_e"), 1)
            act(nbeta[:], gsm[:, :, NG:24], ACT.Exp, scale=-1.0)
            link(act(alog_row[:], alog_row[:], ACT.Exp))
            e.wait_ge(S("gsm2"), 1)
            act(t2[:], t2[:], ACT.Ln).then_inc(S("gsm_ln"), 1)

            def evac(i, kind, blk=True):
                for m in range(4):
                    if m == 2 and blk:
                        e.wait_ge(S("ada_mm"), i + 4)
                        act(mod_rows[:, 0, :], ps[:, 6, 0:P], ACT.Copy).then_inc(S("mod_row"), 1)
                    e.wait_ge(S("proj_mm"), i * 4 + (m + 1))
                    src = ps[:, 2 + m, 0:TOK]
                    if kind[0] == "u":
                        tile = i * 4 + (m + kind[1])
                        dst = U[:, bass.ds(tile, 1), :].rearrange("p a n -> p (a n)")
                        act(dst[:, HALO:SROW], src[:, 0:SEQ], ACT.Copy)
                        act(dst[:, SROW:ROW].rearrange("p (b t) -> p b t", t=STEP)[:, :, HALO:STEP],
                            src[:, SEQ:TOK].rearrange("p (b t) -> p b t", t=NT), ACT.Copy).then_inc(S("proj_read"), 1)
                    else:
                        dst = ZC[:, bass.ds(i * 4 + (m + kind[1]), 1), :].rearrange("p a n -> p (a n)")
                        act(dst, src, kind[0]).then_inc(S("proj_read"), 1)

            def mod_evac(i):
                e.wait_ge(S("mod_mm"), i + 4)
                act(modT[:, bass.ds(i * 4 + 12, 4), :], ps[:, 6, P:2 * P].rearrange("p (m c) -> p m c", c=CPAD)[:, :, 0:NC],
                    ACT.Copy).then_inc(S("mod_read"), 1)

            def conv_silu(first, bias):
                for m in range(NQ):
                    e.wait_ge(S("cv"), first + m + 1)
                    b = {"bias": colB[:, B_CONVB + m:B_CONVB + m + 1]} if bias else {}
                    act(CO[:, first + m, 0:SEQ], cv[:, m, 0:SEQ], ACT.Silu, **b)
                    act(CO[:, first + m, SEQ:TOK].rearrange("p (b t) -> p b t", t=NT),
                        cv_sample(m), ACT.Silu, **b).then_inc(S("co"), 1)

            def cv_sample(m):
                return arena[:, cv_at + m * CROW + SROW:cv_at + m * CROW + SROW + NB * STEP].rearrange(
                    "p (b t) -> p b t", t=STEP)[:, :, 0:NT]

            e.wait_ge(S("halo_read"), 2)
            evac(0, ("u", 0), False)
            with e.Fori(1, 3) as i:
                evac(i, ("u", 0))
                mod_evac(i)
            with e.Fori(3, 4) as i:
                evac(i, (ACT.Silu, -12))
                mod_evac(i)
            conv_silu(0, False)
            with e.Fori(4, 7) as i:
                evac(i, ("u", -4))
                mod_evac(i)
            e.wait_ge(S("co"), NQ)
            act(sq, CO[:, 0:2 * DH, :], ACT.Square).then_inc(S("qk_sq"), 1)
            with e.Fori(7, 9) as i:
                evac(i, (ACT.Silu, -24))
                mod_evac(i)
            for m in range(2 * DH):
                e.wait_ge(S("qk_mm"), m + 1)
                act(sq[:, m, :], ps[:, m % 2, 0:TOK], ACT.Ln, bias=eps_c[:]).then_inc(S("qk_ln"), 1)
            e.wait_ge(S("qk_ln"), 2 * DH)
            act(sq, sq, ACT.Exp, scale=-0.5).then_inc(S("qk_root"), 1)
            e.wait_ge(S("sums_mm"), 1)
            act(dcol[:, 0:NB], ps[0:SH, 7, 0:NB], ACT.Exp).then_inc(S("dcol"), 1)
            e.wait_ge(S("dte_arg"), 1)
            act(dte[:], dte[:], ACT.Exp)
            act(ecs[:], csum[:], ACT.Exp)
            act(elast[:].rearrange("p a b -> p (a b)"), ps[:, 0, 64:64 + 2 * NG], ACT.Exp)
            act(EL2[:].rearrange("p a b -> p (a b)"), ps[:, 1, 0:NG * NB], ACT.Exp).then_inc(S("sums"), 1)
            conv_silu(NQ, True)
            with e.Fori(9, 11) as i:
                evac(i, (ACT.Sigmoid, -24))
                mod_evac(i)
            for i in range(NU // 4):
                e.wait_ge(S("cstate_mm"), i + 1)
                act(cst[:, 4 * i:4 * i + 4, :].rearrange("p a b -> p (a b)"), ps[0:27, i % 2, :], ACT.Copy).then_inc(S("cstate"), 1)
            with e.Fori(11, 13) as i:
                evac(i, (ACT.Sigmoid, -24))
                mod_evac(i)

            lv = 0
            for n, t in enumerate(ORDER):
                o, p = TILES[t]
                e.wait_ge(S("dn_mm"), n + 1)
                if n:
                    e.wait_ge(S("y_out"), 2 * n)
                act(EB[:, 0:DH, 0:p], heads(0, DH, p), ACT.Exp).then_inc(S("dn_eb"), 1)
                e.wait_ge(S("dn_arg"), n + 1)
                act(D2[0:p, 0:DH, 0:p], D2[0:p, 0:DH, 0:p], ACT.Exp).then_inc(S("dn_exp"), 1)
                e.wait_ge(S("yt_mm"), n + 1)
                if t == 2:
                    act(Yt[0:p, :, 0:p], heads(0, DH, p, p), ACT.Copy).then_inc(S("yt"), 1)
                    e.wait_ge(S("w_mm"), 1)
                    act(Wt[0:p, :, 0:p], heads(1, DH, p, p), ACT.Copy).then_inc(S("w"), 1)
                    lv += 1
                else:
                    act(Yt_c, heads(0, DH, HF, P, HF), ACT.Copy).then_inc(S("yt"), 1)
                    for l in range(1, 7):
                        e.wait_ge(S("w_mm"), lv + 1)
                        r = slice(0 if l < 6 else HF, P)
                        act(Wt[r, :, 0:HF], ps[r, 1, 0:DH * HF].rearrange("p (h c) -> p h c", c=HF), ACT.Copy).then_inc(S("w"), 1)
                        lv += 1
                e.wait_ge(S("vnew_mm"), n + 1)
                act(vnew[0:p], heads(0, DH, P, p), ACT.Copy).then_inc(S("vnew"), 1)
                e.wait_ge(S("o_mm"), n + 1)
                act(sqm[:, :, 0:p], heads(4, DH, p), ACT.Square).then_inc(S("o_sq"), 1)
                e.wait_ge(S("o_ms"), n + 1)
                inverse_root(rs[:, :, 0:p], heads(6, DH, p), P, "o_root")
                for g in range(2):
                    i = 2 * n + g
                    e.wait_ge(S("s_mm"), i + 1)
                    e.wait_ge(S("o_out"), n + 1)
                    if g:
                        e.wait_ge(S("y_out"), i)
                    if t:
                        act(EB[:, :, 0:p], heads(1, 8, p), ACT.Exp).then_inc(S("s_eb"), 1)
                    e.wait_ge(S("s_arg"), i + 1)
                    act(D2[0:p, :, 0:p], D2[0:p, :, 0:p], ACT.Exp).then_inc(S("s_exp"), 1)
                    if t == 2:
                        for b in range(NB):
                            e.wait_ge(S("hst_mm"), 8 * g + b + 1)
                            act(HsT[:, b, :], ps[:, 5 + b % 2, :], ACT.Copy).then_inc(S("hst"), 1)
                    e.wait_ge(S("y1"), i + 1)
                    act(sqm[:, :, 0:p], R[:, :, 0:p], ACT.Square).then_inc(S("y_sq"), 1)
                    e.wait_ge(S("y_ms"), i + 1)
                    inverse_root(rs[:, 0, 0:p], ps[:, 0, 0:p], 4 * P, "y_root")
            for i in range(2):
                e.wait_ge(S("ht_mm"), i + 1)
                act(hT_out[:, 4 * i:4 * i + 4, :].rearrange("p a b -> p (a b)"), ps[:, 2 + i, :], ACT.Copy).then_inc(S("ht_out"), 1)
            tail_act(e, inverse_root)

        @block.vector
        def _(e):
            v = nc.vector
            tt, ts, stt = v.tensor_tensor, v.tensor_scalar, v.scalar_tensor_tensor
            n_ = [0]

            def link(ins):
                n_[0] += 1
                ins.then_inc(S("dve_chain"), 1)
                e.wait_ge(S("dve_chain"), n_[0])

            e.wait_ge(S("cT_mm"), 1)
            link(v.memset(cT[:], 0.0))
            v.tensor_copy(cT[:, :, 0:NC], ps[:, 1, 0:KT * NC].rearrange("p (k c) -> p k c", c=NC)).then_inc(S("cT"), 1)
            e.wait_ge(S("tab_mm"), 1)
            v.tensor_copy(colB[:], ps[:, 0, 128:128 + B_ROWS])
            link(v.tensor_copy(colA[:], ps[:, 0, 0:A_ROWS]))
            e.nop().then_inc(S("col"), 1)
            for i in range(4):
                e.wait_ge(S("ada_mm"), i + 1)
                if i >= 2:
                    e.wait_ge(S("mod_mm"), i - 1)
                v.tensor_copy(mod_rows[:, i % 2, :], ps[:, 6 + i % 2, 0:P]).then_inc(S("mod_row"), 1)
                e.wait_ge(S("mod_mm"), i + 1)
                v.tensor_copy(modT[:, 4 * i:4 * i + 4, :],
                              ps[:, 6 + i % 2, P:2 * P].rearrange("p (m c) -> p m c", c=CPAD)[:, :, 0:NC]).then_inc(S("mod_read"), 1)
            e.wait_ge(S("mod_read"), 4)

            def mod_bias(first, n, col):
                b = col.unsqueeze(2).broadcast_to([P, n, NC])
                link(tt(modT[:, first:first + n, :], modT[:, first:first + n, :], b, ALU.add))

            def norm_scale(weight, scale):
                link(stt(scl[:], modT[:, scale:scale + KT, :], 1.0, weight.unsqueeze(2).broadcast_to([P, KT, NC]),
                         ALU.add, ALU.mult))

            def modulated(out, shift):
                link(tt(out, xT[:], rstd[:].unsqueeze(1).broadcast_to([P, KT, TOK]), ALU.mult))
                for k in range(KT):
                    ts(out[:, k, 0:SEQ], out[:, k, 0:SEQ], scl[:, k, 0:1], modT[:, shift + k, 0:1], ALU.mult, ALU.add)
                s = out[:, :, SEQ:TOK].rearrange("p k (b t) -> p k b t", t=NT)
                link(tt(s, s, scl[:, :, 1:NC].unsqueeze(3).broadcast_to([P, KT, NB, NT]), ALU.mult))
                link(tt(s, s, modT[:, shift:shift + KT, 1:NC].unsqueeze(3).broadcast_to([P, KT, NB, NT]), ALU.add))

            mod_bias(0, 16, colA[:, 0:16])
            norm_scale(colA[:, A_NORM:A_NORM + KT], SCALE1)
            e.wait_ge(S("root"), 1)
            modulated(HN, SHIFT1)
            e.nop().then_inc(S("hn"), 1)
            for i in range(2):
                e.wait_ge(S("halo_mm"), i + 1)
                for b in range(NB):
                    l = v.tensor_copy(U[:, NQ * i:NQ * (i + 1), SROW + b * STEP:SROW + b * STEP + HALO],
                                      ps[:, 2 + i, 0:NQ * 24].rearrange("p (m r) -> p m r", r=24)[:, :, 3 * b:3 * b + 3])
                l.then_inc(S("halo_read"), 1)
            e.wait_ge(S("gsm_mm"), 1)
            e.wait_ge(S("consts0"), 1)
            for t, (o, p) in enumerate(TILES):
                v.tensor_copy(gsm[0:p, t, NG:24], ps[0:p, 1, t * 24 + NG:t * 24 + 24])
                l = tt(gsm[0:p, t, 0:NG], ps[0:p, 1, t * 24:t * 24 + NG], bias_row[0:p, :], ALU.add)
            link(l)
            a = gsm[:, :, 0:NG]
            link(ts(t1[:], a, -1.0, None, ALU.mult))
            tt(t1[:], t1[:], a, ALU.max).then_inc(S("gsm1"), 1)
            e.wait_ge(S("gsm_e"), 1)
            link(ts(t2[:], t1[:], 1.0, None, ALU.add))
            link(ts(sp[:], t2[:], -1.0, 1e-30, ALU.add, ALU.add))
            link(v.reciprocal(sp[:], sp[:]))
            link(tt(sp[:], sp[:], t1[:], ALU.mult))
            e.nop().then_inc(S("gsm2"), 1)
            e.wait_ge(S("gsm_ln"), 1)
            e.wait_ge(S("act_chain"), 1)
            link(ts(t2[:], t2[:], 1e-30, None, ALU.add))
            link(tt(sp[:], sp[:], t2[:], ALU.mult))
            link(stt(sp[:], a, 0.0, sp[:], ALU.max, ALU.add))
            ts(nbeta[:], nbeta[:], 1.0, None, ALU.add)
            link(stt(G[:], sp[:], -1.0, alog_row[:].unsqueeze(1).broadcast_to([P, 3, NG]), ALU.mult, ALU.mult))
            link(v.reciprocal(beta[:], nbeta[:]))
            link(ts(nbeta[:], beta[:], -1.0, None, ALU.mult))
            e.nop().then_inc(S("gates"), 1)
            e.wait_ge(S("consts"), 1)
            tt(GM[:], G[0:SMP, 2, :].unsqueeze(2).broadcast_to([SMP, NG, NB]),
               seq_of[:].unsqueeze(1).broadcast_to([SMP, NG, NB]), ALU.mult).then_inc(S("gm"), 1)

            for first, conv in ((0, colA[:, A_CONV:A_CONV + 48]), (NQ, colB[:, B_CONV:B_CONV + 48])):
                for m in range(NQ):
                    tile = first + m
                    e.wait_ge(S("proj_read"), tile + 1 + (4 if first else 0))
                    if first:
                        e.wait_ge(S("co"), m + 1)
                    acc, u = cv[:, m, :], U[:, tile, :]
                    link(ts(acc, u[:, 0:CROW], conv[:, m:m + 1], None, ALU.mult))
                    for i in range(1, 4):
                        l = stt(acc, u[:, i:i + CROW], conv[:, NQ * i + m:NQ * i + m + 1], acc, ALU.mult, ALU.add)
                        if i < 3:
                            link(l)
                    l.then_inc(S("cv"), 1)
            e.wait_ge(S("qk_root"), 1)
            stt(CO[:, 0:DH, :], sq[:, 0:DH, :], P ** -0.5, CO[:, 0:DH, :], ALU.mult, ALU.mult)
            link(tt(CO[:, DH:2 * DH, :], sq[:, DH:2 * DH, :], CO[:, DH:2 * DH, :], ALU.mult))
            e.nop().then_inc(S("qk_normed"), 1)
            e.wait_ge(S("sums_mm"), 1)
            link(v.memset(csum[:], 0.0))
            link(v.memset(dte[:], 0.0))
            for t, (o, p) in enumerate(TILES):
                l = v.tensor_copy(csum[0:p, t, :], ps[0:p, 0, t * NG:(t + 1) * NG])
            link(l)
            for t, (o, p) in enumerate(TILES):
                l = tt(dte[0:p, t, :], ps[0:p, 0, 64 + t * NG:64 + (t + 1) * NG], csum[0:p, t, :], ALU.subtract)
            link(l)
            e.nop().then_inc(S("dte_arg"), 1)
            e.wait_ge(S("drep_mm"), 1)
            link(v.tensor_copy(drep[:].rearrange("p a b -> p (a b)"), ps[:, 7, 16:16 + KT * NC]))
            e.nop().then_inc(S("drep"), 1)
            e.wait_ge(S("co"), NU)
            e.wait_ge(S("mod_read"), 16)
            mod_bias(16, 32, colA[:, 16:48])
            mod_bias(48, 16, colB[:, B_BFIN:B_BFIN + 16])
            e.wait_ge(S("sums"), 1)
            e.wait_ge(S("c_new"), 1)

            lv = [0]
            for n, t in enumerate(ORDER):
                o, p = TILES[t]
                ng = neg if p == P else neg_s
                e.wait_ge(S("dn_mm"), n + 1)
                e.wait_ge(S("dn_eb"), n + 1)
                for h in range(DH):
                    l = stt(D2[0:p, h, 0:p], heads(0, DH, p, p)[:, h], csum[0:p, t, h:h + 1], ng[0:p, 0:p], ALU.subtract, ALU.add)
                l.then_inc(S("dn_arg"), 1)
                v.tensor_copy(kTok[0:p], heads(4, DH, P, p))
                link(v.tensor_copy(vTok[0:p], heads(5, DH, P, p)))
                for h in range(DH):
                    ts(kd[0:p, h, :], kTok[0:p, h, :], dte[0:p, t, h:h + 1], None, ALU.mult)
                e.wait_ge(S("dn_exp"), n + 1)
                dec = D2[0:p, 0:DH, 0:p]
                link(tt(Lt[0:p, :, 0:p], heads(2, DH, p, p), dec, ALU.mult))
                tt(Qd[0:p, :, 0:p], heads(3, DH, p, p), dec, ALU.mult)
                lo, hi = slice(0, HF), slice(HF, P)
                if t == 2:
                    def lev(l):
                        return level[0:p, l:l + 1, 0:p].broadcast_to([p, DH, p])

                    link(tt(Lt[0:p, :, 0:p], heads(1, DH, p, p), Lt[0:p, :, 0:p], ALU.mult))
                    link(tt(Y[0:p, :, 0:p], Lt[0:p, :, 0:p], lev(0), ALU.mult))
                    tt(Mk[0:p, :, 0:p], Lt[0:p, :, 0:p], lev(1), ALU.mult).then_inc(S("mk"), 1)
                    link(tt(Y[0:p, :, 0:p], ident[0:p, 0:p].unsqueeze(1).broadcast_to([p, DH, p]), Y[0:p, :, 0:p], ALU.subtract))
                else:
                    def lev(l):
                        return level[:, l:l + 1, 0:HF].broadcast_to([P, DH, HF])

                    for r in (lo, hi):
                        tt(L_c[r], heads(1, DH, P)[r, :, r], Lt[r, :, r], ALU.mult)
                    link(tt(Lt[lo, :, hi], heads(1, DH, P)[lo, :, hi], Lt[lo, :, hi], ALU.mult))
                    link(tt(Y_c, L_c, lev(0), ALU.mult))
                    tt(Mk_c, L_c, lev(1), ALU.mult).then_inc(S("mk"), 1)
                    for r in (lo, hi):
                        l = tt(Y_c[r], ident[r, r].unsqueeze(1).broadcast_to([HF, DH, HF]), Y_c[r], ALU.subtract)
                    link(l)
                e.nop().then_inc(S("y0"), 1)
                if t != 2:
                    v.memset(Y[hi, :, lo], 0.0)
                if t == 0:
                    for h in range(DH):
                        l = ts(R[0:p, h, :], vTok[0:p, h, :], beta[0:p, t, h:h + 1], None, ALU.mult)
                else:
                    e.wait_ge(S("ks_mm"), n if t == 1 else 1)
                    for h in range(DH):
                        l = stt(R[0:p, h, :], heads(6, DH, P, p)[:, h], ecs[0:p, t, h:h + 1], vTok[0:p, h, :], ALU.mult, ALU.subtract)
                    link(l)
                    for h in range(DH):
                        l = ts(R[0:p, h, :], R[0:p, h, :], nbeta[0:p, t, h:h + 1], None, ALU.mult)
                    tt(qe[:, :, 0:p], CO[:, 0:DH, o:o + p], EB[:, 0:DH, 0:p], ALU.mult)
                link(l)
                e.nop().then_inc(S("r"), 1)
                for l_ in range(1, 7 if t != 2 else 2):
                    e.wait_ge(S("w_mm"), lv[0] + 1)
                    if t != 2 and l_ < 5:
                        tt(Mk_c, L_c, lev(l_ + 1), ALU.mult).then_inc(S("mk"), 1)
                    if l_ == 6:
                        for r in (lo, hi):
                            v.tensor_copy(Y[r, :, r], Y_c[r])
                    e.wait_ge(S("wy_mm"), lv[0] + 1)
                    if t == 2:
                        tt(Y[0:p, :, 0:p], Y[0:p, :, 0:p], heads(2, DH, p, p), ALU.subtract).then_inc(S("y_up"), 1)
                    elif l_ < 6:
                        tt(Yt_c, Yt_c, heads(3, DH, HF, P, HF), ALU.subtract)
                        link(tt(Y_c, Y_c, heads(2, DH, HF, P, HF), ALU.subtract))
                        e.nop().then_inc(S("y_up"), 1)
                    else:
                        ts(Y[lo, :, hi], heads(2, DH, HF, P, HF)[lo], -1.0, None, ALU.mult).then_inc(S("y_up"), 1)
                    lv[0] += 1
                if t == 2:
                    for h in range(DH):
                        e.wait_ge(S("sin_mm"), h + 1)
                        e.wait_ge(S("sin_decayed"), h + 1)
                        tt(Sin[:, h], Sin[:, h], heads(2 * (h % 2), NB, P), ALU.add).then_inc(S("sin_new"), 1)
                else:
                    e.wait_ge(S("ds_mm"), t + 1)
                    e.wait_ge(S("o_mm"), n + 1)
                    if t == 0:
                        l = v.tensor_copy(Sd, heads(5, DH, P))
                    else:
                        for h in range(DH):
                            l = stt(Sd[:, h, :], Sd[:, h, :], elast[:, t, h:h + 1], heads(5, DH, P)[:, h], ALU.mult, ALU.add)
                    l.then_inc(S("sd_new"), 1)
                e.wait_ge(S("o_root"), n + 1)
                on = CO[:, 0:DH, o:o + p]
                link(tt(on, heads(4, DH, p), rs[:, :, 0:p], ALU.mult))
                link(stt(on, on, colB[:, B_DNORM:B_DNORM + 1], ZC[:, 0:DH, o:o + p], ALU.mult, ALU.mult))
                e.nop().then_inc(S("o_out"), 1)

                for g in range(2):
                    i = 2 * n + g
                    hs = slice(DH + 8 * g, DH + 8 * g + 8)
                    e.wait_ge(S("s_mm"), i + 1)
                    if t:
                        e.wait_ge(S("s_eb"), g + 1 + (2 if t == 1 else 0))
                    for h in range(8):
                        c = DH + 8 * g + h
                        l = stt(D2[0:p, h, 0:p], heads(1, 8, p, p)[:, h], csum[0:p, t, c:c + 1], ng[0:p, 0:p], ALU.subtract, ALU.add)
                    l.then_inc(S("s_arg"), 1)
                    v.tensor_copy(Bt[0:p, :], ps[0:p, 3, 0:P]).then_inc(S("bt"), 1)
                    x8 = heads(4, 8, HD, p, HD)
                    link(tt(xdt[0:p], x8, sp[0:p, t, hs].unsqueeze(2).broadcast_to([p, 8, HD]), ALU.mult))
                    tt(xw[0:p], xdt[0:p], dte[0:p, t, hs].unsqueeze(2).broadcast_to([p, 8, HD]), ALU.mult)
                    e.wait_ge(S("s_exp"), i + 1)
                    l = tt(CBd[0:p, :, 0:p], D2[0:p, :, 0:p], ps[0:p, 0:1, 0:p].broadcast_to([p, 8, p]), ALU.mult)
                    if t:
                        l = tt(CE[:, :, 0:p], EB[:, :, 0:p], CO[:, 22 + g:23 + g, o:o + p].broadcast_to([P, 8, p]), ALU.mult)
                    l.then_inc(S("s_ready"), 1)
                    e.wait_ge(S("y_mm"), i + 1)
                    for j in range(4):
                        l = stt(R[:, j, 0:p], CO[:, NQ + 4 * g + j, o:o + p], drep[:, 4 * g + j, NB:NC], heads(5, 4, p)[:, j],
                                ALU.mult, ALU.add)
                    link(l)
                    if t == 2:
                        inter = ps[:, 6, 0:256].rearrange("p (j b a t) -> p j b a t", j=4, b=NB, a=2)
                        for a in range(2):
                            half = slice(HD * a, HD * (a + 1))
                            for j in range(4):
                                r = R[half, j, 0:p].rearrange("p (b t) -> p b t", t=NT)
                                l = tt(r, r, inter[half, j, :, a, :], ALU.add)
                        link(l)
                    tt(R[:, :, 0:p], R[:, :, 0:p], ZC[:, 4 + 4 * g:8 + 4 * g, o:o + p], ALU.mult).then_inc(S("y1"), 1)
                    if t == 2:
                        for j in range(4):
                            e.wait_ge(S("hs_mm"), 4 * g + j + 1)
                            e.wait_ge(S("hs_decayed"), 4 * g + j + 1)
                            tt(Hs[:, j], Hs[:, j], heads(1 + 2 * (j % 2), NB, P), ALU.add).then_inc(S("hs_new"), 1)
                    else:
                        e.wait_ge(S("dh_mm"), 2 * t + g + 1)
                        hg = hT[:, 8 * g:8 * g + 8, :]
                        dh = heads(7, 8, HD, P, HD)
                        if t == 0:
                            v.tensor_copy(hg, dh).then_inc(S("ht"), 1)
                        else:
                            link(tt(hg, hg, elast[:, t, hs].unsqueeze(2).broadcast_to([P, 8, HD]), ALU.mult))
                            tt(hg, hg, dh, ALU.add).then_inc(S("ht"), 1)
                    e.wait_ge(S("y_root"), i + 1)
                    for j in range(4):
                        c = B_SNORM + 4 * g + j
                        l = stt(CO[:, NQ + 4 * g + j, o:o + p], R[:, j, 0:p], colB[:, c:c + 1], rs[:, 0, 0:p], ALU.mult, ALU.mult)
                    l.then_inc(S("y_out"), 1)
            tail_dve(e, link, norm_scale, modulated)


_INS = ["x_prompt", "x_sample", "c_prompt", "c_sample", "state_dn_conv", "state_dn_rec", "state_ssm_conv",
        "state_ssm_rec", "w_ada", "b_ada", "norm_mix_w", "w_in", "dn_conv_w", "dn_A_log", "dn_dt_bias", "dn_norm_w",
        "w_dn_out", "ssm_conv_w", "ssm_conv_b", "ssm_A_log", "ssm_dt_bias", "ssm_D", "ssm_norm_w", "w_ssm_out",
        "w_out", "norm_ffn_w", "w_group_router", "b_group_router", "w_expert_router", "b_expert_router",
        "w_exp_gate", "w_exp_up", "w_exp_down", "w_ada_final", "b_ada_final", "final_norm_w"]
_OUTS = [("y_p", (1, 256, 1024)), ("y_s", (8, 4, 1024)), ("dn_conv_p", (1, 1, 3, 1536)), ("dn_rec_p", (1, 1, 4, 128, 128)),
         ("ssm_conv_p", (1, 1, 3, 1536)), ("ssm_rec_p", (1, 1, 16, 64, 128)), ("dn_conv_s", (1, 8, 3, 1536)),
         ("dn_rec_s", (1, 8, 4, 128, 128)), ("ssm_conv_s", (1, 8, 3, 1536)), ("ssm_rec_s", (1, 8, 16, 64, 128))]


def kernel(**inputs):
    import numpy as _np
    import concourse.bacc as _bacc
    from concourse.bass_utils import run_bass_kernel_spmd as _run

    nc = _bacc.Bacc("TRN2", target_bir_lowering=False, num_devices=1)
    arrays, ins, outs = {}, {}, {}
    for name in _INS:
        a = _np.ascontiguousarray(inputs[name])
        arrays[f"in_{name}"] = a
        ins[name] = nc.dram_tensor(f"in_{name}", a.shape, F32, kind="ExternalInput").ap()
    for name, shape in _OUTS:
        outs[name] = nc.dram_tensor(f"out_{name}", shape, F32, kind="ExternalOutput").ap()
    hybrid_step(nc, ins, outs)
    r = _run(nc, [arrays], core_ids=[0])
    return tuple(r.results[0][f"out_{name}"] for name, _ in _OUTS)
```

```python
from contextlib import ExitStack

import concourse.bass as bass
from concourse import mybir

F32 = mybir.dt.float32
I32 = mybir.dt.int32
ALU = mybir.AluOpType
ACT = mybir.ActivationFunctionType
AX = mybir.AxisListType

P = 128
D = 1024
KT = D // P
SEQ = 256
NB, NT = 8, 4
SMP = NB * NT
TOK = SEQ + SMP
TILES = [(0, P), (P, P), (SEQ, SMP)]
HF = P // 2
ORDER = [2, 0, 1]
NC = 1 + NB
CPAD = 32
DH = 4
SH = 16
HD = 64
NG = DH + SH
QKV = 1536
NQ = QKV // P
NU = 2 * NQ
HALO = 3
SROW = HALO + SEQ
STEP = HALO + NT
ROW = SROW + NB * STEP
CROW = ROW - HALO
ADA_N = 512
WN = 256
E = 32
EG, EPG = 4, 8
FF = 256
FT = FF // P
PAIRS = 2 * TOK
CW = 64
SLOTS = PAIRS + CW
ST = SLOTS // P
ESLOT = 4
ETURN = 2 * ESLOT
EXW = 3 * D * FF // P
EPS = 1e-6
NEG = -1.0e30
C_Z, C_A, C_B, C_XBC, C_DT, C_GATE = 1536, 2048, 2052, 2056, 4616, 4632
RUNS = [(4, 0), (5, C_XBC), (4, C_GATE)]
ZT = 28
SHIFT1, SCALE1, GATE1, SHIFT2, SCALE2, GATE2, SHIFT_F, SCALE_F = range(0, 64, 8)
A_BADA, A_NORM, A_CONV = 0, 48, 56
B_CONV, B_CONVB, B_SNORM, B_FFN, B_BFIN, B_FIN, B_DNORM, B_ROWS = 0, 48, 60, 68, 76, 92, 100, 101
A_ROWS = 104


def hybrid_step(nc, T, O):
    ctx = ExitStack()
    with ctx:
        def sb(name, shape, dt=F32):
            return ctx.enter_context(nc.sbuf_tensor(name, shape, dt))

        sems = {}

        def S(name):
            if name not in sems:
                sems[name] = ctx.enter_context(nc.semaphore(name))
            return sems[name]

        ident = sb("ident", [P, P])
        ones = sb("ones", [P, P])
        tri = sb("tri", [P, P])
        neg = sb("neg", [P, P])
        tri_s = sb("tri_s", [SMP, SMP])
        neg_s = sb("neg_s", [SMP, SMP])
        same_s = sb("same_s", [SMP, SMP])
        seq_of = sb("seq_of", [SMP, NB])
        level = sb("level", [P, 7, P])
        head_rows = sb("head_rows", [SH, KT, P])
        eps_c = sb("eps_c", [P, 1])
        xT = sb("xT", [P, KT, TOK])
        modT = sb("modT", [P, 64, NC])
        colA = sb("colA", [P, A_ROWS])
        colB = sb("colB", [P, B_ROWS])
        scl = sb("scl", [P, KT, NC])
        gsm = sb("gsm", [P, 3, 24])
        rstd = sb("rstd", [P, TOK])
        cT = sb("cT", [P, KT, CPAD])
        mod_rows = sb("mod_rows", [P, 2, P])
        wsm = sb("wsm", [P, KT, 24])
        c_new = sb("c_new", [P, NU, 27])
        MIX = 28970
        NA = MIX + (NU + ZT) * TOK
        arena = sb("arena", [P, NA])

        def carve(at, *shape, parts=P):
            n = 1
            for d in shape:
                n *= d
            assert at + n <= NA, (at, shape)
            ap = arena[0:parts, at:at + n]
            if len(shape) == 2:
                ap = ap.rearrange("p (a b) -> p a b", b=shape[1])
            if len(shape) == 3:
                ap = ap.rearrange("p (a b c) -> p a b c", b=shape[1], c=shape[2])
            return ap, at + n

        CO, at = carve(MIX, NU, TOK)
        ZC, at = carve(at, ZT, TOK)
        at = 0
        ada_ring, w_ring = [], []
        for _ in range(2):
            v, at = carve(at, KT, ADA_N)
            ada_ring.append(v)
        for _ in range(2):
            v, at = carve(at, KT, WN)
            w_ring.append(v)
        cst, _ = carve(KT * ADA_N, NU, P, parts=27)
        U, at = carve(at, NU, ROW)
        cv_at = at
        cv, at = carve(at, NQ, CROW)
        dn_halo, q = carve(cv_at, QKV, parts=NB * HALO)
        ssm_halo, q = carve(q, QKV, parts=NB * HALO)
        tabA, q = carve(q, P, parts=A_ROWS)
        tabB, q = carve(q, P, parts=B_ROWS)
        c_tok, _ = carve(at, D, parts=NC)
        HN, at = carve(at, KT, TOK)
        sq, _ = carve(at, KT, TOK)
        x_tok, at = carve(at, 3, D)
        at = 0
        Sin, at = carve(at, DH, NB, P)
        Hs, at = carve(at, 4, NB, P)
        HsT, at = carve(at, NB, 4 * P)
        hT_out, _ = carve(at, KT, P)
        D2, at = carve(at, 8, P)
        YI, _ = carve(at, 2, 512)
        EB, at = carve(at, 8, P)
        Qd, at = carve(at, DH, P)
        CBd, _ = carve(at, 8, P)
        Lt, at = carve(at, DH, P)
        Mk, at = carve(at, DH, P)
        CE, _ = carve(at, 8, P)
        CE_s, _ = carve(at, NB, SMP)
        Y, at = carve(at, DH, P)
        Yt, at = carve(at, DH, P)
        Wt, at = carve(at, DH, P)
        kTok, at = carve(at, DH, P)
        vTok, at = carve(at, DH, P)
        Yt_c, Y_c, Mk_c, L_c = (m[:, :, c:c + HF] for m in (Yt, Mk) for c in (0, HF))
        R, at = carve(at, DH, P)
        xdt, at = carve(at, 8, HD)
        xw, at = carve(at, 8, HD)
        vnew, at = carve(at, DH, P)
        kd, at = carve(at, DH, P)
        qe, at = carve(at, DH, P)
        Bm, _ = carve(at, NB, P, parts=SMP)
        Vm = []
        for _ in range(2):
            v, at = carve(at, NB, P, parts=SMP)
            Vm.append(v)
        Bt, at = carve(at, P)
        rs, at = carve(at, DH, P)
        sqm, at = carve(at, DH, P)
        Km, at = carve(at, NB, DH, SMP)
        q = at - NB * DH * SMP - 2 * DH * P - 2 * NB * P - P
        CBd2, q = carve(q, 8, P)
        CE2, q = carve(q, 8, P)
        Rs, _ = carve(at - NB * DH * SMP, DH, P)
        o_s, _ = carve(at - NB * DH * SMP, DH, SMP)
        Sd, at = carve(at, DH, P)
        hT, at = carve(at, SH, HD)

        w_dn, at = carve(0, DH, D)
        w_so, at = carve(at, KT, D)
        w_o, at = carve(at + 2 * 8 * P, KT, D)
        merged, at = carve(at, KT, TOK)
        mtmp, at = carve(at, 2, TOK)
        assert at <= MIX
        at = 0
        ex = []
        for i in range(ESLOT):
            at = (0, EXW, MIX, MIX + EXW)[i]
            wgu, at = carve(at, 2 * KT, FF)
            wd, at = carve(at, FT, D)
            ex.append((wgu, wd))
        H2, at = carve(at, KT, TOK)
        XsT, at = carve(2 * EXW, KT, SLOTS)
        ys_at = at
        YsT, at = carve(at, KT, SLOTS)
        tok_at = at
        h2_tok, at = carve(at, 3, D)
        Pm, at = carve(at, 3, SLOTS)
        iota, at = carve(at, SLOTS)
        assert at <= MIX
        Pw, q = carve(ys_at, 3, SLOTS)
        LG, q = carve(q, 3, EG + E)
        r_em, q = carve(q, 3, E)
        r_eq, q = carve(q, 3, E)
        r_o1, q = carve(q, 3, E)
        r_o2, q = carve(q, 3, E)
        r_sp, q = carve(q, 3, E)
        r_g, q = carve(q, 3, EG)
        r_g2, q = carve(q, 3, EG)
        r_m, q = carve(q, 10, 3)
        r_n, q = carve(q, 4, E)
        r_c, q = carve(q, E)
        second, q = carve(q, SLOTS)
        lg_row, q = carve(q, TOK, parts=EG + E)
        assert q <= ys_at + KT * SLOTS
        Ys, _ = carve(2 * EXW, ST, D)
        PT, q = carve(tok_at, ST, TOK)
        xwin, q = carve(q, KT, CW)
        y_row, q = carve(q, D // 2)
        y_col, q = carve(q, 4, P)
        assert q <= tok_at + 3 * D
        y_fin, _ = carve(ys_at, KT, TOK)
        o_tok, _ = carve(0, 3, D)
        w_rt = sb("w_rt", [P, KT, EG + E])
        b_rt = sb("b_rt", [P, EG + E])
        valid = sb("valid", [P, 3])
        tab = sb("tab", [P, 3, E], I32)
        h_row = sb("h_row", [P, P])
        hact = sb("hact", [P, FT, CW])
        bias_row = sb("bias_row", [P, NG])
        alog_row = sb("alog_row", [P, NG])
        dcol = sb("dcol", [SH, NC])
        sp = sb("sp", [P, 3, NG])
        t1 = sb("t1", [P, 3, NG])
        t2 = sb("t2", [P, 3, NG])
        G = sb("G", [P, 3, NG])
        csum = sb("csum", [P, 3, NG])
        ecs = sb("ecs", [P, 3, NG])
        dte = sb("dte", [P, 3, NG])
        beta = sb("beta", [P, 3, DH])
        nbeta = sb("nbeta", [P, 3, DH])
        elast = sb("elast", [P, 2, NG])
        GM = sb("GM", [SMP, NG, NB])
        EL2 = sb("EL2", [P, NG, NB])
        drep = sb("drep", [P, KT, NC])

        ps = ctx.enter_context(nc.psum_tensor("ps", [P, 8, 512], F32))

        def heads(i, n, cols, parts=P, width=P):
            k = -(-n * width // 512)
            v = ps[0:parts, i:i + k, :].rearrange("p a (h c) -> p (a h) c", c=width)
            return v[:, 0:n, 0:cols]

        SSD_S = ((0, 3, 0, 1, 4, 5, 7, (0, 0)), (CBd, CE, R))
        SSD_P = ((3, 3, P, 4, 6, 7, 6, (0, 3)), (CBd2, CE2, Rs))
        DN_S, DN_P = (4, 5, 6), (2, 1, 0)

        wi = T["w_in"][0].rearrange("(k p) n -> p k n", p=P)
        block = ctx.enter_context(nc.Block())

        def tail_loads(e, load, store):
            e.wait_ge(S("y_out"), 6)
            e.wait_ge(S("o_out"), 3)
            load(w_o, T["w_out"][0].rearrange("(k p) n -> p k n", p=P), "wo_ld")
            wg_, wu_, wd_ = (T[n][0].rearrange("e (k p) f -> p e k f", p=P) for n in ("w_exp_gate", "w_exp_up", "w_exp_down"))

            def expert(idx, s, end=None):
                wgu, wd = ex[s]
                if end is not None:
                    e.wait_ge(S("gu_mm"), end + 1)
                for dst, src in ((wgu[:, 0:KT, :], wg_), (wgu[:, KT:2 * KT, :], wu_), (wd, wd_)):
                    if end is not None and src is wd_:
                        e.wait_ge(S("down_mm"), end)
                    load(dst, src[:, bass.ds(idx, 1)].rearrange("p e k f -> p (e k) f"), f"ex_ld{s}")

            e.wait_ge(S("ssm_mm"), KT)
            expert(0, 0)
            expert(1, 1)
            e.wait_ge(S("merged"), KT)
            expert(2, 2)
            expert(3, 3)
            e.wait_ge(S("tab"), 1)
            with e.Fori(1, E // ESLOT) as i:
                for s in range(ESLOT):
                    idx = e.snap(i * ESLOT + s, min_val=0, max_val=E - 1)
                    end = e.value_load(tab[0:1, 1, bass.ds(i * ESLOT + (s - ESLOT), 1)], min_val=1, max_val=E * 5)
                    expert(idx, s, end)
            for t, (o, p) in enumerate(TILES):
                e.wait_ge(S("o_tok"), 2 * t + 2)
                if t < 2:
                    store(O["y_p"][0, o:o + p, :], o_tok[0:p, t, :])
                else:
                    store(O["y_s"].rearrange("b t d -> (b t) d"), o_tok[0:p, t, :])

        def tail_pool_early(e, link):
            g = nc.gpsimd
            link(g.memset(valid[:], 1.0))
            link(g.affine_select(out=valid[:, 2:3], in_=valid[:, 2:3], pattern=[[0, 1]], base=SMP - 1, channel_multiplier=-1,
                                 compare_op=ALU.is_ge, fill=0.0))

        def tail_pool(e, link):
            g = nc.gpsimd
            e.wait_ge(S("y_out"), 6)
            e.wait_ge(S("o_out"), 3)
            e.wait_ge(S("x2"), KT)
            link(g.iota(iota, pattern=[[1, SLOTS]], base=0, channel_multiplier=0, allow_small_or_imprecise_dtypes=True))
            link(g.memset(LG, 0.0))
            link(g.memset(XsT[:, :, PAIRS:SLOTS], 0.0))
            e.nop().then_inc(S("iota"), 1)
            e.wait_ge(S("tab"), 1)
            e.wait_ge(S("pt_mm"), ST)
            e.nop().then_inc(S("ys_w"), 3)
            with e.Fori(0, E // ETURN) as i:
                first = e.value_load(tab[0:1, 0, bass.ds(i * ETURN, 1)], min_val=0, max_val=5 * E - 1)
                for s in range(ETURN):
                    end, slot = expert_end(e, i, s)
                    with e.Fori(first, end) as c:
                        off = window(e, c, first, slot)
                        e.wait_ge(S("y_col"), c + 3)
                        g.tensor_copy(out=YsT[:, :, bass.ds(off, CW)].rearrange("p (h m) n -> p m h n", h=2),
                                      in_=y_col.rearrange("p m (h n) -> p m h n", h=2)).then_inc(S("ys_w"), 1)
                    first = end

        def tail_pe(e):
            mm, tr = nc.tensor.matmul, nc.tensor.transpose
            e.wait_ge(S("wout_ld"), 32)
            e.wait_ge(S("ht_out"), 2)
            for m in range(KT):
                b = 2 * (m % 2)
                if m >= 2:
                    e.wait_ge(S("merged"), m - 1)
                for k in range(DH):
                    mm(ps[:, b, 0:TOK], w_dn[:, k, m * P:(m + 1) * P], CO[:, k, :], start=(k == 0), stop=(k == DH - 1))
                for k in range(KT):
                    l = mm(ps[:, b + 1, 0:TOK], w_so[:, k, m * P:(m + 1) * P], CO[:, NQ + k, :], start=(k == 0), stop=(k == KT - 1))
                l.then_inc(S("ssm_mm"), 1)
            e.wait_ge(S("wo_ld"), 16)
            e.wait_ge(S("merged"), KT)

            def mean_square(n, k):
                e.wait_ge(S("sq"), 1 + KT * (n - 2) + k + 1)
                l = mm(ps[:, 0, 0:TOK], ones[:, :], H2[:, k, :], start=(k == 0), stop=(k == KT - 1))
                if k == KT - 1:
                    l.then_inc(S("ms_mm"), 1)

            for m in range(KT):
                if m >= 2:
                    e.wait_ge(S("x2"), m - 1)
                    mean_square(2, m - 2)
                for k in range(KT):
                    l = mm(ps[:, 4 + m % 2, 0:TOK], w_o[:, k, m * P:(m + 1) * P], merged[:, k, :], start=(k == 0), stop=(k == KT - 1))
                l.then_inc(S("wo_mm"), 1)

            mean_square(2, KT - 2)
            mean_square(2, KT - 1)
            e.wait_ge(S("h2"), 1)
            e.wait_ge(S("x_mod"), 2 * KT)
            e.wait_ge(S("rt_ld"), 64)
            for k in range(KT):
                l = mm(ps[0:EG + E, 1, 0:TOK], w_rt[:, k, :], H2[:, k, :], start=(k == 0), stop=(k == KT - 1))
            l.then_inc(S("rt_mm"), 1)
            for t, (o, p) in enumerate(TILES):
                for half in range(2):
                    for k in range(4):
                        l = tr(ps[0:p, 2 + 2 * t + half if t < 2 else 6 + half, k * P:(k + 1) * P], H2[:, 4 * half + k, o:o + p], ident[:, :])
                    l.then_inc(S("h2t_mm"), 1)
            e.wait_ge(S("lg_row"), 1)
            for t, (o, p) in enumerate(TILES):
                l = tr(ps[0:p, 0, t * 36:(t + 1) * 36], lg_row[:, o:o + p], ident[0:EG + E, 0:EG + E])
            l.then_inc(S("rt_mm"), 1)
            e.wait_ge(S("routed"), 2)
            for t in range(3):
                for u in range(t):
                    mm(ps[:, 0, t * E:(t + 1) * E], ones[:, :], r_eq[:, u, :], start=(u == 0), stop=False)
                mm(ps[:, 0, t * E:(t + 1) * E], tri[:, :], r_eq[:, t, :], start=(t == 0), stop=True)
            for t in range(3):
                l = mm(ps[:, 0, 3 * E:4 * E], ones[:, :], r_eq[:, t, :], start=(t == 0), stop=(t == 2))
            l.then_inc(S("count_mm"), 1)
            e.wait_ge(S("h2_tok"), 6)
            e.wait_ge(S("placed"), 1)
            for k in range(KT):
                b = 4 + 2 * (k % 2)
                if k >= 2:
                    e.wait_ge(S("xs"), k - 1)
                for c0, n in ((0, 512), (512, PAIRS - 512)):
                    for t, (o, p) in enumerate(TILES):
                        l = mm(ps[:, b + c0 // 512, 0:n], h2_tok[0:p, t, k * P:(k + 1) * P], Pm[0:p, t, c0:c0 + n],
                               start=(t == 0), stop=(t == 2))
                l.then_inc(S("xs_mm"), 1)
            e.wait_ge(S("placed"), 2)
            for s in range(ST):
                w = min(P, PAIRS - s * P)
                if s >= 2:
                    e.wait_ge(S("pt"), s - 1)
                for t, (o, p) in enumerate(TILES):
                    l = tr(ps[0:w, s % 2, o:o + p], Pw[0:p, t, s * P:s * P + w], ident[0:p, 0:p])
                l.then_inc(S("pt_mm"), 1)
            e.wait_ge(S("pt"), ST)
            e.wait_ge(S("tab"), 1)
            e.nop().then_inc(S("yrow_mm"), 1)
            e.nop().then_inc(S("gu_mm"), 1)

            def result_transposed(n):
                e.wait_ge(S("y_row"), n + 1)
                e.wait_ge(S("y_col"), n + 1)
                for m in range(4):
                    l = tr(ps[:, 3, m * P:(m + 1) * P], y_row[:, m * P:(m + 1) * P], ident[:, :])
                l.then_inc(S("yrow_mm"), 1)

            with e.Fori(0, E // ETURN) as i:
                bounds = [e.value_load(tab[0:1, 0, bass.ds(i * ETURN, 1)], min_val=0, max_val=5 * E - 1)]
                for s in range(ETURN):
                    wgu, wd = ex[s % ESLOT]
                    gate_up = wgu.rearrange("p (g k) f -> p g k f", g=2)
                    e.wait_ge(S(f"ex_ld{s % ESLOT}"), i * (48 * ETURN // ESLOT) + 48 * (s // ESLOT + 1))
                    bounds.append(e.value_load(tab[0:1, 1, bass.ds(i * ETURN + s, 1)], min_val=1, max_val=5 * E))
                    with e.Fori(bounds[s], bounds[s + 1]) as c:
                        e.wait_ge(S("xwin"), c + 1)
                        for k in range(KT):
                            for f in range(FT):
                                l = mm(ps[CW * f:CW * (f + 1), 0, 0:2 * P].rearrange("p (g f) -> p g f", g=2), xwin[:, k, :],
                                       gate_up[:, :, k, f * P:(f + 1) * P], start=(k == 0), stop=(k == KT - 1))
                        l.then_inc(S("gu_mm"), 1)
                        result_transposed(c)
                        e.wait_ge(S("h_row"), c + 1)
                        tr(ps[:, 1, 0:P], h_row[:], ident[:, :]).then_inc(S("h_mm"), 1)
                        e.wait_ge(S("hact"), c + 1)
                        for f in range(FT):
                            for m in range(2):
                                l = mm(ps[CW * m:CW * (m + 1), 2, :], hact[:, f, :], wd[:, f, m * 512:(m + 1) * 512],
                                       start=(f == 0), stop=(f == FT - 1))
                        l.then_inc(S("down_mm"), 1)
            chunks = e.value_load(tab[0:1, 1, E - 1:E], min_val=1, max_val=5 * E)
            result_transposed(chunks)
            e.wait_ge(S("ys_w"), chunks + 3)
            for s in range(ST):
                w = min(P, PAIRS - s * P)
                for half in range(2):
                    i = 2 * s + half
                    if i >= 4:
                        e.wait_ge(S("ys"), i - 3)
                    for k in range(4):
                        l = tr(ps[0:w, 4 + i % 4, k * P:(k + 1) * P], YsT[:, 4 * half + k, s * P:s * P + w], ident[:, :])
                    l.then_inc(S("ys_mm"), 1)
            e.wait_ge(S("ys"), 2 * ST)
            for k in range(KT):
                if k >= 2:
                    e.wait_ge(S("x3"), k - 1)
                    mean_square(3, k - 2)
                for s in range(ST):
                    w = min(P, PAIRS - s * P)
                    l = mm(ps[:, 2 + k % 2, 0:TOK], Ys[0:w, s, k * P:(k + 1) * P], PT[0:w, s, :], start=(s == 0), stop=(s == ST - 1))
                l.then_inc(S("comb_mm"), 1)
            mean_square(3, KT - 2)
            mean_square(3, KT - 1)
            e.wait_ge(S("y_fin"), 1)
            e.wait_ge(S("x_mod"), 3 * KT)
            for t, (o, p) in enumerate(TILES):
                for half in range(2):
                    i = 2 * t + half
                    for k in range(4):
                        l = tr(ps[0:p, 2 + i, k * P:(k + 1) * P], y_fin[:, 4 * half + k, o:o + p], ident[:, :])
                    l.then_inc(S("ot_mm"), 1)

        def expert_end(e, i, s):
            at_ = i * ETURN + s
            return (e.value_load(tab[0:1, 1, bass.ds(at_, 1)], min_val=1, max_val=5 * E),
                    e.value_load(tab[0:1, 2, bass.ds(at_, 1)], min_val=0, max_val=PAIRS))

        def window(e, c, first, slot):
            return nc.s_assert_within((c - first) * CW + slot, min_val=0, max_val=PAIRS, 
                                      skip_runtime_bounds_check_because="a chunk starts before its expert's end, at slot 576 at most")

        def tail_act(e, inverse_root, prompt_modulated):
            act = nc.scalar.activation
            e.wait_ge(S("merged"), KT)
            for k in range(KT):
                e.wait_ge(S("x2"), k + 1)
                act(H2[:, k, :], xT[:, k, :], ACT.Square).then_inc(S("sq"), 1)
            e.wait_ge(S("ms_mm"), 2)
            inverse_root(rstd[:], ps[:, 0, 0:TOK], D, "root")
            prompt_modulated(H2, SHIFT2, 2)
            for t, (o, p) in enumerate(TILES):
                for half in range(2):
                    e.wait_ge(S("h2t_mm"), 2 * t + half + 1)
                    act(h2_tok[0:p, t, half * 512:(half + 1) * 512], ps[0:p, 2 + 2 * t + half if t < 2 else 6 + half, :],
                        ACT.Copy).then_inc(S("h2_tok"), 1)
            e.wait_ge(S("routed"), 1)
            act(r_g2, r_g2, ACT.Exp)
            act(r_m[:, 6, :], r_m[:, 6, :], ACT.Exp).then_inc(S("r_exp"), 1)
            for k in range(KT):
                e.wait_ge(S("xs_mm"), k + 1)
                b = 4 + 2 * (k % 2)
                act(XsT[:, k, 0:PAIRS], ps[:, b:b + 2, :].rearrange("p a n -> p (a n)")[:, 0:PAIRS], ACT.Copy).then_inc(S("xs"), 1)
            e.wait_ge(S("tab"), 1)
            e.wait_ge(S("pt_mm"), ST)
            e.wait_ge(S("xs"), KT)
            e.wait_ge(S("iota"), 1)

            def result_copied(n):
                e.wait_ge(S("yrow_mm"), n + 1)
                e.wait_ge(S("ys_w"), n + 1)
                act(y_col.rearrange("p m n -> p (m n)"), ps[:, 3, :], ACT.Copy).then_inc(S("y_col"), 1)

            with e.Fori(0, E // ETURN) as i:
                first = e.value_load(tab[0:1, 0, bass.ds(i * ETURN, 1)], min_val=0, max_val=5 * E - 1)
                for s in range(ETURN):
                    end, slot = expert_end(e, i, s)
                    with e.Fori(first, end) as c:
                        off = window(e, c, first, slot)
                        e.wait_ge(S("gu_mm"), c + 1)
                        act(xwin, XsT[:, :, bass.ds(off, CW)], ACT.Copy).then_inc(S("xwin"), 1)
                        result_copied(c)
                        e.wait_ge(S("gu_mm"), c + 2)
                        act(h_row[:], ps[:, 0, 0:P], ACT.Silu).then_inc(S("h_silu"), 1)
                        e.wait_ge(S("h_mm"), c + 1)
                        act(hact[:].rearrange("p f n -> p (f n)"), ps[:, 1, 0:P], ACT.Copy).then_inc(S("hact"), 1)
                    first = end
            chunks = e.value_load(tab[0:1, 1, E - 1:E], min_val=1, max_val=5 * E)
            result_copied(chunks)
            result_copied(chunks + 1)
            for s in range(ST):
                w = min(P, PAIRS - s * P)
                for half in range(2):
                    i = 2 * s + half
                    e.wait_ge(S("ys_mm"), i + 1)
                    act(Ys[0:w, s, half * 512:(half + 1) * 512], ps[0:w, 4 + i % 4, :], ACT.Copy).then_inc(S("ys"), 1)
            for k in range(KT):
                e.wait_ge(S("x3"), k + 1)
                act(H2[:, k, :], xT[:, k, :], ACT.Square).then_inc(S("sq"), 1)
            e.wait_ge(S("ms_mm"), 3)
            inverse_root(rstd[:], ps[:, 0, 0:TOK], D, "root")
            prompt_modulated(y_fin, SHIFT_F, 3)
            for t, (o, p) in enumerate(TILES):
                for half in range(2):
                    i = 2 * t + half
                    e.wait_ge(S("ot_mm"), i + 1)
                    act(o_tok[0:p, t, half * 512:(half + 1) * 512], ps[0:p, 2 + i, :], ACT.Copy).then_inc(S("o_tok"), 1)

        def tail_dve(e, link, norm_scale, modulated, samples_modulated):
            v = nc.vector
            tt, ts, stt = v.tensor_tensor, v.tensor_scalar, v.scalar_tensor_tensor

            for m in range(KT):
                e.wait_ge(S("ssm_mm"), m + 1)
                b = 2 * (m % 2)
                if m:
                    e.wait_ge(S("merged"), m)
                tt(mtmp[:, 0, :], ZC[:, 12 + m, :], ps[:, b, 0:TOK], ALU.mult)
                link(tt(mtmp[:, 1, :], ZC[:, 20 + m, :], ps[:, b + 1, 0:TOK], ALU.mult))
                tt(merged[:, m, :], mtmp[:, 0, :], mtmp[:, 1, :], ALU.add).then_inc(S("merged"), 1)

            def gated_add(m, src, gate, sem):
                stt(xT[:, m, 0:SEQ], src[:, 0:SEQ], modT[:, gate + m, 0:1], xT[:, m, 0:SEQ], ALU.mult, ALU.add)
                s = mtmp[:, 0, 0:SMP].rearrange("p (b t) -> p b t", t=NT)
                if m:
                    e.wait_ge(S(sem), m)
                link(tt(s, src[:, SEQ:TOK].rearrange("p (b t) -> p b t", t=NT),
                        modT[:, gate + m, 1:NC].unsqueeze(2).broadcast_to([P, NB, NT]), ALU.mult))
                tt(xT[:, m, SEQ:TOK], xT[:, m, SEQ:TOK], mtmp[:, 0, 0:SMP], ALU.add).then_inc(S(sem), 1)

            for m in range(KT):
                e.wait_ge(S("wo_mm"), m + 1)
                gated_add(m, ps[:, 4 + m % 2, :], GATE1, "x2")
            e.wait_ge(S("x2"), KT)
            norm_scale(colB[:, B_FFN:B_FFN + KT], SCALE2)
            e.wait_ge(S("root"), 2)
            modulated(H2)
            samples_modulated(H2, SHIFT2, 2)
            e.nop().then_inc(S("h2"), 1)

            e.wait_ge(S("rt_mm"), 1)
            v.tensor_copy(lg_row, ps[0:EG + E, 1, 0:TOK]).then_inc(S("lg_row"), 1)
            e.wait_ge(S("rt_mm"), 2)
            e.wait_ge(S("iota"), 1)
            for t, (o, p) in enumerate(TILES):
                l = tt(LG[0:p, t, :], ps[0:p, 0, t * 36:(t + 1) * 36], b_rt[0:p, :], ALU.add)
            link(l)
            gl, el = LG[:, :, 0:EG], LG[:, :, EG:EG + E]

            def first_of(out, src, maximum, n):
                link(v.tensor_reduce(out=maximum, in_=src, op=ALU.max, axis=AX.X))
                link(tt(out, src, maximum.unsqueeze(2).broadcast_to([P, 3, n]), ALU.is_equal))
                for t in range(3):
                    l = stt(out[:, t, :], out[:, t, :], -float(2 * E), iota[:, 0:n], ALU.mult, ALU.add)
                link(l)
                link(v.tensor_reduce(out=r_m[:, 9, :], in_=out, op=ALU.min, axis=AX.X))
                link(tt(out, out, r_m[:, 9, :].unsqueeze(2).broadcast_to([P, 3, n]), ALU.is_equal))

            first_of(r_g, gl, r_m[:, 0, :], EG)
            link(tt(r_g2, gl, r_m[:, 0, :].unsqueeze(2).broadcast_to([P, 3, EG]), ALU.subtract))
            em4 = r_em.rearrange("p t (g x) -> p t g x", g=EG)
            link(tt(em4, el.rearrange("p t (g x) -> p t g x", g=EG), r_g.unsqueeze(3).broadcast_to([P, 3, EG, EPG]), ALU.mult))
            link(ts(r_g, r_g, -NEG, NEG, ALU.mult, ALU.add))
            link(tt(em4, em4, r_g.unsqueeze(3).broadcast_to([P, 3, EG, EPG]), ALU.add))
            first_of(r_o1, r_em, r_m[:, 1, :], E)
            link(stt(r_em, r_o1, 2 * NEG, r_em, ALU.mult, ALU.add))
            first_of(r_o2, r_em, r_m[:, 2, :], E)
            link(tt(r_m[:, 6, :], r_m[:, 2, :], r_m[:, 1, :], ALU.subtract))
            e.nop().then_inc(S("routed"), 1)
            for oh in (r_o1, r_o2):
                link(tt(oh, oh, valid[:].unsqueeze(2).broadcast_to([P, 3, E]), ALU.mult))
            link(tt(r_eq, r_o1, r_o2, ALU.add))
            e.nop().then_inc(S("routed"), 1)
            e.wait_ge(S("r_exp"), 1)
            link(v.tensor_reduce(out=r_m[:, 3, :], in_=r_g2, op=ALU.add, axis=AX.X))
            link(stt(r_m[:, 3, :], r_m[:, 6, :], 1.0, r_m[:, 3, :], ALU.add, ALU.mult))
            link(v.reciprocal(r_m[:, 4, :], r_m[:, 3, :]))
            link(tt(r_m[:, 5, :], r_m[:, 4, :], r_m[:, 6, :], ALU.mult))
            e.wait_ge(S("count_mm"), 1)
            link(v.tensor_copy(r_n[:, 0, :], ps[:, 0, 3 * E:4 * E]))
            link(v.memset(r_c, 1.0))
            link(v.tensor_tensor_scan(out=r_n[:, 1, :], data0=r_c, data1=r_n[:, 0, :], initial=0.0, op0=ALU.mult, op1=ALU.add))
            link(tt(r_n[:, 1, :], r_n[:, 1, :], r_n[:, 0, :], ALU.subtract))
            link(v.memset(r_n[:, 2, :], 1.0))
            for q_ in range(1, 5):
                link(stt(r_n[:, 2, :], r_n[:, 0, :], float(q_ * CW), r_n[:, 2, :], ALU.is_gt, ALU.add))
            link(v.tensor_tensor_scan(out=r_n[:, 3, :], data0=r_c, data1=r_n[:, 2, :], initial=0.0, op0=ALU.mult, op1=ALU.add))
            tt(tab[:, 0, :], r_n[:, 3, :], r_n[:, 2, :], ALU.subtract)
            v.tensor_copy(tab[:, 1, :], r_n[:, 3, :])
            v.tensor_copy(tab[:, 2, :], r_n[:, 1, :]).then_inc(S("tab"), 1)
            link(tt(r_sp, ps[:, 0, 0:3 * E].rearrange("p (t x) -> p t x", t=3), r_n[:, 1:2, :].broadcast_to([P, 3, E]), ALU.add))
            for oh, at_ in ((r_o1, 7), (r_o2, 8)):
                link(tt(oh, oh, r_sp, ALU.mult))
                link(v.tensor_reduce(out=r_m[:, at_, :], in_=oh, op=ALU.add, axis=AX.X))
                link(ts(r_m[:, at_, :], r_m[:, at_, :], -1.0, None, ALU.add))
            for t in range(3):
                s1, s2 = r_m[:, 7, t:t + 1], r_m[:, 8, t:t + 1]
                link(ts(Pm[:, t, :], iota, s1, None, ALU.is_equal))
                link(stt(Pm[:, t, :], iota, s2, Pm[:, t, :], ALU.is_equal, ALU.add))
            e.nop().then_inc(S("placed"), 1)
            for t in range(3):
                s1, s2, w1, w2 = (r_m[:, x, t:t + 1] for x in (7, 8, 4, 5))
                ts(Pw[:, t, :], iota, s1, w1, ALU.is_equal, ALU.mult)
                link(ts(second, iota, s2, w2, ALU.is_equal, ALU.mult))
                link(tt(Pw[:, t, :], Pw[:, t, :], second, ALU.add))
            e.nop().then_inc(S("placed"), 1)

            for s in range(ST):
                w = min(P, PAIRS - s * P)
                e.wait_ge(S("pt_mm"), s + 1)
                v.tensor_copy(PT[0:w, s, :], ps[0:w, s % 2, 0:TOK]).then_inc(S("pt"), 1)
            v.memset(y_row, 0.0).then_inc(S("y_row"), 1)
            chunks = e.value_load(tab[0:1, 1, E - 1:E], min_val=1, max_val=5 * E)
            with e.Fori(0, chunks) as c:
                e.wait_ge(S("h_silu"), c + 1)
                tt(h_row[:], h_row[:], ps[:, 0, P:2 * P], ALU.mult).then_inc(S("h_row"), 1)
                e.wait_ge(S("down_mm"), c + 1)
                e.wait_ge(S("yrow_mm"), c + 2)
                v.tensor_copy(y_row, ps[:, 2, :]).then_inc(S("y_row"), 1)
            for k in range(KT):
                e.wait_ge(S("comb_mm"), k + 1)
                gated_add(k, ps[:, 2 + k % 2, :], GATE2, "x3")
            e.wait_ge(S("x3"), KT)
            norm_scale(colB[:, B_FIN:B_FIN + KT], SCALE_F)
            e.wait_ge(S("root"), 3)
            modulated(y_fin)
            samples_modulated(y_fin, SHIFT_F, 3)
            e.nop().then_inc(S("y_fin"), 1)

        @block.sync
        def _(e):
            def load(dst, src, s):
                e.dma_start(dst, src).then_inc(S(s), 16)

            stores = [0]

            def store(dst, src):
                e.dma_start(dst, src).then_inc(S("stored"), 16)
                stores[0] += 1

            load(c_tok[0:1, :], T["c_prompt"], "c_ld")
            load(c_tok[1:NC, :], T["c_sample"], "c_ld")
            wa = T["w_ada"][0].rearrange("(k p) n -> p k n", p=P)
            wf = T["w_ada_final"].rearrange("(k p) n -> p k n", p=P)
            for sl in range(2):
                load(ada_ring[sl], wa[:, :, sl * ADA_N:(sl + 1) * ADA_N], f"ada_ld{sl}")
            r = 0
            for n, k in (("b_ada", 48), ("norm_mix_w", 8)):
                load(tabA[r:r + k, :], T[n][0].rearrange("(m p) -> m p", p=P), "tab_ld")
                r += k
            load(tabA[r:r + 48, :], T["dn_conv_w"][0].rearrange("i (m p) -> (i m) p", p=P), "tab_ld")
            load(tabB[0:48, :], T["ssm_conv_w"][0].rearrange("i (m p) -> (i m) p", p=P), "tab_ld")
            r = 48
            for n, k in (("ssm_conv_b", 12), ("ssm_norm_w", 8), ("norm_ffn_w", 8),
                         ("b_ada_final", 16), ("final_norm_w", 8), ("dn_norm_w", 1)):
                a = T[n] if n in ("b_ada_final", "final_norm_w") else T[n][0]
                load(tabB[r:r + k, :], a.rearrange("(m p) -> m p", p=P), "tab_ld")
                r += k
            for t in range(2):
                load(x_tok[:, t, :], T["x_prompt"][0, t * P:(t + 1) * P, :], "x_ld")
            load(x_tok[0:SMP, 2, :], T["x_sample"].rearrange("b t d -> (b t) d"), "x_ld")
            for sl in range(2):
                e.wait_ge(S("ada_mm"), sl + 1)
                load(ada_ring[sl], wa[:, :, (2 + sl) * ADA_N:(3 + sl) * ADA_N], f"ada_ld{sl}")
            load(wsm[:, :, 0:4], wi[:, :, C_A:C_A + 4], "small_ld")
            load(wsm[:, :, 4:20], wi[:, :, C_DT:C_DT + 16], "small_ld")
            load(wsm[:, :, 20:24], wi[:, :, C_B:C_B + 4], "small_ld")
            load(bias_row[:, 0:4], T["dn_dt_bias"].broadcast_to([P, 4]), "small_ld")
            load(bias_row[:, 4:20], T["ssm_dt_bias"].broadcast_to([P, 16]), "small_ld")
            load(alog_row[:, 0:4], T["dn_A_log"].broadcast_to([P, 4]), "small_ld")
            load(alog_row[:, 4:20], T["ssm_A_log"].broadcast_to([P, 16]), "small_ld")
            load(dcol[:, NB:NC], T["ssm_D"].rearrange("o h -> h o"), "small_ld")
            load(dn_halo, T["state_dn_conv"][0].rearrange("b t c -> (b t) c"), "halo_ld")
            load(ssm_halo, T["state_ssm_conv"][0].rearrange("b t c -> (b t) c"), "halo_ld")
            load(w_rt[:, :, 0:EG], T["w_group_router"][0].rearrange("(k p) n -> p k n", p=P), "rt_ld")
            load(w_rt[:, :, EG:], T["w_expert_router"][0].rearrange("(k p) n -> p k n", p=P), "rt_ld")
            load(b_rt[:, 0:EG], T["b_group_router"].broadcast_to([P, EG]), "rt_ld")
            load(b_rt[:, EG:], T["b_expert_router"].broadcast_to([P, E]), "rt_ld")
            done = 0
            for n, first in RUNS:
                wada, ada_first = (wf, -9 * ADA_N) if done == 9 else (wa, 3 * ADA_N)
                if done == 0:
                    for sl in range(2):
                        load(w_ring[sl], wi[:, :, first + sl * WN:first + (sl + 1) * WN], f"win_ld{sl}")
                with e.Fori(1 if done == 0 else 0, n) as i:
                    e.wait_ge(S("ada_mm"), i + (done + 3))
                    e.wait_ge(S("proj_mm"), i * 4 + (4 * done - 2))
                    load(w_ring[0], wi[:, :, bass.ds(i * (2 * WN) + first, WN)], "win_ld0")
                    load(ada_ring[0], wada[:, :, bass.ds(i * ADA_N + (done * ADA_N + ada_first), ADA_N)], "ada_ld0")
                    e.wait_ge(S("proj_mm"), i * 4 + 4 * done)
                    load(w_ring[1], wi[:, :, bass.ds(i * (2 * WN) + (first + WN), WN)], "win_ld1")
                done += n
            e.wait_ge(S("ada_mm"), 16)
            for h in range(DH):
                load(Sin[:, h], T["state_dn_rec"][0, :, h].rearrange("b k v -> k b v"), "sin_ld")
            hs_in = T["state_ssm_rec"][0].rearrange("b h p n -> (h p) b n")
            hs_out = O["ssm_rec_s"][0].rearrange("b h p n -> (h p) b n")
            e.wait_ge(S("cstate"), NU // 4)
            for name, c0 in (("dn_conv", 0), ("ssm_conv", NQ)):
                store(O[name + "_p"][0, 0], cst[0:3, c0:c0 + NQ, :].rearrange("p a b -> p (a b)"))
                store(O[name + "_s"][0].rearrange("b t c -> (b t) c"),
                      cst[3:27, c0:c0 + NQ, :].rearrange("p a b -> p (a b)"))
            e.wait_ge(S("stored"), 64)
            for j in range(4):
                load(Hs[:, j], hs_in[j * P:(j + 1) * P], "hs_ld")
            for h in range(DH):
                e.wait_ge(S("sin_new"), h + 1)
                store(O["dn_rec_s"][0, :, h].rearrange("b k v -> k b v"), Sin[:, h])
            for g in range(2):
                for j in range(4):
                    e.wait_ge(S("hs_new"), 4 * g + j + 1)
                    e.dma_start(hs_out[(4 * g + j) * P:(4 * g + j + 1) * P], Hs[:, j]).then_inc(S("hs_stored"), 16)
                e.wait_ge(S("hs_stored"), 64 * (g + 1))
                if g == 0:
                    for j in range(4):
                        load(Hs[:, j], hs_in[(4 + j) * P:(5 + j) * P], "hs_ld")
            e.wait_ge(S("stored"), 16 * stores[0])
            load(w_dn, T["w_dn_out"][0].rearrange("(k p) n -> p k n", p=P), "wout_ld")
            load(w_so, T["w_ssm_out"][0].rearrange("(k p) n -> p k n", p=P), "wout_ld")
            e.wait_ge(S("sd_new"), 2)
            store(O["dn_rec_p"][0, 0].rearrange("h k v -> k h v"), Sd)
            e.wait_ge(S("ht_out"), 2)
            store(O["ssm_rec_p"][0, 0].rearrange("(j a) p n -> (a p) j n", a=2), hT_out)
            tail_loads(e, load, store)
            e.wait_ge(S("stored"), 16 * stores[0])

        @block.gpsimd
        def _(e):
            n = [0]

            def link(ins):
                n[0] += 1
                ins.then_inc(S("pool_chain"), 1)
                e.wait_ge(S("pool_chain"), n[0])

            g = nc.gpsimd
            tail_pool_early(e, link)

            def select(ap, pattern, base, mult, op=ALU.is_ge, fill=0.0):
                link(g.affine_select(out=ap, in_=ap, pattern=pattern, base=base, channel_multiplier=mult,
                                     compare_op=op, fill=fill))

            link(g.memset(ident[:], 0.0))
            select(ident[:], [[-1, P]], 0, 1, ALU.not_equal, 1.0)
            link(g.memset(ones[:], 1.0))
            link(g.memset(eps_c[:], EPS))
            link(g.memset(U[:, :, 0:HALO], 0.0))
            link(g.memset(gsm[:], 0.0))
            g.memset(dcol[:, 0:NB], 0.0).then_inc(S("consts"), 1)
            link(g.memset(tri[:], 1.0))
            select(tri[:], [[1, P]], 0, -1)
            link(g.memset(neg[:], 0.0))
            select(neg[:], [[1, P]], 0, -1, fill=NEG)
            for m, start, fill in ((tri_s, 1.0, 0.0), (neg_s, 0.0, NEG)):
                link(g.memset(m[:], start))
                select(m[:], [[1, SMP]], 0, -1, fill=fill)
                select(m[:].rearrange("p (b t) -> p b t", t=NT), [[-NT, NB], [0, NT]], 0, 1, fill=fill)
            link(g.memset(same_s[:], 1.0))
            select(same_s[:].rearrange("p (b t) -> p b t", t=NT), [[-NT, NB], [0, NT]], 0, 1)
            select(same_s[:].rearrange("p (b t) -> p b t", t=NT), [[NT, NB], [0, NT]], NT - 1, -1)
            link(g.memset(seq_of[:], 1.0))
            select(seq_of[:], [[-NT, NB]], 0, 1)
            select(seq_of[:], [[NT, NB]], NT - 1, -1)
            link(g.memset(level[:], 0.0))
            for l in range(7):
                s = 1 << l
                odd = level[:, l, :].rearrange("p (n c s) -> p n c s", c=2, s=s)[:, :, 1, :]
                link(g.memset(odd, 1.0))
                select(odd, [[-2 * s, P // (2 * s)], [0, s]], 0, 1)
                select(odd, [[2 * s, P // (2 * s)], [0, s]], s - 1, -1)
            link(g.tensor_copy(out=level[HF:P, 0:6, 0:HF], in_=level[HF:P, 0:6, HF:P]))
            link(g.memset(head_rows[:], 0.0))
            hv = head_rows[:].rearrange("p j (a c) -> p j a c", a=2)
            g.affine_select(out=hv, in_=hv, pattern=[[-2, KT], [-1, 2], [0, HD]], base=0, channel_multiplier=1,
                            compare_op=ALU.not_equal, fill=1.0).then_inc(S("consts"), 1)
            e.wait_ge(S("proj_read"), 28)
            link(g.tensor_copy(out=c_new[:, :, 0:HALO], in_=U[:, :, SROW - HALO:SROW]))
            for b in range(NB):
                c0 = SROW + b * STEP + NT
                link(g.tensor_copy(out=c_new[:, :, HALO * (b + 1):HALO * (b + 2)], in_=U[:, :, c0:c0 + HALO]))
            e.nop().then_inc(S("c_new"), 1)
            e.wait_ge(S("qk_normed"), 1)
            e.wait_ge(S("co"), NU)
            e.wait_ge(S("proj_mm"), 52)
            link(g.memset(Km, 0.0))
            for b in range(NB):
                c0 = SEQ + b * NT
                link(g.tensor_copy(out=Km[:, b, :, b * NT:(b + 1) * NT], in_=CO[:, DH:2 * DH, c0:c0 + NT]))
            e.nop().then_inc(S("km"), 1)
            e.wait_ge(S("vnew"), 1)
            for h in range(DH):
                if h >= 2:
                    e.wait_ge(S("sin_mm"), h - 1)
                link(g.tensor_tensor(out=Vm[h % 2], in0=vnew[0:SMP, h:h + 1, :].broadcast_to([SMP, NB, P]),
                                     in1=seq_of[:].unsqueeze(2).broadcast_to([SMP, NB, P]), op=ALU.mult))
                e.nop().then_inc(S("vm"), 1)
            for h in range(2):
                e.wait_ge(S("bt"), h + 1)
                e.wait_ge(S("sin_mm"), DH)
                link(g.tensor_tensor(out=Bm, in0=Bt[0:SMP, :].unsqueeze(1).broadcast_to([SMP, NB, P]),
                                     in1=seq_of[:].unsqueeze(2).broadcast_to([SMP, NB, P]), op=ALU.mult))
                e.nop().then_inc(S("bm"), 1)
                e.wait_ge(S("hst_mm"), 8 * (h + 1))
                for j in range(4):
                    link(g.tensor_tensor(out=Hs[:, j], in0=Hs[:, j],
                                         in1=drep[:, 4 * h + j, 0:NB].unsqueeze(2).broadcast_to([P, NB, P]), op=ALU.mult))
                    e.nop().then_inc(S("hs_decayed"), 1)
            tail_pool(e, link)

        @block.tensor
        def _(e):
            mm, tr = nc.tensor.matmul, nc.tensor.transpose
            e.wait_ge(S("consts"), 1)
            e.wait_ge(S("c_silu"), 1)
            for k in range(KT):
                l = tr(ps[:, 1, k * NC:(k + 1) * NC], c_tok[:, k * P:(k + 1) * P], ident[0:NC, 0:NC])
            l.then_inc(S("first_mm"), 1)
            e.wait_ge(S("tab_ld"), 16 * 10)
            tr(ps[:, 0, 0:A_ROWS], tabA, ident[0:A_ROWS, 0:A_ROWS])
            tr(ps[:, 0, 128:128 + B_ROWS], tabB, ident[0:B_ROWS, 0:B_ROWS]).then_inc(S("first_mm"), 1)

            def ada_products(slot, bank):
                for k in range(KT):
                    for q in range(4):
                        l = mm(ps[CPAD * q:CPAD * (q + 1), bank, 0:P], cT[:, k, :], ada_ring[slot][:, k, q * P:(q + 1) * P],
                               start=(k == 0), stop=(k == KT - 1))
                l.then_inc(S("ada_mm"), 1)

            def ada_transposed(slot, bank):
                tr(ps[:, bank, P:2 * P], mod_rows[:, slot, :], ident[:, :]).then_inc(S("mod_mm"), 1)

            e.wait_ge(S("cT"), 1)
            for i in range(2):
                for sl in range(2):
                    e.wait_ge(S(f"ada_ld{sl}"), i * 16 + 16)
                    if i:
                        e.wait_ge(S("mod_read"), sl + 1)
                    ada_products(sl, 6 + sl)
                    e.wait_ge(S("mod_row"), 2 * i + sl + 1)
                    ada_transposed(sl, 6 + sl)
                if i == 0:
                    e.wait_ge(S("x_ld"), 48)
                    for k in range(KT):
                        if k >= 4:
                            e.wait_ge(S("xT"), k - 3)
                        for t, (o, p) in enumerate(TILES):
                            l = tr(ps[:, k % 4 + 2, o:o + p], x_tok[0:p, t, k * P:(k + 1) * P], ident[0:p, 0:p])
                        l.then_inc(S("x_mm"), 1)
            e.wait_ge(S("sq"), 1)
            e.wait_ge(S("col"), 1)
            for k in range(KT):
                l = mm(ps[:, 0, 0:TOK], ones[:, :], sq[:, k, :], start=(k == 0), stop=(k == KT - 1))
            l.then_inc(S("ms_mm"), 1)
            e.wait_ge(S("halo_ld"), 32)
            e.wait_ge(S("xT"), 8)
            for i, halo in enumerate((dn_halo, ssm_halo)):
                for m in range(NQ):
                    l = tr(ps[:, 2 + i, m * 24:(m + 1) * 24], halo[:, m * P:(m + 1) * P], ident[0:24, 0:24])
                l.then_inc(S("halo_mm"), 1)
            e.wait_ge(S("hn"), 1)
            e.wait_ge(S("x_mod"), KT)
            e.wait_ge(S("small_ld"), 16 * 8)
            for t, (o, p) in enumerate(TILES):
                for k in range(KT):
                    l = mm(ps[0:p, 1, t * 24:(t + 1) * 24], HN[:, k, o:o + p], wsm[:, k, :], start=(k == 0), stop=(k == KT - 1))
            l.then_inc(S("gsm_mm"), 1)
            e.wait_ge(S("halo_read"), 2)
            e.wait_ge(S("mod_read"), 4)

            def project(i, first):
                for sl in range(2):
                    e.wait_ge(S(f"win_ld{sl}"), i * 16 + 16)
                    if not first:
                        e.wait_ge(S("proj_read"), i * 4 + (2 * sl - 2))
                    for m in range(2):
                        for k in range(KT):
                            l = mm(ps[:, 2 + 2 * sl + m, 0:TOK], w_ring[sl][:, k, m * P:(m + 1) * P], HN[:, k, :],
                                   start=(k == 0), stop=(k == KT - 1))
                        l.then_inc(S("proj_mm"), 1)
                    if sl == 1 and not first:
                        e.wait_ge(S("mod_row"), i + 4)
                        ada_transposed(0, 6)
                    if sl == 0 and not first:
                        e.wait_ge(S("ada_ld0"), i * 16 + 32)
                        e.wait_ge(S("mod_read"), i + 3)
                        ada_products(0, 6)

            project(0, True)
            with e.Fori(1, 9) as i:
                project(i, False)
            e.wait_ge(S("qk_sq"), 1)
            for m in range(2 * DH):
                if m >= 2:
                    e.wait_ge(S("qk_ln"), m - 1)
                mm(ps[:, m % 2, 0:TOK], ones[:, :], sq[:, m, :], start=True, stop=True).then_inc(S("qk_mm"), 1)
            e.wait_ge(S("consts"), 2)
            e.wait_ge(S("gates"), 2)
            e.wait_ge(S("qk_ln"), 2 * DH)
            for t, (o, p) in enumerate(TILES):
                mm(ps[0:p, 0, t * NG:(t + 1) * NG], (tri if p == P else tri_s)[0:p, 0:p], G[0:p, t, :], start=True, stop=True)
                mm(ps[0:p, 0, 64 + t * NG:64 + (t + 1) * NG], (ones if p == P else same_s)[0:p, 0:p], G[0:p, t, :],
                   start=True, stop=True)
            mm(ps[:, 1, 0:NG * NB], ones[0:SMP, :], GM[:].rearrange("p a b -> p (a b)"), start=True, stop=True)
            mm(ps[0:SH, 7, 0:NB], G[0:SMP, 2, DH:NG], seq_of[:], start=True, stop=True).then_inc(S("sums_mm"), 1)
            e.wait_ge(S("dcol"), 1)
            for j in range(KT):
                l = mm(ps[:, 7, 16 + j * NC:16 + (j + 1) * NC], head_rows[:, j, :], dcol[:], start=True, stop=True)
            l.then_inc(S("drep_mm"), 1)
            with e.Fori(9, 11) as i:
                project(i, False)
            e.wait_ge(S("c_new"), 1)
            e.wait_ge(S("sums"), 1)
            e.wait_ge(S("drep"), 1)
            for i in range(NU // 4):
                if i >= 2:
                    e.wait_ge(S("cstate"), i - 1)
                for m in range(4):
                    l = tr(ps[0:27, i % 2, m * P:(m + 1) * P], c_new[:, 4 * i + m, :], ident[:, :])
                l.then_inc(S("cstate_mm"), 1)
            with e.Fori(11, 13) as i:
                project(i, False)
            e.wait_ge(S("proj_read"), 52)
            e.wait_ge(S("cstate"), NU // 4)
            e.wait_ge(S("mod_read"), 16)

            e.wait_ge(S("sums"), 1)
            e.wait_ge(S("qk_normed"), 1)

            def ssd_front(n, t, g):
                (o, p), (bc, bb, cb, cs, bx, by, bh, bm) = TILES[t], (SSD_S if t == 2 else SSD_P)[0]
                U_ = tri if p == P else tri_s
                B_, C_ = CO[:, 20 + g, o:o + p], CO[:, 22 + g, o:o + p]
                for h in range(8):
                    l = mm(heads(cs, 8, p)[:, h], G[0:p, t, DH + 8 * g + h:DH + 8 * g + h + 1].broadcast_to([p, P]), U_[0:p, 0:p],
                           start=True, stop=True)
                l.then_inc(S("s_sums"), 1)
                mm(ps[0:p, bc, 0:p], B_, C_, start=True, stop=True)
                tr(ps[0:p, bb, cb:cb + P], B_, ident[:, :])
                if t != 2 and g:
                    e.wait_ge(S("ht"), 2 * t + 1)
                for j in range(4):
                    l = tr(heads(bx, 4, P, p)[:, j], CO[:, NQ + 4 * g + j, o:o + p], ident[:, :])
                l.then_inc(S("s_mm"), 1)
                if t == 2:
                    e.wait_ge(S("hs_ld"), 64 * (g + 1))
                    for b in range(NB):
                        if b >= 2:
                            e.wait_ge(S("hst"), 8 * g + b - 1)
                        for j in range(4):
                            l = tr(ps[:, 5 + b % 2, j * P:(j + 1) * P], Hs[:, j, b, :], ident[:, :])
                        l.then_inc(S("hst_mm"), 1)

            def ssd_y(n, t, g):
                p, ((bc, bb, cb, cs, bx, by, bh, bm), (CBd_, CE_, R_)) = TILES[t][1], SSD_S if t == 2 else SSD_P
                e.wait_ge(S("s_ready"), 2 * n + g + 1)
                if t == 2:
                    e.wait_ge(S("hst"), 8 * (g + 1))
                for j in range(4):
                    for a in range(2):
                        h = 2 * j + a
                        out = heads(by, 4, p)[HD * a:HD * (a + 1), j]
                        l = mm(out, xdt[0:p, h, :], CBd_[0:p, h, 0:p], start=True, stop=(t != 1))
                        if t == 1:
                            l = mm(out, hT[:, 8 * g + h, :], CE_[:, h, :], start=False, stop=True)
                if t == 2:
                    for b in range(NB):
                        l = mm(ps[SMP * (b % 4):SMP * (b % 4 + 1), 6 + b // 4, :], CE_s[:, b, :], HsT[:, b, :],
                               start=True, stop=True)
                    l.then_inc(S("inter_mm"), 1)
                    e.wait_ge(S("inter"), g + 2)
                    for c in range(2):
                        for j in range(4):
                            l = tr(ps[:, 6 + c, j * P:(j + 1) * P], YI[:, c, j * P:(j + 1) * P], ident[:, :])
                l.then_inc(S("y_mm"), 1)
                if t != 2:
                    mm(ps[:, bh, :], Bt[0:p, :], xw[0:p, :, :].rearrange("p a b -> p (a b)"), start=True, stop=True).then_inc(S("dh_mm"), 1)
                else:
                    e.wait_ge(S("bm"), g + 1)
                    for j in range(4):
                        if j == 2:
                            ssd_squares(n, t, g)
                        if j >= 2:
                            e.wait_ge(S("hs_new"), 4 * g + j - 1)
                        for c in range(2):
                            l = mm(ps[:, 1 + 2 * (j % 2) + c, :], xw[0:p, 2 * j:2 * j + 2, :].rearrange("p a b -> p (a b)"),
                                   Bm[:, 4 * c:4 * c + 4, :].rearrange("p b v -> p (b v)"), start=True, stop=True)
                        l.then_inc(S("hs_mm"), 1)

            def o_squares(n, t, bank):
                p = TILES[t][1]
                e.wait_ge(S("o_sq"), n + 1)
                mm(heads(bank, DH, p), ones[:, :], sqm[:, :, 0:p], start=True, stop=True).then_inc(S("o_ms"), 1)

            def ssd_squares(n, t, g):
                p, bm = TILES[t][1], (SSD_S if t == 2 else SSD_P)[0][7][g]
                e.wait_ge(S("y_sq"), 2 * n + g + 1)
                for j in range(4):
                    l = mm(ps[:, bm, 0:p], ones[:, :], sqm[:, j, 0:p], start=(j == 0), stop=(j == 3))
                l.then_inc(S("y_ms"), 1)

            lv, mk = [0], [0]
            for n, t in enumerate(ORDER):
                o, p = TILES[t]
                U_ = (tri if p == P else tri_s)
                if n:
                    e.wait_ge(S("y_out"), 2 * n)
                    e.wait_ge(S("o_out"), n)
                if t == 1:
                    e.wait_ge(S("sd_new"), 1)
                for h in range(DH):
                    l = mm(heads(0, DH, p)[:, h], G[0:p, t, h:h + 1].broadcast_to([p, P]), U_[0:p, 0:p], start=True, stop=True)
                l.then_inc(S("dn_sums"), 1)
                for h in range(DH):
                    mm(heads(1, DH, p)[:, h], beta[0:p, t, h:h + 1].broadcast_to([p, P]), ident[0:p, 0:p], start=True, stop=True)
                for h in range(DH):
                    k_, q_ = CO[:, DH + h, o:o + p], CO[:, h, o:o + p]
                    mm(heads(2, DH, p, p)[:, h], k_, k_, start=True, stop=True)
                    mm(heads(3, DH, p, p)[:, h], k_, q_, start=True, stop=True)
                for h in range(DH):
                    tr(heads(4, DH, P, p)[:, h], CO[:, DH + h, o:o + p], ident[:, :])
                    l = tr(heads(5, DH, P, p)[:, h], CO[:, 2 * DH + h, o:o + p], ident[:, :])
                l.then_inc(S("dn_mm"), 1)
                if t == 2:
                    e.wait_ge(S("km"), 1)
                    e.wait_ge(S("sin_ld"), 64)
                    for h in range(DH):
                        for b in range(NB):
                            l = mm(heads(6, DH, P, p)[:, h], Km[:, b, h, :], Sin[:, h, b, :], start=(b == 0), stop=(b == NB - 1))
                    l.then_inc(S("ks_mm"), 1)
                if t == 1:
                    e.wait_ge(S("sd_new"), 1)
                    for h in range(DH):
                        l = mm(heads(6, DH, P, p)[:, h], CO[:, DH + h, o:o + p], Sd[:, h, :], start=True, stop=True)
                    l.then_inc(S("ks_mm"), 1)
                e.wait_ge(S("y0"), n + 1)
                if t == 2:
                    for h in range(DH):
                        l = tr(heads(0, DH, p, p)[:, h], Y[0:p, h, 0:p], ident[0:p, 0:p])
                    l.then_inc(S("yt_mm"), 1)
                    e.wait_ge(S("mk"), 1)
                    mk[0] += 1
                    e.wait_ge(S("yt"), 1)
                    for h in range(DH):
                        l = mm(heads(1, DH, p, p)[:, h], Mk[0:p, h, 0:p], Yt[0:p, h, 0:p], start=True, stop=True)
                    l.then_inc(S("w_mm"), 1)
                    e.wait_ge(S("w"), 1)
                    for h in range(DH):
                        l = mm(heads(2, DH, p, p)[:, h], Wt[0:p, h, 0:p], Y[0:p, h, 0:p], start=True, stop=True)
                    l.then_inc(S("wy_mm"), 1)
                    e.wait_ge(S("y_up"), 1)
                    lv[0] += 1
                else:
                    blocks = [(h, slice(HF * b, HF * (b + 1))) for h in range(DH) for b in range(2)]

                    def half(bank, h, rows):
                        return ps[rows, bank, h * HF:(h + 1) * HF]

                    for h, r in blocks:
                        l = mm(half(0, h, r), Y_c[r, h, :], ident[r, r], start=True, stop=True)
                    l.then_inc(S("yt_mm"), 1)
                    for l_ in range(1, 6):
                        e.wait_ge(S("mk"), mk[0] + 1)
                        mk[0] += 1
                        if l_ == 1:
                            e.wait_ge(S("yt"), n + 1)
                        for h, r in blocks:
                            l = mm(half(1, h, r), Mk_c[r, h, :], Yt_c[r, h, :], start=True, stop=True)
                        l.then_inc(S("w_mm"), 1)
                        e.wait_ge(S("w"), lv[0] + 1)
                        for h, r in blocks:
                            mm(half(2, h, r), Wt[r, h, 0:HF], Y_c[r, h, :], start=True, stop=True)
                            l = mm(half(2, h + DH, r), Y_c[r, h, :], Wt[r, h, 0:HF], start=True, stop=True)
                        l.then_inc(S("wy_mm"), 1)
                        if l_ == 1:
                            e.wait_ge(S("r"), n + 1)
                            ssd_front(n, t, 0)
                        if l_ == 3:
                            ssd_y(n, t, 0)
                        if l_ == 4:
                            ssd_squares(n, t, 0)
                            ssd_front(n, t, 1)
                        e.wait_ge(S("y_up"), lv[0] + 1)
                        lv[0] += 1
                    lo, hi = slice(0, HF), slice(HF, P)
                    for h in range(DH):
                        l = mm(half(1, h, hi), Lt[lo, h, HF:P], Yt_c[lo, h, :], start=True, stop=True)
                    l.then_inc(S("w_mm"), 1)
                    e.wait_ge(S("w"), lv[0] + 1)
                    for h in range(DH):
                        l = mm(half(2, h, lo), Wt[hi, h, 0:HF], Y_c[hi, h, :], start=True, stop=True)
                    l.then_inc(S("wy_mm"), 1)
                    ssd_y(n, t, 1)
                    e.wait_ge(S("y_up"), lv[0] + 1)
                    lv[0] += 1
                e.wait_ge(S("r"), n + 1)
                for h in range(DH):
                    l = mm(heads(0, DH, P, p)[:, h], Y[0:p, h, 0:p], R[0:p, h, :], start=True, stop=True)
                l.then_inc(S("vnew_mm"), 1)
                if t != 2:
                    ssd_squares(n, t, 1)
                bo, bs, bm = DN_S if t == 2 else DN_P
                e.wait_ge(S("vnew"), n + 1)
                for h in range(DH):
                    out = heads(bo, DH, p)[:, h]
                    l = mm(out, vnew[0:p, h, :], Qd[0:p, h, 0:p], start=True, stop=(t != 1))
                    if t == 1:
                        l = mm(out, Sd[:, h, :], qe[:, h, :], start=False, stop=True)
                if t == 2:
                    for h in range(DH):
                        for b in range(NB):
                            l = mm(ps[SMP * (b % 4):SMP * (b % 4 + 1), 6 + b // 4, h * P:(h + 1) * P], qe[:, h, 0:SMP],
                                   Sin[:, h, b, :], start=True, stop=True)
                    l.then_inc(S("inter_mm"), 1)
                    e.wait_ge(S("inter"), 1)
                    for c in range(2):
                        for h in range(DH):
                            l = tr(ps[:, 6 + c, h * P:(h + 1) * P], YI[:, c, h * P:(h + 1) * P], ident[:, :])
                l.then_inc(S("o_mm"), 1)
                if t != 2:
                    for h in range(DH):
                        l = mm(heads(bs, DH, P)[:, h], kd[0:p, h, :], vnew[0:p, h, :], start=True, stop=True)
                    l.then_inc(S("ds_mm"), 1)
                else:
                    for h in range(DH):
                        e.wait_ge(S("vm"), h + 1)
                        if h >= 2:
                            e.wait_ge(S("sin_new"), h - 1)
                        for c in range(2):
                            l = mm(ps[:, 2 * (h % 2) + c, :], kd[0:p, h, :],
                                   Vm[h % 2][:, 4 * c:4 * c + 4, :].rearrange("p b v -> p (b v)"), start=True, stop=True)
                        l.then_inc(S("sin_mm"), 1)
                        if h == 1:
                            o_squares(n, t, bm)
                if t != 2:
                    o_squares(n, t, bm)

                if t == 2:
                    for g in range(2):
                        e.wait_ge(S("o_out"), n + 1)
                        if g:
                            e.wait_ge(S("y_out"), 1)
                            e.wait_ge(S("hs_new"), 4)
                        else:
                            e.wait_ge(S("sin_new"), DH)
                        ssd_front(n, t, g)
                        ssd_y(n, t, g)
            e.wait_ge(S("ht"), 4)
            e.wait_ge(S("y_out"), 6)
            e.wait_ge(S("o_out"), 3)
            for j in range(KT):
                l = tr(ps[:, 2 + j // 4, (j % 4) * P:(j % 4 + 1) * P], hT[:, 2 * j:2 * j + 2, :].rearrange("p a b -> p (a b)"), ident[:, :])
                if j % 4 == 3:
                    l.then_inc(S("ht_mm"), 1)
            tail_pe(e)

        @block.scalar
        def _(e):
            act = nc.scalar.activation
            n_ = [0]

            def link(ins):
                n_[0] += 1
                ins.then_inc(S("act_chain"), 1)
                e.wait_ge(S("act_chain"), n_[0])

            e.wait_ge(S("c_ld"), 32)
            act(c_tok, c_tok, ACT.Silu).then_inc(S("c_silu"), 1)
            for k in range(KT):
                e.wait_ge(S("x_mm"), k + 1)
                act(xT[:, k, :], ps[:, k % 4 + 2, 0:TOK], ACT.Copy).then_inc(S("xT"), 1)
            e.wait_ge(S("xT"), KT)
            e.wait_ge(S("x_mm"), KT)
            act(sq, xT[:], ACT.Square).then_inc(S("sq"), 1)

            def inverse_root(out, src, n, sem):
                link(act(out, src, ACT.Ln, bias=eps_c[:], scale=1.0 / n))
                act(out, out, ACT.Exp, scale=-0.5).then_inc(S(sem), 1)

            e.wait_ge(S("ms_mm"), 1)
            inverse_root(rstd[:], ps[:, 0, 0:TOK], D, "root")

            def prompt_modulated(out, shift, n):
                for k in range(KT):
                    e.wait_ge(S("x_scaled"), KT * (n - 1) + k + 1)
                    act(out[:, k, 0:SEQ], out[:, k, 0:SEQ], ACT.Identity, scale=scl[:, k, 0:1],
                        bias=modT[:, shift + k, 0:1]).then_inc(S("x_mod"), 1)

            prompt_modulated(HN, SHIFT1, 1)
            e.wait_ge(S("gsm_arg"), 1)
            act(t1[:], t1[:], ACT.Exp, scale=-1.0).then_inc(S("gsm_f"), 1)
            act(nbeta[:], gsm[:, :, NG:24], ACT.Exp, scale=-1.0)
            link(act(alog_row[:], alog_row[:], ACT.Exp))
            e.wait_ge(S("gsm_arg"), 2)
            act(t2[:], t2[:], ACT.Ln).then_inc(S("gsm_f"), 1)

            def evac(i, kind, blk=True):
                for m in range(4):
                    if m == 2 and blk:
                        e.wait_ge(S("ada_mm"), i + 4)
                        act(mod_rows[:, 0, :], ps[:, 6, 0:P], ACT.Copy).then_inc(S("mod_row"), 1)
                    e.wait_ge(S("proj_mm"), i * 4 + (m + 1))
                    src = ps[:, 2 + m, 0:TOK]
                    if kind[0] == "u":
                        tile = i * 4 + (m + kind[1])
                        dst = U[:, bass.ds(tile, 1), :].rearrange("p a n -> p (a n)")
                        act(dst[:, HALO:SROW], src[:, 0:SEQ], ACT.Copy)
                        act(dst[:, SROW:ROW].rearrange("p (b t) -> p b t", t=STEP)[:, :, HALO:STEP],
                            src[:, SEQ:TOK].rearrange("p (b t) -> p b t", t=NT), ACT.Copy).then_inc(S("proj_read"), 1)
                    else:
                        dst = ZC[:, bass.ds(i * 4 + (m + kind[1]), 1), :].rearrange("p a n -> p (a n)")
                        act(dst, src, kind[0]).then_inc(S("proj_read"), 1)

            def mod_evac(i):
                e.wait_ge(S("mod_mm"), i + 4)
                act(modT[:, bass.ds(i * 4 + 12, 4), :], ps[:, 6, P:2 * P].rearrange("p (m c) -> p m c", c=CPAD)[:, :, 0:NC],
                    ACT.Copy).then_inc(S("mod_read"), 1)

            def conv_silu(first, bias):
                for m in range(NQ):
                    e.wait_ge(S("cv"), first + m + 1)
                    b = {"bias": colB[:, B_CONVB + m:B_CONVB + m + 1]} if bias else {}
                    act(CO[:, first + m, 0:SEQ], cv[:, m, 0:SEQ], ACT.Silu, **b)
                    act(CO[:, first + m, SEQ:TOK].rearrange("p (b t) -> p b t", t=NT),
                        cv_sample(m), ACT.Silu, **b).then_inc(S("co"), 1)

            def cv_sample(m):
                return arena[:, cv_at + m * CROW + SROW:cv_at + m * CROW + SROW + NB * STEP].rearrange(
                    "p (b t) -> p b t", t=STEP)[:, :, 0:NT]

            e.wait_ge(S("halo_read"), 2)
            evac(0, ("u", 0), False)
            with e.Fori(1, 3) as i:
                evac(i, ("u", 0))
                mod_evac(i)
            with e.Fori(3, 4) as i:
                evac(i, (ACT.Silu, -12))
                mod_evac(i)
            conv_silu(0, False)
            with e.Fori(4, 7) as i:
                evac(i, ("u", -4))
                mod_evac(i)
            e.wait_ge(S("co"), NQ)
            act(sq, CO[:, 0:2 * DH, :], ACT.Square).then_inc(S("qk_sq"), 1)
            with e.Fori(7, 9) as i:
                evac(i, (ACT.Silu, -24))
                mod_evac(i)
            for m in range(2 * DH):
                e.wait_ge(S("qk_mm"), m + 1)
                act(sq[:, m, :], ps[:, m % 2, 0:TOK], ACT.Ln, bias=eps_c[:]).then_inc(S("qk_ln"), 1)
            e.wait_ge(S("qk_ln"), 2 * DH)
            act(sq, sq, ACT.Exp, scale=-0.5).then_inc(S("qk_root"), 1)
            e.wait_ge(S("sums_mm"), 1)
            act(dcol[:, 0:NB], ps[0:SH, 7, 0:NB], ACT.Exp).then_inc(S("dcol"), 1)
            e.wait_ge(S("dte_arg"), 1)
            act(dte[:], dte[:], ACT.Exp)
            act(ecs[:], csum[:], ACT.Exp)
            act(elast[:].rearrange("p a b -> p (a b)"), ps[:, 0, 64:64 + 2 * NG], ACT.Exp)
            act(EL2[:].rearrange("p a b -> p (a b)"), ps[:, 1, 0:NG * NB], ACT.Exp).then_inc(S("sums"), 1)
            conv_silu(NQ, True)
            with e.Fori(9, 11) as i:
                evac(i, (ACT.Sigmoid, -24))
                mod_evac(i)
            for i in range(NU // 4):
                e.wait_ge(S("cstate_mm"), i + 1)
                act(cst[:, 4 * i:4 * i + 4, :].rearrange("p a b -> p (a b)"), ps[0:27, i % 2, :], ACT.Copy).then_inc(S("cstate"), 1)
            with e.Fori(11, 13) as i:
                evac(i, (ACT.Sigmoid, -24))
                mod_evac(i)

            def ssd_bounds(n, t, g):
                p, cs = TILES[t][1], (SSD_S if t == 2 else SSD_P)[0][3]
                e.wait_ge(S("s_sums"), 2 * n + g + 1)
                if t:
                    act(EB[:, :, 0:p], heads(cs, 8, p), ACT.Exp).then_inc(S("s_eb"), 1)

            def ssd_decays(n, t, g):
                p = TILES[t][1]
                e.wait_ge(S("s_arg"), 2 * n + g + 1)
                act(D2[0:p, :, 0:p], D2[0:p, :, 0:p], ACT.Exp).then_inc(S("s_exp"), 1)
                if t == 2:
                    for b in range(NB):
                        e.wait_ge(S("hst_mm"), 8 * g + b + 1)
                        act(HsT[:, b, :], ps[:, 5 + b % 2, :], ACT.Copy).then_inc(S("hst"), 1)
                    e.wait_ge(S("inter_mm"), g + 2)
                    act(YI, ps[:, 6:8, :], ACT.Copy).then_inc(S("inter"), 1)

            def ssd_norm(n, t, g):
                p, ((bc, bb, cb, cs, bx, by, bh, bm), (CBd_, CE_, R_)) = TILES[t][1], SSD_S if t == 2 else SSD_P
                i = 2 * n + g
                e.wait_ge(S("y1"), i + 1)
                act(sqm[:, :, 0:p], R_[:, :, 0:p], ACT.Square).then_inc(S("y_sq"), 1)
                e.wait_ge(S("y_ms"), i + 1)
                if i:
                    e.wait_ge(S("y_out"), i)
                inverse_root(rs[:, 0, 0:p], ps[:, bm[g], 0:p], 4 * P, "y_root")

            lv = 0
            for n, t in enumerate(ORDER):
                o, p = TILES[t]
                e.wait_ge(S("dn_sums"), n + 1)
                if n:
                    e.wait_ge(S("y_out"), 2 * n)
                    e.wait_ge(S("o_out"), n)
                act(EB[:, 0:DH, 0:p], heads(0, DH, p), ACT.Exp).then_inc(S("dn_eb"), 1)
                e.wait_ge(S("dn_arg"), n + 1)
                act(D2[0:p, 0:DH, 0:p], D2[0:p, 0:DH, 0:p], ACT.Exp).then_inc(S("dn_exp"), 1)
                e.wait_ge(S("yt_mm"), n + 1)
                if t == 2:
                    act(Yt[0:p, :, 0:p], heads(0, DH, p, p), ACT.Copy).then_inc(S("yt"), 1)
                    e.wait_ge(S("w_mm"), 1)
                    act(Wt[0:p, :, 0:p], heads(1, DH, p, p), ACT.Copy).then_inc(S("w"), 1)
                    lv += 1
                else:
                    act(Yt_c, heads(0, DH, HF, P, HF), ACT.Copy).then_inc(S("yt"), 1)
                    for l in range(1, 7):
                        e.wait_ge(S("w_mm"), lv + 1)
                        r = slice(0 if l < 6 else HF, P)
                        act(Wt[r, :, 0:HF], ps[r, 1, 0:DH * HF].rearrange("p (h c) -> p h c", c=HF), ACT.Copy).then_inc(S("w"), 1)
                        lv += 1
                        if l == 1:
                            e.wait_ge(S("r"), n + 1)
                            ssd_bounds(n, t, 0)
                        if l == 2:
                            ssd_decays(n, t, 0)
                        if l == 4:
                            ssd_norm(n, t, 0)
                            ssd_bounds(n, t, 1)
                        if l == 5:
                            ssd_decays(n, t, 1)
                e.wait_ge(S("vnew_mm"), n + 1)
                act(vnew[0:p], heads(0, DH, P, p), ACT.Copy).then_inc(S("vnew"), 1)
                if t != 2:
                    ssd_norm(n, t, 1)
                    e.wait_ge(S("y_out"), 2 * n + 2)
                bo, bs, bm = DN_S if t == 2 else DN_P
                if t == 2:
                    e.wait_ge(S("inter_mm"), 1)
                    act(YI, ps[:, 6:8, :], ACT.Copy).then_inc(S("inter"), 1)
                    e.wait_ge(S("o_sum"), 1)
                    act(sqm[:, :, 0:p], o_s, ACT.Square).then_inc(S("o_sq"), 1)
                else:
                    e.wait_ge(S("o_mm"), n + 1)
                    act(sqm[:, :, 0:p], heads(bo, DH, p), ACT.Square).then_inc(S("o_sq"), 1)
                e.wait_ge(S("o_ms"), n + 1)
                inverse_root(rs[:, :, 0:p], heads(bm, DH, p), P, "o_root")
                if t == 2:
                    for g in range(2):
                        e.wait_ge(S("o_out"), n + 1)
                        if g:
                            e.wait_ge(S("y_out"), 1)
                        ssd_bounds(n, t, g)
                        ssd_decays(n, t, g)
                        ssd_norm(n, t, g)
            for i in range(2):
                e.wait_ge(S("ht_mm"), i + 1)
                act(hT_out[:, 4 * i:4 * i + 4, :].rearrange("p a b -> p (a b)"), ps[:, 2 + i, :], ACT.Copy).then_inc(S("ht_out"), 1)
            tail_act(e, inverse_root, prompt_modulated)

        @block.vector
        def _(e):
            v = nc.vector
            tt, ts, stt = v.tensor_tensor, v.tensor_scalar, v.scalar_tensor_tensor
            n_ = [0]

            def link(ins):
                n_[0] += 1
                ins.then_inc(S("dve_chain"), 1)
                e.wait_ge(S("dve_chain"), n_[0])

            e.wait_ge(S("first_mm"), 1)
            link(v.memset(cT[:], 0.0))
            v.tensor_copy(cT[:, :, 0:NC], ps[:, 1, 0:KT * NC].rearrange("p (k c) -> p k c", c=NC)).then_inc(S("cT"), 1)
            e.wait_ge(S("first_mm"), 2)
            v.tensor_copy(colB[:], ps[:, 0, 128:128 + B_ROWS])
            link(v.tensor_copy(colA[:], ps[:, 0, 0:A_ROWS]))
            e.nop().then_inc(S("col"), 1)
            for i in range(4):
                e.wait_ge(S("ada_mm"), i + 1)
                if i >= 2:
                    e.wait_ge(S("mod_mm"), i - 1)
                v.tensor_copy(mod_rows[:, i % 2, :], ps[:, 6 + i % 2, 0:P]).then_inc(S("mod_row"), 1)
                e.wait_ge(S("mod_mm"), i + 1)
                v.tensor_copy(modT[:, 4 * i:4 * i + 4, :],
                              ps[:, 6 + i % 2, P:2 * P].rearrange("p (m c) -> p m c", c=CPAD)[:, :, 0:NC]).then_inc(S("mod_read"), 1)
            e.wait_ge(S("mod_read"), 4)

            def mod_bias(first, n, col):
                b = col.unsqueeze(2).broadcast_to([P, n, NC])
                link(tt(modT[:, first:first + n, :], modT[:, first:first + n, :], b, ALU.add))

            def norm_scale(weight, scale):
                link(stt(scl[:], modT[:, scale:scale + KT, :], 1.0, weight.unsqueeze(2).broadcast_to([P, KT, NC]),
                         ALU.add, ALU.mult))

            def modulated(out):
                for k in range(KT):
                    tt(out[:, k, :], xT[:, k, :], rstd[:], ALU.mult).then_inc(S("x_scaled"), 1)

            def samples_modulated(out, shift, n):
                e.wait_ge(S("x_scaled"), KT * n)
                s = out[:, :, SEQ:TOK].rearrange("p k (b t) -> p k b t", t=NT)
                link(tt(s, s, scl[:, :, 1:NC].unsqueeze(3).broadcast_to([P, KT, NB, NT]), ALU.mult))
                link(tt(s, s, modT[:, shift:shift + KT, 1:NC].unsqueeze(3).broadcast_to([P, KT, NB, NT]), ALU.add))

            mod_bias(0, 16, colA[:, 0:16])
            norm_scale(colA[:, A_NORM:A_NORM + KT], SCALE1)
            e.wait_ge(S("root"), 1)
            modulated(HN)
            samples_modulated(HN, SHIFT1, 1)
            e.nop().then_inc(S("hn"), 1)
            for i in range(2):
                e.wait_ge(S("halo_mm"), i + 1)
                for b in range(NB):
                    l = v.tensor_copy(U[:, NQ * i:NQ * (i + 1), SROW + b * STEP:SROW + b * STEP + HALO],
                                      ps[:, 2 + i, 0:NQ * 24].rearrange("p (m r) -> p m r", r=24)[:, :, 3 * b:3 * b + 3])
                l.then_inc(S("halo_read"), 1)
            e.wait_ge(S("gsm_mm"), 1)
            e.wait_ge(S("consts"), 1)
            for t, (o, p) in enumerate(TILES):
                v.tensor_copy(gsm[0:p, t, NG:24], ps[0:p, 1, t * 24 + NG:t * 24 + 24])
                l = tt(gsm[0:p, t, 0:NG], ps[0:p, 1, t * 24:t * 24 + NG], bias_row[0:p, :], ALU.add)
            link(l)
            a = gsm[:, :, 0:NG]
            link(ts(t1[:], a, -1.0, None, ALU.mult))
            tt(t1[:], t1[:], a, ALU.max).then_inc(S("gsm_arg"), 1)
            e.wait_ge(S("gsm_f"), 1)
            link(ts(t2[:], t1[:], 1.0, None, ALU.add))
            link(ts(sp[:], t2[:], -1.0, 1e-30, ALU.add, ALU.add))
            link(v.reciprocal(sp[:], sp[:]))
            link(tt(sp[:], sp[:], t1[:], ALU.mult))
            e.nop().then_inc(S("gsm_arg"), 1)
            e.wait_ge(S("gsm_f"), 2)
            e.wait_ge(S("act_chain"), 1)
            link(ts(t2[:], t2[:], 1e-30, None, ALU.add))
            link(tt(sp[:], sp[:], t2[:], ALU.mult))
            link(stt(sp[:], a, 0.0, sp[:], ALU.max, ALU.add))
            ts(nbeta[:], nbeta[:], 1.0, None, ALU.add)
            link(stt(G[:], sp[:], -1.0, alog_row[:].unsqueeze(1).broadcast_to([P, 3, NG]), ALU.mult, ALU.mult))
            link(v.reciprocal(beta[:], nbeta[:]))
            link(ts(nbeta[:], beta[:], -1.0, None, ALU.mult))
            e.nop().then_inc(S("gates"), 1)
            e.wait_ge(S("consts"), 2)
            tt(GM[:], G[0:SMP, 2, :].unsqueeze(2).broadcast_to([SMP, NG, NB]),
               seq_of[:].unsqueeze(1).broadcast_to([SMP, NG, NB]), ALU.mult).then_inc(S("gates"), 1)

            for first, conv in ((0, colA[:, A_CONV:A_CONV + 48]), (NQ, colB[:, B_CONV:B_CONV + 48])):
                for m in range(NQ):
                    tile = first + m
                    e.wait_ge(S("proj_read"), tile + 1 + (4 if first else 0))
                    if first:
                        e.wait_ge(S("co"), m + 1)
                    acc, u = cv[:, m, :], U[:, tile, :]
                    link(ts(acc, u[:, 0:CROW], conv[:, m:m + 1], None, ALU.mult))
                    for i in range(1, 4):
                        l = stt(acc, u[:, i:i + CROW], conv[:, NQ * i + m:NQ * i + m + 1], acc, ALU.mult, ALU.add)
                        if i < 3:
                            link(l)
                    l.then_inc(S("cv"), 1)
            e.wait_ge(S("qk_root"), 1)
            stt(CO[:, 0:DH, :], sq[:, 0:DH, :], P ** -0.5, CO[:, 0:DH, :], ALU.mult, ALU.mult)
            link(tt(CO[:, DH:2 * DH, :], sq[:, DH:2 * DH, :], CO[:, DH:2 * DH, :], ALU.mult))
            e.nop().then_inc(S("qk_normed"), 1)
            e.wait_ge(S("sums_mm"), 1)
            link(v.memset(csum[:], 0.0))
            link(v.memset(dte[:], 0.0))
            for t, (o, p) in enumerate(TILES):
                l = v.tensor_copy(csum[0:p, t, :], ps[0:p, 0, t * NG:(t + 1) * NG])
            link(l)
            for t, (o, p) in enumerate(TILES):
                l = tt(dte[0:p, t, :], ps[0:p, 0, 64 + t * NG:64 + (t + 1) * NG], csum[0:p, t, :], ALU.subtract)
            link(l)
            e.nop().then_inc(S("dte_arg"), 1)
            e.wait_ge(S("drep_mm"), 1)
            link(v.tensor_copy(drep[:].rearrange("p a b -> p (a b)"), ps[:, 7, 16:16 + KT * NC]))
            e.nop().then_inc(S("drep"), 1)
            e.wait_ge(S("co"), NU)
            e.wait_ge(S("mod_read"), 16)
            mod_bias(16, 32, colA[:, 16:48])
            mod_bias(48, 16, colB[:, B_BFIN:B_BFIN + 16])
            e.wait_ge(S("sums"), 1)
            e.wait_ge(S("c_new"), 1)

            def ssd_front(n, t, g):
                p, (bc, bb, cb, cs, bx, by, bh, bm) = TILES[t][1], (SSD_S if t == 2 else SSD_P)[0]
                ng = neg if p == P else neg_s
                hs = slice(DH + 8 * g, DH + 8 * g + 8)
                e.wait_ge(S("s_sums"), 2 * n + g + 1)
                if t:
                    e.wait_ge(S("s_eb"), g + 1 + (2 if t == 1 else 0))
                for h in range(8):
                    c = DH + 8 * g + h
                    l = stt(D2[0:p, h, 0:p], heads(cs, 8, p, p)[:, h], csum[0:p, t, c:c + 1], ng[0:p, 0:p], ALU.subtract, ALU.add)
                l.then_inc(S("s_arg"), 1)
                e.wait_ge(S("s_mm"), 2 * n + g + 1)
                v.tensor_copy(Bt[0:p, :], ps[0:p, bb, cb:cb + P]).then_inc(S("bt"), 1)
                link(tt(xdt[0:p], heads(bx, 8, HD, p, HD), sp[0:p, t, hs].unsqueeze(2).broadcast_to([p, 8, HD]), ALU.mult))
                tt(xw[0:p], xdt[0:p], dte[0:p, t, hs].unsqueeze(2).broadcast_to([p, 8, HD]), ALU.mult)

            def ssd_decays(n, t, g):
                (o, p), ((bc, bb, cb, cs, bx, by, bh, bm), (CBd_, CE_, R_)) = TILES[t], SSD_S if t == 2 else SSD_P
                e.wait_ge(S("s_exp"), 2 * n + g + 1)
                l = tt(CBd_[0:p, :, 0:p], D2[0:p, :, 0:p], ps[0:p, bc:bc + 1, 0:p].broadcast_to([p, 8, p]), ALU.mult)
                if t == 1:
                    l = tt(CE_[:, :, 0:p], EB[:, :, 0:p], CO[:, 22 + g:23 + g, o:o + p].broadcast_to([P, 8, p]), ALU.mult)
                if t == 2:
                    l = tt(CE_s.rearrange("p b (h t) -> p h b t", t=NT), EB[:, :, 0:p].rearrange("p h (b t) -> p h b t", t=NT),
                           CO[:, 22 + g, o:o + p].rearrange("p (b t) -> p b t", t=NT).unsqueeze(1).broadcast_to([P, 8, NB, NT]),
                           ALU.mult)
                l.then_inc(S("s_ready"), 1)

            def ssd_y(n, t, g):
                (o, p), ((bc, bb, cb, cs, bx, by, bh, bm), (CBd_, CE_, R_)) = TILES[t], SSD_S if t == 2 else SSD_P
                hs = slice(DH + 8 * g, DH + 8 * g + 8)
                e.wait_ge(S("y_mm"), 2 * n + g + 1)
                for j in range(4):
                    l = stt(R_[:, j, 0:p], CO[:, NQ + 4 * g + j, o:o + p], drep[:, 4 * g + j, NB:NC], heads(by, 4, p)[:, j],
                            ALU.mult, ALU.add)
                link(l)
                if t == 2:
                    for a in range(2):
                        half = slice(HD * a, HD * (a + 1))
                        for j in range(4):
                            r = R_[half, j, 0:p].rearrange("p (c b t) -> p c b t", c=2, t=NT)
                            inter = ps[half, 6:8, j * P:(j + 1) * P].rearrange("p c (b h t) -> p c b h t", h=8, t=NT)
                            l = tt(r, r, inter[:, :, :, 2 * j + a, :], ALU.add)
                    link(l)
                tt(R_[:, :, 0:p], R_[:, :, 0:p], ZC[:, 4 + 4 * g:8 + 4 * g, o:o + p], ALU.mult).then_inc(S("y1"), 1)
                if t == 2:
                    for j in range(4):
                        e.wait_ge(S("hs_mm"), 4 * g + j + 1)
                        e.wait_ge(S("hs_decayed"), 4 * g + j + 1)
                        tt(Hs[:, j], Hs[:, j], heads(1 + 2 * (j % 2), NB, P), ALU.add).then_inc(S("hs_new"), 1)
                else:
                    e.wait_ge(S("dh_mm"), 2 * t + g + 1)
                    hg = hT[:, 8 * g:8 * g + 8, :]
                    dh = heads(bh, 8, HD, P, HD)
                    if t == 0:
                        v.tensor_copy(hg, dh).then_inc(S("ht"), 1)
                    else:
                        link(tt(hg, hg, elast[:, t, hs].unsqueeze(2).broadcast_to([P, 8, HD]), ALU.mult))
                        tt(hg, hg, dh, ALU.add).then_inc(S("ht"), 1)

            def ssd_out(n, t, g):
                (o, p), R_ = TILES[t], (SSD_S if t == 2 else SSD_P)[1][2]
                e.wait_ge(S("y_root"), 2 * n + g + 1)
                for j in range(4):
                    c = B_SNORM + 4 * g + j
                    l = stt(CO[:, NQ + 4 * g + j, o:o + p], R_[:, j, 0:p], colB[:, c:c + 1], rs[:, 0, 0:p], ALU.mult, ALU.mult)
                l.then_inc(S("y_out"), 1)

            lv = [0]
            for n, t in enumerate(ORDER):
                o, p = TILES[t]
                ng = neg if p == P else neg_s
                e.wait_ge(S("dn_eb"), n + 1)
                for h in range(DH):
                    l = stt(D2[0:p, h, 0:p], heads(0, DH, p, p)[:, h], csum[0:p, t, h:h + 1], ng[0:p, 0:p], ALU.subtract, ALU.add)
                l.then_inc(S("dn_arg"), 1)
                e.wait_ge(S("dn_mm"), n + 1)
                v.tensor_copy(kTok[0:p], heads(4, DH, P, p))
                link(v.tensor_copy(vTok[0:p], heads(5, DH, P, p)))
                for h in range(DH):
                    ts(kd[0:p, h, :], kTok[0:p, h, :], dte[0:p, t, h:h + 1], None, ALU.mult)
                e.wait_ge(S("dn_exp"), n + 1)
                dec = D2[0:p, 0:DH, 0:p]
                link(tt(Lt[0:p, :, 0:p], heads(2, DH, p, p), dec, ALU.mult))
                tt(Qd[0:p, :, 0:p], heads(3, DH, p, p), dec, ALU.mult)
                lo, hi = slice(0, HF), slice(HF, P)
                if t == 2:
                    def lev(l):
                        return level[0:p, l:l + 1, 0:p].broadcast_to([p, DH, p])

                    link(tt(Lt[0:p, :, 0:p], heads(1, DH, p, p), Lt[0:p, :, 0:p], ALU.mult))
                    link(tt(Y[0:p, :, 0:p], Lt[0:p, :, 0:p], lev(0), ALU.mult))
                    tt(Mk[0:p, :, 0:p], Lt[0:p, :, 0:p], lev(1), ALU.mult).then_inc(S("mk"), 1)
                    link(tt(Y[0:p, :, 0:p], ident[0:p, 0:p].unsqueeze(1).broadcast_to([p, DH, p]), Y[0:p, :, 0:p], ALU.subtract))
                else:
                    def lev(l):
                        return level[:, l:l + 1, 0:HF].broadcast_to([P, DH, HF])

                    for r in (lo, hi):
                        tt(L_c[r], heads(1, DH, P)[r, :, r], Lt[r, :, r], ALU.mult)
                    link(tt(Lt[lo, :, hi], heads(1, DH, P)[lo, :, hi], Lt[lo, :, hi], ALU.mult))
                    link(tt(Y_c, L_c, lev(0), ALU.mult))
                    tt(Mk_c, L_c, lev(1), ALU.mult).then_inc(S("mk"), 1)
                    for r in (lo, hi):
                        l = tt(Y_c[r], ident[r, r].unsqueeze(1).broadcast_to([HF, DH, HF]), Y_c[r], ALU.subtract)
                    link(l)
                e.nop().then_inc(S("y0"), 1)
                if t != 2:
                    v.memset(Y[hi, :, lo], 0.0)
                if t == 0:
                    for h in range(DH):
                        l = ts(R[0:p, h, :], vTok[0:p, h, :], beta[0:p, t, h:h + 1], None, ALU.mult)
                else:
                    e.wait_ge(S("ks_mm"), n if t == 1 else 1)
                    for h in range(DH):
                        l = stt(R[0:p, h, :], heads(6, DH, P, p)[:, h], ecs[0:p, t, h:h + 1], vTok[0:p, h, :], ALU.mult, ALU.subtract)
                    link(l)
                    for h in range(DH):
                        l = ts(R[0:p, h, :], R[0:p, h, :], nbeta[0:p, t, h:h + 1], None, ALU.mult)
                    l = tt(qe[:, :, 0:p], CO[:, 0:DH, o:o + p], EB[:, 0:DH, 0:p], ALU.mult)
                link(l)
                e.nop().then_inc(S("r"), 1)
                for l_ in range(1, 7 if t != 2 else 2):
                    e.wait_ge(S("w_mm"), lv[0] + 1)
                    if t != 2 and l_ < 5:
                        tt(Mk_c, L_c, lev(l_ + 1), ALU.mult).then_inc(S("mk"), 1)
                    if l_ == 6:
                        for r in (lo, hi):
                            v.tensor_copy(Y[r, :, r], Y_c[r])
                    e.wait_ge(S("wy_mm"), lv[0] + 1)
                    if t == 2:
                        tt(Y[0:p, :, 0:p], Y[0:p, :, 0:p], heads(2, DH, p, p), ALU.subtract).then_inc(S("y_up"), 1)
                    elif l_ < 6:
                        upd = ps[:, 2, :].rearrange("p (a h c) -> p a h c", a=2, c=HF)
                        tt(Yt_c, Yt_c, upd[:, 1], ALU.subtract)
                        link(tt(Y_c, Y_c, upd[:, 0], ALU.subtract))
                        e.nop().then_inc(S("y_up"), 1)
                    else:
                        ts(Y[lo, :, hi], heads(2, DH, HF, P, HF)[lo], -1.0, None, ALU.mult).then_inc(S("y_up"), 1)
                    lv[0] += 1
                    if t != 2:
                        if l_ == 1:
                            ssd_front(n, t, 0)
                        if l_ == 2:
                            ssd_decays(n, t, 0)
                        if l_ == 3:
                            ssd_y(n, t, 0)
                        if l_ == 4:
                            ssd_out(n, t, 0)
                            ssd_front(n, t, 1)
                        if l_ == 5:
                            ssd_decays(n, t, 1)
                        if l_ == 6:
                            ssd_y(n, t, 1)
                            ssd_out(n, t, 1)
                bo, bs, bm = DN_S if t == 2 else DN_P
                if t == 2:
                    e.wait_ge(S("inter_mm"), 1)
                    for h in range(DH):
                        tt(Sin[:, h], Sin[:, h], EL2[:, h, :].unsqueeze(2).broadcast_to([P, NB, P]), ALU.mult)
                    e.wait_ge(S("o_mm"), 1)
                    link(v.tensor_copy(out=o_s, in_=heads(bo, DH, SMP)))
                    for b in range(NB):
                        at_ = slice(b * NT, (b + 1) * NT)
                        inter = ps[:, 6 + b // 4, :].rearrange("p (h b t) -> p h b t", h=DH, b=4)[:, :, b % 4, at_]
                        l = tt(o_s[:, :, at_], o_s[:, :, at_], inter, ALU.add)
                    link(l)
                    e.nop().then_inc(S("o_sum"), 1)
                    for h in range(DH):
                        e.wait_ge(S("sin_mm"), h + 1)
                        tt(Sin[:, h], Sin[:, h], heads(2 * (h % 2), NB, P), ALU.add).then_inc(S("sin_new"), 1)
                else:
                    e.wait_ge(S("ds_mm"), t + 1)
                    e.wait_ge(S("o_mm"), n + 1)
                    if t == 0:
                        l = v.tensor_copy(Sd, heads(bs, DH, P))
                    else:
                        for h in range(DH):
                            l = stt(Sd[:, h, :], Sd[:, h, :], elast[:, t, h:h + 1], heads(bs, DH, P)[:, h], ALU.mult, ALU.add)
                    l.then_inc(S("sd_new"), 1)
                e.wait_ge(S("o_root"), n + 1)
                on = CO[:, 0:DH, o:o + p]
                link(tt(on, o_s if t == 2 else heads(bo, DH, p), rs[:, :, 0:p], ALU.mult))
                link(stt(on, on, colB[:, B_DNORM:B_DNORM + 1], ZC[:, 0:DH, o:o + p], ALU.mult, ALU.mult))
                e.nop().then_inc(S("o_out"), 1)

                if t == 2:
                    for g in range(2):
                        ssd_front(n, t, g)
                        ssd_decays(n, t, g)
                        ssd_y(n, t, g)
                        ssd_out(n, t, g)
            tail_dve(e, link, norm_scale, modulated, samples_modulated)


_INS = ["x_prompt", "x_sample", "c_prompt", "c_sample", "state_dn_conv", "state_dn_rec", "state_ssm_conv",
        "state_ssm_rec", "w_ada", "b_ada", "norm_mix_w", "w_in", "dn_conv_w", "dn_A_log", "dn_dt_bias", "dn_norm_w",
        "w_dn_out", "ssm_conv_w", "ssm_conv_b", "ssm_A_log", "ssm_dt_bias", "ssm_D", "ssm_norm_w", "w_ssm_out",
        "w_out", "norm_ffn_w", "w_group_router", "b_group_router", "w_expert_router", "b_expert_router",
        "w_exp_gate", "w_exp_up", "w_exp_down", "w_ada_final", "b_ada_final", "final_norm_w"]
_OUTS = [("y_p", (1, 256, 1024)), ("y_s", (8, 4, 1024)), ("dn_conv_p", (1, 1, 3, 1536)), ("dn_rec_p", (1, 1, 4, 128, 128)),
         ("ssm_conv_p", (1, 1, 3, 1536)), ("ssm_rec_p", (1, 1, 16, 64, 128)), ("dn_conv_s", (1, 8, 3, 1536)),
         ("dn_rec_s", (1, 8, 4, 128, 128)), ("ssm_conv_s", (1, 8, 3, 1536)), ("ssm_rec_s", (1, 8, 16, 64, 128))]


def kernel(**inputs):
    import numpy as _np
    import concourse.bacc as _bacc
    from concourse.bass_utils import run_bass_kernel_spmd as _run

    nc = _bacc.Bacc("TRN2", target_bir_lowering=False, num_devices=1)
    arrays, ins, outs = {}, {}, {}
    for name in _INS:
        a = _np.ascontiguousarray(inputs[name])
        arrays[f"in_{name}"] = a
        ins[name] = nc.dram_tensor(f"in_{name}", a.shape, F32, kind="ExternalInput").ap()
    for name, shape in _OUTS:
        outs[name] = nc.dram_tensor(f"out_{name}", shape, F32, kind="ExternalOutput").ap()
    hybrid_step(nc, ins, outs)
    r = _run(nc, [arrays], core_ids=[0])
    return tuple(r.results[0][f"out_{name}"] for name, _ in _OUTS)
```
